# Optimizing a Trainium2 kernel written in Bass

```python
import math
import jax
import jax.numpy as jnp
from jax import lax
import numpy as np

D_MODEL = 1024
BATCH = 1
SEQ = 256
DEPTH = 4

CHUNK = 64
Q_BLOCK = 128
HEAD_DIM = 64
FOX_HEADS = D_MODEL // HEAD_DIM
DIFF_HEADS = D_MODEL // (2 * HEAD_DIM)
ROT_DIM = HEAD_DIM // 4
ROPE_THETA = 500000.0
CONV_WIDTH = 31
D_FF = ((8 * D_MODEL // 3 + 127) // 128) * 128
N_MIXERS = 3
N_FOX = (DEPTH + 2) // 3
N_CONV = (DEPTH + 1) // 3
N_DIFF = DEPTH // 3
EPS = 1e-6

kernel_name = 'hybrid_fox_conformer_diffattn_trunk'

def _rms_norm(x, g):
    xf = x.astype(jnp.float32)
    y = xf * lax.rsqrt(jnp.mean(xf * xf, axis=-1, keepdims=True) + EPS)
    return (y * g.astype(jnp.float32)).astype(x.dtype)

def _layer_norm(x, g, b):
    xf = x.astype(jnp.float32)
    mu = jnp.mean(xf, axis=-1, keepdims=True)
    var = jnp.mean(jnp.square(xf - mu), axis=-1, keepdims=True)
    y = (xf - mu) * lax.rsqrt(var + EPS)
    return (y * g.astype(jnp.float32) + b.astype(jnp.float32)).astype(x.dtype)

def _swiglu(h, w_gate, w_up, w_down):
    return (jax.nn.silu(h @ w_gate) * (h @ w_up)) @ w_down

def _partial_rope(x, cos, sin):
    half = ROT_DIM // 2
    x1 = x[..., :half]
    x2 = x[..., half:ROT_DIM]
    xp = x[..., ROT_DIM:]
    return jnp.concatenate([x1 * cos - x2 * sin, x2 * cos + x1 * sin, xp], axis=-1)

def _fox_mixer(h, w_in, b_f, q_gain, k_gain, w_out):
    bsz, seq, _ = h.shape
    proj = h @ w_in
    q = proj[..., :D_MODEL].reshape(bsz, seq, FOX_HEADS, HEAD_DIM)
    k = proj[..., D_MODEL:2 * D_MODEL].reshape(bsz, seq, FOX_HEADS, HEAD_DIM)
    v = proj[..., 2 * D_MODEL:3 * D_MODEL].reshape(bsz, seq, FOX_HEADS, HEAD_DIM)
    f_logit = proj[..., 3 * D_MODEL:] + b_f
    q = _rms_norm(q, q_gain)
    k = _rms_norm(k, k_gain)
    log_f = jax.nn.log_sigmoid(f_logit.astype(jnp.float32))
    cum = jnp.cumsum(log_f, axis=1).transpose(0, 2, 1)
    scale = HEAD_DIM ** -0.5
    outs = []
    for q0 in range(0, seq, Q_BLOCK):
        q1 = q0 + Q_BLOCK
        s = jnp.einsum('bqhd,bkhd->bhqk', q[:, q0:q1], k[:, :q1]).astype(jnp.float32) * scale
        s = s + cum[:, :, q0:q1, None] - cum[:, :, None, :q1]
        causal = jnp.arange(q1)[None, :] <= jnp.arange(q0, q1)[:, None]
        p = jax.nn.softmax(jnp.where(causal, s, -jnp.inf), axis=-1)
        outs.append(jnp.einsum('bhqk,bkhd->bqhd', p.astype(v.dtype), v[:, :q1]))
    o = jnp.concatenate(outs, axis=1).reshape(bsz, seq, D_MODEL)
    return o @ w_out

def _conv_module(h, w_pw1, b_pw1, w_dw, b_dw, ln_g, ln_b, w_pw2, b_pw2):
    u = h @ w_pw1 + b_pw1
    u = u[..., :D_MODEL] * jax.nn.sigmoid(u[..., D_MODEL:])
    u = lax.conv_general_dilated(
        u, w_dw[:, None, :].astype(u.dtype), window_strides=(1,),
        padding=[(CONV_WIDTH - 1, 0)], dimension_numbers=('NWC', 'WIO', 'NWC'),
        feature_group_count=D_MODEL) + b_dw
    u = jax.nn.silu(_layer_norm(u, ln_g, ln_b))
    return u @ w_pw2 + b_pw2

def _diff_mixer(h, cos, sin, w_in, q_gain, k_gain, lam_q1, lam_k1, lam_q2, lam_k2,
                sub_gain, w_out, lambda_init):
    bsz, seq, _ = h.shape
    proj = h @ w_in
    q = proj[..., :D_MODEL].reshape(bsz, seq, DIFF_HEADS, 2, HEAD_DIM)
    k = proj[..., D_MODEL:2 * D_MODEL].reshape(bsz, seq, DIFF_HEADS, 2, HEAD_DIM)
    v = proj[..., 2 * D_MODEL:].reshape(bsz, seq, DIFF_HEADS, 2 * HEAD_DIM)
    q = _partial_rope(_rms_norm(q, q_gain), cos, sin)
    k = _partial_rope(_rms_norm(k, k_gain), cos, sin)
    lam = (jnp.exp(jnp.sum(lam_q1.astype(jnp.float32) * lam_k1.astype(jnp.float32)))
           - jnp.exp(jnp.sum(lam_q2.astype(jnp.float32) * lam_k2.astype(jnp.float32)))
           + lambda_init)
    scale = HEAD_DIM ** -0.5
    outs = []
    for q0 in range(0, seq, Q_BLOCK):
        q1 = q0 + Q_BLOCK
        s = jnp.einsum('bqhmd,bkhmd->bhmqk', q[:, q0:q1], k[:, :q1]).astype(jnp.float32) * scale
        visible = (jnp.arange(q1)[None, :] // CHUNK) <= (jnp.arange(q0, q1)[:, None] // CHUNK)
        p = jax.nn.softmax(jnp.where(visible, s, -jnp.inf), axis=-1)
        a = p[:, :, 0] - lam * p[:, :, 1]
        outs.append(jnp.einsum('bhqk,bkhe->bqhe', a.astype(v.dtype), v[:, :q1]))
    o = jnp.concatenate(outs, axis=1)
    o = _rms_norm(o, sub_gain) * (1.0 - lambda_init)
    return o.reshape(bsz, seq, D_MODEL) @ w_out

def setup_inputs(seed: int = 0) -> dict:
    key = jax.random.key(seed)
    ks = iter(list(jax.random.split(key, 40)))
    f32 = jnp.float32

    def nrm(shape, fan_in):
        return jax.random.normal(next(ks), shape, f32) * (fan_in ** -0.5)

    def gain(shape):
        return 1.0 + 0.05 * jax.random.normal(next(ks), shape, f32)

    def bias(shape):
        return 0.02 * jax.random.normal(next(ks), shape, f32)

    x = jax.random.normal(next(ks), (BATCH, SEQ, D_MODEL), f32)
    offset = CHUNK * jax.random.randint(next(ks), (BATCH, 1), 0, 64, dtype=jnp.int32)
    positions = (jnp.arange(SEQ, dtype=jnp.int32)[None, :] + offset).astype(jnp.int32)
    return {
        'x': x,
        'positions': positions,
        'norm_ffn1': gain((DEPTH, D_MODEL)),
        'norm_mix': gain((DEPTH, D_MODEL)),
        'norm_ffn2': gain((DEPTH, D_MODEL)),
        'ffn1_w_gate': nrm((DEPTH, D_MODEL, D_FF), D_MODEL),
        'ffn1_w_up': nrm((DEPTH, D_MODEL, D_FF), D_MODEL),
        'ffn1_w_down': nrm((DEPTH, D_FF, D_MODEL), D_FF),
        'ffn2_w_gate': nrm((DEPTH, D_MODEL, D_FF), D_MODEL),
        'ffn2_w_up': nrm((DEPTH, D_MODEL, D_FF), D_MODEL),
        'ffn2_w_down': nrm((DEPTH, D_FF, D_MODEL), D_FF),
        'fox_w_in': nrm((N_FOX, D_MODEL, 3 * D_MODEL + FOX_HEADS), D_MODEL),
        'fox_b_f': 1.0 + 3.0 * jax.random.uniform(next(ks), (N_FOX, FOX_HEADS), f32),
        'fox_q_gain': gain((N_FOX, HEAD_DIM)),
        'fox_k_gain': gain((N_FOX, HEAD_DIM)),
        'fox_w_out': nrm((N_FOX, D_MODEL, D_MODEL), D_MODEL),
        'conv_w_pw1': nrm((N_CONV, D_MODEL, 2 * D_MODEL), D_MODEL),
        'conv_b_pw1': bias((N_CONV, 2 * D_MODEL)),
        'conv_w_dw': nrm((N_CONV, CONV_WIDTH, D_MODEL), CONV_WIDTH),
        'conv_b_dw': bias((N_CONV, D_MODEL)),
        'conv_ln_g': gain((N_CONV, D_MODEL)),
        'conv_ln_b': bias((N_CONV, D_MODEL)),
        'conv_w_pw2': nrm((N_CONV, D_MODEL, D_MODEL), D_MODEL),
        'conv_b_pw2': bias((N_CONV, D_MODEL)),
        'diff_w_in': nrm((N_DIFF, D_MODEL, 3 * D_MODEL), D_MODEL),
        'diff_q_gain': gain((N_DIFF, HEAD_DIM)),
        'diff_k_gain': gain((N_DIFF, HEAD_DIM)),
        'diff_lambda_q1': 0.1 * jax.random.normal(next(ks), (N_DIFF, HEAD_DIM), f32),
        'diff_lambda_k1': 0.1 * jax.random.normal(next(ks), (N_DIFF, HEAD_DIM), f32),
        'diff_lambda_q2': 0.1 * jax.random.normal(next(ks), (N_DIFF, HEAD_DIM), f32),
        'diff_lambda_k2': 0.1 * jax.random.normal(next(ks), (N_DIFF, HEAD_DIM), f32),
        'diff_sub_gain': gain((N_DIFF, 2 * HEAD_DIM)),
        'diff_w_out': nrm((N_DIFF, D_MODEL, D_MODEL), D_MODEL),
    }

def reference(x, positions, norm_ffn1, norm_mix, norm_ffn2,
              ffn1_w_gate, ffn1_w_up, ffn1_w_down, ffn2_w_gate, ffn2_w_up, ffn2_w_down,
              fox_w_in, fox_b_f, fox_q_gain, fox_k_gain, fox_w_out,
              conv_w_pw1, conv_b_pw1, conv_w_dw, conv_b_dw, conv_ln_g, conv_ln_b,
              conv_w_pw2, conv_b_pw2,
              diff_w_in, diff_q_gain, diff_k_gain, diff_lambda_q1, diff_lambda_k1,
              diff_lambda_q2, diff_lambda_k2, diff_sub_gain, diff_w_out):
    inv_freq = ROPE_THETA ** (-jnp.arange(0, ROT_DIM, 2, dtype=jnp.float32) / ROT_DIM)
    ang = positions.astype(jnp.float32)[..., None] * inv_freq
    cos = jnp.cos(ang)[:, :, None, None, :].astype(x.dtype)
    sin = jnp.sin(ang)[:, :, None, None, :].astype(x.dtype)

    i_fox = 0
    i_conv = 0
    i_diff = 0
    for i in range(DEPTH):
        x = x + 0.5 * _swiglu(_rms_norm(x, norm_ffn1[i]), ffn1_w_gate[i], ffn1_w_up[i], ffn1_w_down[i])
        h = _rms_norm(x, norm_mix[i])
        kind = i % N_MIXERS
        if kind == 0:
            y = _fox_mixer(h, fox_w_in[i_fox], fox_b_f[i_fox], fox_q_gain[i_fox],
                           fox_k_gain[i_fox], fox_w_out[i_fox])
            i_fox += 1
        elif kind == 1:
            y = _conv_module(h, conv_w_pw1[i_conv], conv_b_pw1[i_conv], conv_w_dw[i_conv],
                             conv_b_dw[i_conv], conv_ln_g[i_conv], conv_ln_b[i_conv],
                             conv_w_pw2[i_conv], conv_b_pw2[i_conv])
            i_conv += 1
        else:
            lambda_init = 0.8 - 0.6 * math.exp(-0.3 * i)
            y = _diff_mixer(h, cos, sin, diff_w_in[i_diff], diff_q_gain[i_diff],
                            diff_k_gain[i_diff], diff_lambda_q1[i_diff], diff_lambda_k1[i_diff],
                            diff_lambda_q2[i_diff], diff_lambda_k2[i_diff],
                            diff_sub_gain[i_diff], diff_w_out[i_diff], lambda_init)
            i_diff += 1
        x = x + y
        x = x + 0.5 * _swiglu(_rms_norm(x, norm_ffn2[i]), ffn2_w_gate[i], ffn2_w_up[i], ffn2_w_down[i])
    return x


_drawn_inputs = setup_inputs


def setup_inputs(seed=0):
    import zlib

    import numpy as np

    out = dict(_drawn_inputs(seed))
    spreads = {}
    factors = {'fox_q_gain': 2.878,
     'fox_k_gain': 2.783,
     'conv_b_pw1': 3.614,
     'conv_ln_b': 3.774,
     'diff_q_gain': 2.877,
     'diff_k_gain': 3.156,
     'diff_lambda_k2': 8.0,
     'diff_sub_gain': 2.887}
    for name, (base, spread) in spreads.items():
        noise = np.random.default_rng([zlib.crc32(name.encode()), seed]).standard_normal(out[name].shape)
        drawn = base * np.exp(spread * noise) if base else spread * noise
        out[name] = jnp.asarray(drawn.astype(out[name].dtype))
    for name, factor in factors.items():
        out[name] = (out[name] * factor).astype(out[name].dtype)
    return out
```

```python
import math
from contextlib import ExitStack

import concourse.bass as bass
from concourse import mybir

F32 = mybir.dt.float32
F32R = mybir.dt.float32r
I32 = mybir.dt.int32
ALU = mybir.AluOpType
ACT = mybir.ActivationFunctionType
AX = mybir.AxisListType

P = 128
DEPTH = 4
SEQ = 256
D = 1024
KT = D // P
D_FF = ((8 * D // 3 + 127) // 128) * 128
PAIRS = D_FF // 256
HEAD = 64
FOX_HEADS = D // HEAD
GROUPS = D // 256
TAPS = 31
ROT = HEAD // 4
ROPE_THETA = 500000.0
EPS = 1e-6
RING = 3
MASKED = -1e30
ROUND = 1.5 * 2.0 ** 23
TWO_PI_1, TWO_PI_2 = 6.28125, 1.9350051879882812e-3
TWO_PI_3 = 2.0 * math.pi - TWO_PI_1 - TWO_PI_2

MIXERS = ["fox", "conv", "diff"]
PHASES = [k for i in range(DEPTH) for k in ("ffn", MIXERS[i % 3], "ffn")]
BLOCKS = {"ffn": 3 * PAIRS, "fox": 4 * GROUPS, "conv": 3 * GROUPS, "diff": 4 * GROUPS}

NORM_COL = 0
PW1_COL = NORM_COL + 3 * DEPTH * KT
DW_B_COL = PW1_COL + 16
LN_G_COL = DW_B_COL + KT
LN_B_COL = LN_G_COL + KT
PW2_COL = LN_B_COL + KT
HEAD_COL = PW2_COL + KT
DW_COL = HEAD_COL + 7
VEC_COLS = DW_COL + TAPS * KT


def build_trunk(nc, A, out):
    phases = PHASES
    starts = [sum(BLOCKS[k] for k in phases[:i]) for i in range(len(phases) + 1)]
    n_blocks = starts[-1]

    def number(i):
        family = {"ffn": ("ffn",), "fox": ("fox", "diff"), "diff": ("fox", "diff"), "conv": ("conv",)}[phases[i]]
        return sum(k in family for k in phases[:i])

    def layer_of(i):
        return i // 3

    with ExitStack() as ctx:
        def sb(name, shape, dt=F32):
            return ctx.enter_context(nc.sbuf_tensor("sb_" + name, shape, dt))

        def sem(name):
            return ctx.enter_context(nc.semaphore(name))

        raw = [sb(f"raw{i}", [P, 2048]) for i in range(RING)]
        w_high = [sb(f"w_high{i}", [P, 2048], F32R) for i in range(RING)]
        w_low = [sb(f"w_low{i}", [P, 2048], F32R) for i in range(RING)]

        xT = sb("xT", [P, KT, SEQ])
        x_square = sb("x_square", [P, KT, SEQ])
        x_high = sb("x_high", [P, KT, SEQ], F32R)
        x_low = sb("x_low", [P, KT, SEQ], F32R)
        root = sb("root", [P, SEQ + 2])
        inv_rms = sb("inv_rms", [P, SEQ + 2])

        gate_in = sb("gate_in", [P, 512])
        gate_silu = sb("gate_silu", [P, 512])
        gate_scaled = sb("gate_scaled", [P, 512])
        hidden = sb("hidden", [P, 512])
        h_high = [sb(f"h_high{i}", [P, 512], F32R) for i in range(2)]
        h_low = [sb(f"h_low{i}", [P, 512], F32R) for i in range(2)]

        q_raw, k_raw = sb("q_raw", [P, 512]), gate_scaled
        q_square, k_square = sb("q_square", [P, 512]), sb("k_square", [P, 512])
        q_inv, k_inv = sb("q_inv", [P, 512]), sb("k_inv", [P, 512])
        qT, kT = sb("qT", [P, 512]), sb("kT", [P, 512])
        v_nat = sb("v_nat", [P, 2, 256])
        scores = [sb(f"scores{i}", [P, 384]) for i in range(2)]
        probsT = [sb(f"probsT{i}", [P, 384]) for i in range(2)]
        neg_max = [sb(f"neg_max{i}", [P, 2]) for i in range(2)]
        row_sum = [sb(f"row_sum{i}", [P, 2]) for i in range(2)]
        inv_sum = [sb(f"inv_sum{i}", [P, 2]) for i in range(2)]
        lam_inv_sum = sb("lam_inv_sum", [P, 2])
        o_high = sb("o_high", [P, KT, SEQ], F32R)
        o_low = sb("o_low", [P, KT, SEQ], F32R)
        gate_w = sb("gate_w", [P, KT, FOX_HEADS])
        gate_w_high = sb("gate_w_high", [P, KT, FOX_HEADS], F32R)
        gate_w_low = sb("gate_w_low", [P, KT, FOX_HEADS], F32R)
        logit = sb("logit", [P, 2, FOX_HEADS])
        logit_abs = sb("logit_abs", [P, 2, FOX_HEADS])
        logit_neg = sb("logit_neg", [P, 2, FOX_HEADS])
        log_f = sb("log_f", [P, 2, FOX_HEADS])
        cum_q = sb("cum_q", [P, 2 * FOX_HEADS])
        neg_cumT = sb("neg_cumT", [FOX_HEADS, SEQ])
        wide = sb("wide", [P, FOX_HEADS * SEQ])
        neg_cum_heads = wide[:, :].rearrange("p (h n) -> p h n", h=FOX_HEADS)
        by_token = [wide[:, tt * D:(tt + 1) * D] for tt in range(2)]
        u_pad = sb("u_pad", [P, KT, TAPS - 1 + SEQ])
        y_conv = x_square
        ln_work = u_pad[:, :, TAPS - 1:]
        ln_inv = q_raw[:, 0:SEQ]

        ident = sb("ident", [P, P])
        ones = sb("ones", [P, P])
        ones_heads = sb("ones_heads", [P, P])
        upper = sb("upper", [P, P])
        causal = sb("causal", [P, 384])
        chunked = sb("chunked", [P, 384])
        swap = sb("swap", [P, P])
        vec = sb("vec", [P, VEC_COLS])
        vec_rows = sb("vec_rows", [P, 4, P])
        head_rows = sb("head_rows", [7, P])
        eps = sb("eps", [P, 1])
        half_pi = sb("half_pi", [P, 1])
        rope_rows = sb("rope_rows", [1, 3, P])
        rope_cols = sb("rope_cols", [P, 3])
        not_rotated = sb("not_rotated", [P, 1])
        pos_int = sb("pos_int", [1, SEQ], I32)
        pos_row = sb("pos_row", [1, SEQ])
        angle, turns = q_inv[:, 0:SEQ], k_inv[:, 0:SEQ]
        cosT, sinT = sb("cosT", [P, SEQ]), sb("sinT", [P, SEQ])
        fox_bias_row = sb("fox_bias_row", [1, 2 * FOX_HEADS])
        fox_bias = sb("fox_bias", [P, 2 * FOX_HEADS])
        lam_rows = sb("lam_rows", [1, 4, HEAD])
        lam_products = sb("lam_products", [1, 2, HEAD])
        lam_sums = sb("lam_sums", [1, 2])
        lam_exps = sb("lam_exps", [1, 2])
        neg_lam_row = sb("neg_lam_row", [1, 1])
        neg_lam = sb("neg_lam", [P, 1])

        bank = [ctx.enter_context(nc.psum_tensor(f"bank{i}", [P, 512], F32)) for i in range(8)]

        names = (
            "x_loaded vec_loaded const_loaded pool_consts dve_consts out_stored "
            "block_done out_bank_done sumsq_done high_ready low_ready "
            "x_ready xhigh_ready xsq_ready xlow_ready root_ready inv_rms_ready "
            "gate_in_ready silu_ready gate_scaled_ready hidden_ready h_high_ready h_low_ready "
            "x_turned vec_turned vec_copied small_done rope_step act_rope_step lam_step "
            "q_raw_ready k_raw_ready q_sq_ready k_sq_ready q_log_ready k_log_ready q_inv_ready k_inv_ready "
            "q_sum_done k_sum_done q_normed k_normed q_swapped k_swapped q_cos q_sin k_cos k_sin "
            "q_ready k_ready v_ready v_half_ready scores_done score_added masked exp_ready exp_half "
            "inv_sum_ready probs_ready probs_half probs_turned probsT_ready pv_done o_high_ready o_bank_free "
            "o_copied o_sq_ready o_sum_done o_log_ready o_inv_ready o_normed lam_scaled "
            "gate_w_loaded gate_w_high_ready gate_w_low_ready logits_done logit_ready logit_parts log_f_ready "
            "logit_neg_ready cum_done cum_q_ready neg_cumT_ready neg_cum_ready "
            "conv_a_ready conv_g_ready sigmoid_ready u_ready tap_done mean_done centred centred_sq var_done "
            "ln_root_ready ln_inv_ready ln_scaled ln_silu "
            "final_turned final_copied wide_zeroed"
        ).split()
        S = {n: sem(n) for n in names}
        raw_landed = [sem(f"raw_landed{i}") for i in range(RING)]

        def raw_uses(b, u=0, per=0):
            return 16 * (b // RING + 1) + u * (16 * per // RING)

        def pair(t):
            return t.rearrange("p (a n) -> p a n", a=2)

        def over_tokens(row, n=2):
            return row.unsqueeze(1).broadcast_to([P, n, SEQ])

        fox_scale = HEAD ** -0.5
        lambda_init = 0.8 - 0.6 * math.exp(-0.3 * 2)

        N_POOL_CONSTS = 15
        DVE_CONSTS = 19
        turned_before = [sum({"fox": FOX_HEADS, "diff": FOX_HEADS // 2}.get(k, 0) for k in phases[:i])
                         for i in range(len(phases))]
        o_before = [GROUPS * sum(k != "ffn" for k in phases[:i]) for i in range(len(phases))]

        block = ctx.enter_context(nc.Block())

        @block.sync
        def _(sp):
            def load(b, src, u=0, per=0):
                if b >= RING or not isinstance(u, int):
                    sp.wait_ge(S["low_ready"], b - RING + 1 + u * per)
                dst = raw[b % RING][:, :].rearrange("p (k n) -> p k n", k=src.shape[1])
                sp.dma_start(dst, src).then_inc(raw_landed[b % RING], 16)

            def columns(w, at):
                return w[:, bass.ds(at, 256)].rearrange("(k p) n -> p k n", p=P)

            def rows(w, at):
                return w[bass.ds(at, 256), :].rearrange("(f p) n -> p f n", p=P)

            for tt in range(2):
                sp.dma_start(by_token[tt], A["x"][0, tt * P:(tt + 1) * P, :]).then_inc(S["x_loaded"], 16)

            for i, kind in enumerate(phases):
                b, n, layer = starts[i], number(i), layer_of(i)
                if kind == "ffn":
                    which = "ffn1" if i % 3 == 0 else "ffn2"
                    wg, wu, wd = (A[f"{which}_w_{m}"][layer] for m in ("gate", "up", "down"))
                    def two_pairs(u):
                        for q in range(2):
                            at = u * 512 + (q + 1) * 256
                            load(b + 2 + 3 * q, columns(wg, at), u, 6)
                            load(b + 3 + 3 * q, columns(wu, at), u, 6)
                            load(b + 4 + 3 * q, rows(wd, at - 256), u, 6)

                    load(b, columns(wg, 0))
                    load(b + 1, columns(wu, 0))
                    two_pairs(0)
                    with sp.Fori(1, (PAIRS - 1) // 2) as u:
                        two_pairs(u)
                    load(b + 3 * PAIRS - 1, rows(wd, (PAIRS - 1) * 256))
                elif kind == "conv":
                    for j in range(GROUPS):
                        load(b + 2 * j, columns(A["conv_w_pw1"][0], 256 * j))
                        load(b + 2 * j + 1, columns(A["conv_w_pw1"][0], D + 256 * j))
                    for j in range(GROUPS):
                        load(b + 2 * GROUPS + j, rows(A["conv_w_pw2"][0], 256 * j))
                else:
                    which = layer // 3
                    w_in, w_out = A[kind + "_w_in"][which], A[kind + "_w_out"][which]
                    if kind == "fox":
                        if n:
                            sp.wait_ge(S["gate_w_low_ready"], which)
                        sp.dma_start(gate_w[:, :, :],
                                     w_in[:, 3 * D:3 * D + FOX_HEADS].rearrange("(k p) n -> p k n", p=P)
                                     ).then_inc(S["gate_w_loaded"], 16)
                    for part in range(3):
                        load(b + part, columns(w_in, part * D))
                    with sp.Fori(0, GROUPS - 1) as u:
                        for part in range(3):
                            load(b + 3 + part, columns(w_in, u * 256 + part * D + 256), u, 3)
                    for j in range(GROUPS):
                        load(b + 3 * GROUPS + j, rows(w_out, 256 * j))
            for tt in range(2):
                sp.wait_ge(S["final_copied"], 2 * (tt + 1))
                sp.dma_start(out[0, tt * P:(tt + 1) * P, :], by_token[tt]).then_inc(S["out_stored"], 16)
            sp.wait_ge(S["out_stored"], 32)

        @block.gpsimd
        def _(pool):
            zero = [ident, ones_heads, swap, causal, chunked]
            for t in zero:
                pool.memset(t[:, :], 0.0).then_inc(S["pool_consts"], 1)
            pool.memset(ones[:, :], 1.0).then_inc(S["pool_consts"], 1)
            pool.memset(u_pad[:, :, 0:TAPS - 1], 0.0).then_inc(S["pool_consts"], 1)
            pool.wait_ge(S["pool_consts"], 7)
            pool.affine_select(out=ident[:, :], in_=ident[:, :], compare_op=ALU.not_equal, fill=1.0, base=0,
                               pattern=[[-1, P]], channel_multiplier=1).then_inc(S["pool_consts"], 1)
            pool.affine_select(out=upper[:, :], in_=ones[:, :], compare_op=ALU.is_ge, fill=0.0, base=0,
                               pattern=[[1, P]], channel_multiplier=-1).then_inc(S["pool_consts"], 1)
            done = 9
            for at in (0, 256):
                pool.affine_select(out=causal[:, at:at + P], in_=causal[:, at:at + P], compare_op=ALU.is_ge,
                                   fill=MASKED, base=0, pattern=[[-1, P]],
                                   channel_multiplier=1).then_inc(S["pool_consts"], 1)
                pool.wait_ge(S["pool_consts"], done + 1)
                pool.memset(chunked[0:HEAD, at + HEAD:at + P], MASKED).then_inc(S["pool_consts"], 1)
                pool.wait_ge(S["pool_consts"], done + 2)
                done += 2
            for m in range(2):
                r = slice(HEAD * m, HEAD * m + HEAD)
                pool.memset(ones_heads[r, r], 1.0).then_inc(S["pool_consts"], 1)
                pool.wait_ge(S["pool_consts"], done + 1 + m)
            pool.wait_ge(S["x_turned"], 4)
            pool.memset(wide[:, :], 0.0).then_inc(S["wide_zeroed"], 1)
            pool.wait_ge(S["wide_zeroed"], 1)
            for i, kind in enumerate(phases):
                if kind == "fox":
                    w = i // 9
                    pool.wait_ge(S["neg_cumT_ready"], w + 1)
                    pool.tensor_tensor(neg_cum_heads[0:FOX_HEADS, :, :],
                                       neg_cumT[:, :].unsqueeze(1).broadcast_to([FOX_HEADS, FOX_HEADS, SEQ]),
                                       ident[0:FOX_HEADS, 0:FOX_HEADS].unsqueeze(2)
                                       .broadcast_to([FOX_HEADS, FOX_HEADS, SEQ]),
                                       ALU.mult).then_inc(S["neg_cum_ready"], 1)


        @block.scalar
        def _(act):
            def rows_of(v):
                return v.rearrange("a (t p) -> (a t) p", p=P)

            for kind, name in enumerate(("norm_ffn1", "norm_mix", "norm_ffn2")):
                act.dma_start(vec_rows[32 * kind:32 * kind + 32, 0, :], rows_of(A[name])).then_inc(S["vec_loaded"], 16)
            at = 0
            for name in ("conv_b_pw1", "conv_b_dw", "conv_ln_g", "conv_ln_b", "conv_b_pw2"):
                n = 16 if name == "conv_b_pw1" else 8
                act.dma_start(vec_rows[at:at + n, 1, :], rows_of(A[name])).then_inc(S["vec_loaded"], 16)
                at += n
            taps = rows_of(A["conv_w_dw"][0])
            for half in range(2):
                act.dma_start(vec_rows[0:124, 2 + half, :], taps[124 * half:124 * half + 124, :]
                              ).then_inc(S["vec_loaded"], 16)
            r = 0
            for name, n in (("fox_q_gain", 2), ("fox_k_gain", 2), ("diff_q_gain", 1), ("diff_k_gain", 1)):
                for half in range(2):
                    act.dma_start(head_rows[r:r + n, HEAD * half:HEAD * half + HEAD], A[name]
                                  ).then_inc(S["vec_loaded"], 16)
                r += n
            act.dma_start(head_rows[6:7, :], A["diff_sub_gain"]).then_inc(S["vec_loaded"], 16)
            act.dma_start(pos_int[:, :], A["positions"]).then_inc(S["const_loaded"], 16)
            act.dma_start(fox_bias_row[:, :], A["fox_b_f"].rearrange("(o a) n -> o (a n)", o=1)
                          ).then_inc(S["const_loaded"], 16)
            for m, name in enumerate(("q1", "k1", "q2", "k2")):
                act.dma_start(lam_rows[:, m, :], A["diff_lambda_" + name]).then_inc(S["const_loaded"], 16)

            def split_high(b, u=0, per=0):
                if b >= n_blocks:
                    return
                act.wait_ge(raw_landed[b % RING], raw_uses(b, u, per))
                if b >= RING:
                    act.wait_ge(S["block_done"], b - RING + 1 + u * per)
                act.activation(w_high[b % RING][:, :], raw[b % RING][:, :], ACT.Copy).then_inc(S["high_ready"], 1)

            def boundary(i):
                col = NORM_COL + (i % 3) * DEPTH * KT + layer_of(i) * KT
                if i == 0:
                    act.wait_ge(S["vec_copied"], 5)
                for T in range(4):
                    act.wait_ge(S["x_ready"], 4 * i + T + 1)
                    for t in (2 * T, 2 * T + 1):
                        act.activation(x_high[:, t, :], xT[:, t, :], ACT.Copy, scale=vec[:, col + t:col + t + 1]
                                       ).then_inc(S["xhigh_ready"], 1)
                    act.activation(x_square[:, 2 * T:2 * T + 2, :], xT[:, 2 * T:2 * T + 2, :], ACT.Square
                                   ).then_inc(S["xsq_ready"], 1)
                split_high(starts[i] + 1)
                width = SEQ + 2 if phases[i] in ("fox", "diff") else SEQ
                act.wait_ge(S["sumsq_done"], i + 1)
                if i:
                    act.wait_ge(S["inv_rms_ready"], i)
                act.activation(root[:, 0:width], bank[7][:, 0:width], ACT.Sqrt, scale=1.0 / D, bias=eps[:, :]
                               ).then_inc(S["root_ready"], 1)

            def ffn(i):
                b, f = starts[i], number(i)

                def silu(p, u=0):
                    act.wait_ge(S["gate_in_ready"], PAIRS * f + p + 1 + 2 * u)
                    act.activation(gate_silu[:, :], gate_in[:, :], ACT.Silu).then_inc(S["silu_ready"], 1)

                def high(p, u=0):
                    act.wait_ge(S["hidden_ready"], PAIRS * f + p + 1 + 2 * u)
                    act.activation(h_high[p % 2][:, :], hidden[:, :], ACT.Copy).then_inc(S["h_high_ready"], 1)

                def one_pair(p, u=0):
                    split_high(b + 3 * p + 1, u, 6)
                    silu(p, u)
                    split_high(b + 3 * p + 2, u, 6)
                    high(p, u)
                    split_high(b + 3 * p + 3, u, 6)

                split_high(b + 2)
                silu(0)
                split_high(b + 3)
                high(0)
                last = i == len(phases) - 1
                with act.Fori(0, (PAIRS - 1) // 2 - last) as u:
                    one_pair(1, u)
                    one_pair(2, u)
                if last:
                    one_pair(PAIRS - 2)
                    one_pair(PAIRS - 1)

            def attention(i):
                a, b, fox = number(i), starts[i], phases[i] == "fox"
                w = i // 9

                def inverse(x, g, u):
                    buf, at, n = {"q": (q_inv, 3, HEAD), "k": (k_inv, 3, HEAD), "o": (q_square, 6, P)}[x]
                    c = (0 if x == "o" else 4 * a) + g + u + 1
                    act.wait_ge(S[x + "_sum_done"], c)
                    act.activation(buf[:, :], bank[at][:, :], ACT.Ln, scale=1.0 / n, bias=eps[:, :]
                                   ).then_inc(S[x + "_log_ready"], 1)
                    act.wait_ge(S[x + "_log_ready"], c)
                    act.activation(buf[:, :], buf[:, :], ACT.Exp, scale=-0.5).then_inc(S[x + "_inv_ready"], 1)

                def square(x, g, u):
                    src, dst = {"q": (q_raw, q_square), "k": (k_raw, k_square)}[x]
                    act.wait_ge(S[x + "_raw_ready"], 4 * a + g + u + 1)
                    act.activation(dst[:, :], src[:, :], ACT.Square).then_inc(S[x + "_sq_ready"], 1)

                def exps(m, g, u):
                    c = 16 * a + 4 * g + m + 4 * u
                    act.wait_ge(S["masked"], c + 1)
                    s = scores[m % 2]
                    for qb, cols in enumerate((slice(0, P), slice(P, 384))):
                        act.activation(s[:, cols], s[:, cols], ACT.Exp, bias=neg_max[m % 2][:, qb:qb + 1],
                                       accum_out=row_sum[m % 2][:, qb:qb + 1]).then_inc(S["exp_ready"], 1)

                def copy_probs(m, g, u):
                    per = 4 if fox else 2
                    c = turned_before[i] + per * g + m + per * u
                    act.wait_ge(S["probs_turned"], c + 1)
                    src = bank[([6, 5, 6, 4] if fox else [6, 6])[m]]
                    act.activation(probsT[m % 2][:, :], src[:, 0:384], ACT.Copy).then_inc(S["probsT_ready"], 1)

                def o_part(g, u):
                    c = turned_before[i] + (4 if fox else 2) * (g + u + 1)
                    act.wait_ge(S["pv_done"], c)
                    if fox:
                        src = pair(bank[7][:, :])
                    else:
                        act.activation(hidden[:, :], bank[7][:, :], ACT.Copy).then_inc(S["o_copied"], 1)
                        act.activation(gate_in[:, :], bank[7][:, :], ACT.Square).then_inc(S["o_sq_ready"], 1)
                        inverse("o", g, u)
                        act.wait_ge(S["o_normed"], g + u + 1)
                        src = pair(gate_silu[:, :])
                    act.activation(o_high[:, bass.ds(2 * (g + u), 2), :], src, ACT.Copy).then_inc(S["o_high_ready"], 1)

                def group(j, u=0):
                    g = j - 1
                    split_high(b + 3 * j + 2, u, 3)
                    square("q", j, u)
                    if j:
                        exps(0, g, u)
                        exps(1, g, u)
                    split_high(b + 3 * j + 3, u, 3)
                    if j:
                        copy_probs(0, g, u)
                        if fox:
                            copy_probs(1, g, u)
                        exps(2, g, u)
                    square("k", j, u)
                    inverse("q", j, u)
                    if j:
                        exps(3, g, u)
                    split_high(b + 3 * j + 4, u, 3)
                    inverse("k", j, u)
                    if j:
                        if fox:
                            copy_probs(2, g, u)
                            copy_probs(3, g, u)
                        else:
                            copy_probs(1, g, u)
                        o_part(g, u)

                if fox:
                    act.wait_ge(S["gate_w_loaded"], 16 * (w + 1))
                    act.activation(gate_w_high[:, :, :], gate_w[:, :, :], ACT.Copy).then_inc(S["gate_w_high_ready"], 1)
                    act.wait_ge(S["logit_ready"], 2 * w + 2)
                    act.activation(logit_abs[:, :, :], logit[:, :, :], ACT.Abs).then_inc(S["logit_parts"], 1)
                    act.wait_ge(S["logit_parts"], 3 * w + 1)
                    act.activation(logit_abs[:, :, :], logit_abs[:, :, :], ACT.Exp, scale=-1.0
                                   ).then_inc(S["logit_parts"], 1)
                    act.wait_ge(S["logit_parts"], 3 * w + 2)
                    act.activation(logit_abs[:, :, :], logit_abs[:, :, :], ACT.Ln, bias=ones[:, 0:1]
                                   ).then_inc(S["logit_parts"], 1)
                group(0)
                if fox:
                    act.wait_ge(S["cum_done"], w + 1)
                    act.activation(neg_cumT[:, :], bank[6][0:FOX_HEADS, P:P + SEQ], ACT.Copy, scale=-1.0
                                   ).then_inc(S["neg_cumT_ready"], 1)
                with act.Fori(0, GROUPS - 1) as u:
                    group(1, u)
                g = GROUPS - 1
                e = b + 3 * GROUPS
                exps(0, g, 0)
                exps(1, g, 0)
                split_high(e + 2)
                copy_probs(0, g, 0)
                if fox:
                    copy_probs(1, g, 0)
                exps(2, g, 0)
                exps(3, g, 0)
                split_high(e + 3)
                if fox:
                    copy_probs(2, g, 0)
                    copy_probs(3, g, 0)
                else:
                    copy_probs(1, g, 0)
                split_high(e + 4)
                o_part(g, 0)

            def conv(i):
                b = starts[i]
                for j in range(GROUPS):
                    split_high(b + 2 * j + 2)
                    split_high(b + 2 * j + 3)
                    act.wait_ge(S["conv_g_ready"], j + 1)
                    for m in range(2):
                        col = PW1_COL + KT + 2 * j + m
                        act.activation(gate_silu[:, m * SEQ:(m + 1) * SEQ], gate_scaled[:, m * SEQ:(m + 1) * SEQ],
                                       ACT.Sigmoid, bias=vec[:, col:col + 1]).then_inc(S["sigmoid_ready"], 1)
                for T in range(4):
                    act.wait_ge(S["centred"], T + 1)
                    act.activation(ln_work[:, 2 * T:2 * T + 2, :], y_conv[:, 2 * T:2 * T + 2, :], ACT.Square
                                   ).then_inc(S["centred_sq"], 1)
                act.wait_ge(S["var_done"], 1)
                act.activation(root[:, 0:SEQ], bank[5][:, 0:SEQ], ACT.Sqrt, scale=1.0 / D, bias=eps[:, :]
                               ).then_inc(S["ln_root_ready"], 1)
                e = b + 2 * GROUPS
                for T in range(4):
                    act.wait_ge(S["ln_scaled"], T + 1)
                    for t in (2 * T, 2 * T + 1):
                        act.activation(ln_work[:, t, :], y_conv[:, t, :], ACT.Silu,
                                       scale=vec[:, LN_G_COL + t:LN_G_COL + t + 1],
                                       bias=vec[:, LN_B_COL + t:LN_B_COL + t + 1]).then_inc(S["ln_silu"], 1)
                    act.wait_ge(S["ln_silu"], 2 * T + 2)
                    act.activation(o_high[:, 2 * T:2 * T + 2, :], ln_work[:, 2 * T:2 * T + 2, :], ACT.Copy
                                   ).then_inc(S["o_high_ready"], 1)
                for k in range(2, 5):
                    split_high(e + k)

            act.wait_ge(S["pool_consts"], N_POOL_CONSTS)
            act.wait_ge(S["dve_consts"], DVE_CONSTS)
            split_high(0)
            act.wait_ge(S["lam_step"], 2)
            act.activation(lam_exps[:, :], lam_sums[:, :], ACT.Exp).then_inc(S["lam_step"], 1)
            act.wait_ge(S["rope_step"], 9)
            act.activation(sinT[:, :], angle[:, :], ACT.Sin).then_inc(S["act_rope_step"], 1)
            act.activation(turns[:, :], angle[:, :], ACT.Abs).then_inc(S["act_rope_step"], 1)
            act.wait_ge(S["act_rope_step"], 2)
            act.activation(cosT[:, :], turns[:, :], ACT.Sin, scale=-1.0, bias=half_pi[:, :]
                           ).then_inc(S["act_rope_step"], 1)
            for i, kind in enumerate(phases):
                boundary(i)
                {"ffn": ffn, "fox": attention, "diff": attention, "conv": conv}[kind](i)

        @block.vector
        def _(dve):
            def split_low(b, u=0, per=0):
                if b >= n_blocks:
                    return
                dve.wait_ge(S["high_ready"], b + 1 + u * per)
                dve.tensor_tensor(w_low[b % RING][:, :], raw[b % RING][:, :], w_high[b % RING][:, :].bitcast(F32),
                                  ALU.subtract).then_inc(S["low_ready"], 1)

            def wait_out_bank(i, T):
                if T < 3:
                    dve.wait_ge(S["out_bank_done"], 3 * (i - 1) + T + 1)
                else:
                    dve.wait_ge(S["block_done"], starts[i])

            def update_x(i, T):
                if i == 0:
                    dve.wait_ge(S["x_turned"], T + 1)
                    dve.tensor_copy(xT[:, 2 * T:2 * T + 2, :], pair(bank[T][:, :])).then_inc(S["x_ready"], 1)
                    return
                wait_out_bank(i, T)
                if phases[i - 1] == "conv":
                    for m in range(2):
                        t = 2 * T + m
                        ins = dve.scalar_tensor_tensor(xT[:, t, :], bank[T][:, m * SEQ:(m + 1) * SEQ],
                                                       vec[:, PW2_COL + t:PW2_COL + t + 1], xT[:, t, :],
                                                       ALU.add, ALU.add)
                    ins.then_inc(S["x_ready"], 1)
                else:
                    weight = 0.5 if phases[i - 1] == "ffn" else 1.0
                    dve.scalar_tensor_tensor(xT[:, 2 * T:2 * T + 2, :], pair(bank[T][:, :]), weight,
                                             xT[:, 2 * T:2 * T + 2, :], ALU.mult, ALU.add).then_inc(S["x_ready"], 1)

            def boundary(i):
                col = NORM_COL + (i % 3) * DEPTH * KT + layer_of(i) * KT

                def low(T):
                    for t in (2 * T, 2 * T + 1):
                        dve.wait_ge(S["xhigh_ready"], 8 * i + t + 1)
                        dve.scalar_tensor_tensor(x_low[:, t, :], xT[:, t, :], vec[:, col + t:col + t + 1],
                                                 x_high[:, t, :].bitcast(F32), ALU.mult, ALU.subtract
                                                 ).then_inc(S["xlow_ready"], 1)

                for T in range(4):
                    update_x(i, T)
                    if T:
                        low(T - 1)
                low(3)
                split_low(starts[i] + 1)
                width = SEQ + 2 if phases[i] in ("fox", "diff") else SEQ
                dve.wait_ge(S["root_ready"], i + 1)
                dve.reciprocal(inv_rms[:, 0:width], root[:, 0:width]).then_inc(S["inv_rms_ready"], 1)
                dve.wait_ge(S["inv_rms_ready"], i + 1)

            def ffn(i):
                b, f = starts[i], number(i)

                def gate(p, u=0):
                    dve.wait_ge(S["block_done"], b + (3 * p if p else 1) + 6 * u)
                    dve.tensor_tensor(pair(gate_in[:, :]), pair(bank[4][:, :]), over_tokens(inv_rms[:, 0:SEQ]),
                                      ALU.mult).then_inc(S["gate_in_ready"], 1)

                def up(p, u=0):
                    c = PAIRS * f + p + 1 + 2 * u
                    dve.wait_ge(S["silu_ready"], c)
                    dve.tensor_tensor(pair(gate_scaled[:, :]), pair(gate_silu[:, :]), over_tokens(inv_rms[:, 0:SEQ]),
                                      ALU.mult).then_inc(S["gate_scaled_ready"], 1)
                    dve.wait_ge(S["gate_scaled_ready"], c)
                    dve.wait_ge(S["block_done"], b + (3 * p + 1 if p else 2) + 6 * u)
                    dve.tensor_tensor(hidden[:, :], bank[5][:, :], gate_scaled[:, :], ALU.mult
                                      ).then_inc(S["hidden_ready"], 1)

                def low(p, u=0):
                    dve.wait_ge(S["h_high_ready"], PAIRS * f + p + 1 + 2 * u)
                    dve.tensor_tensor(h_low[p % 2][:, :], hidden[:, :], h_high[p % 2][:, :].bitcast(F32),
                                      ALU.subtract).then_inc(S["h_low_ready"], 1)

                def one_pair(p, u=0):
                    split_low(b + 3 * p + 1, u, 6)
                    gate(p, u)
                    split_low(b + 3 * p + 2, u, 6)
                    up(p, u)
                    split_low(b + 3 * p + 3, u, 6)
                    low(p, u)

                split_low(b + 2)
                gate(0)
                split_low(b + 3)
                up(0)
                low(0)
                last = i == len(phases) - 1
                with dve.Fori(0, (PAIRS - 1) // 2 - last) as u:
                    one_pair(1, u)
                    one_pair(2, u)
                if last:
                    one_pair(PAIRS - 2)
                    one_pair(PAIRS - 1)

            def attention(i):
                a, b, fox = number(i), starts[i], phases[i] == "fox"
                w = i // 9
                gain = {"q": HEAD_COL + (w if fox else 4), "k": HEAD_COL + (2 + w if fox else 5)}

                def raw_part(x, j, u):
                    src, dst = {"q": (bank[0], q_raw), "k": (bank[1], k_raw)}[x]
                    c = 4 * a + j + u
                    dve.wait_ge(S["block_done"], b + 3 * j + (1 if x == "q" else 2) + 3 * u)
                    if j or a:
                        dve.wait_ge(S[x + "_ready"], c)
                    dve.tensor_tensor(pair(dst[:, :]), pair(src[:, :]), over_tokens(inv_rms[:, 0:SEQ]), ALU.mult
                                      ).then_inc(S[x + "_raw_ready"], 1)

                def normed(x, j, u):
                    raw_, inv, fin = {"q": (q_raw, q_inv, qT), "k": (k_raw, k_inv, kT)}[x]
                    c = 4 * a + j + u + 1
                    dve.wait_ge(S[x + "_inv_ready"], c)
                    dst, ready = (fin, "_ready") if fox else (raw_, "_normed")
                    dve.scalar_tensor_tensor(dst[:, :], raw_[:, :], vec[:, gain[x]:gain[x] + 1], inv[:, :],
                                             ALU.mult, ALU.mult).then_inc(S[x + ready], 1)

                def rotated(x, j, u):
                    raw_, tmp, fin = {"q": (q_raw, q_square, qT), "k": (k_raw, k_square, kT)}[x]
                    c = j + u + 1
                    tmp2 = {"q": q_inv, "k": k_inv}[x]
                    dve.wait_ge(S[x + "_normed"], c)
                    dve.tensor_tensor(pair(tmp2[:, :]), pair(raw_[:, :]), over_tokens(cosT[:, :]), ALU.mult
                                      ).then_inc(S[x + "_cos"], 1)
                    dve.wait_ge(S[x + "_swapped"], c)
                    dve.tensor_tensor(pair(tmp[:, :]), pair(bank[3][:, :]), over_tokens(sinT[:, :]), ALU.mult
                                      ).then_inc(S[x + "_sin"], 1)
                    dve.wait_ge(S[x + "_cos"], c)
                    dve.wait_ge(S[x + "_sin"], c)
                    dve.tensor_tensor(fin[:, :], tmp2[:, :], tmp[:, :], ALU.add).then_inc(S[x + "_ready"], 1)

                def mask_and_max(m, g, u):
                    c = 16 * a + 4 * g + m + 4 * u
                    s, src = scores[m % 2], bank[4 + m % 2]
                    dve.wait_ge(S["scores_done"], c + 1)
                    parts = ((0, slice(0, P)), (1, slice(P, 384)))
                    for qb, cols in parts:
                        if fox:
                            cq = cum_q[:, bass.ds(u * 4 + (FOX_HEADS * qb + 4 * g + m), 1)]
                            dve.scalar_tensor_tensor(s[:, cols], src[:, cols], cq, causal[:, cols],
                                                     ALU.add, ALU.add).then_inc(S["score_added"], 1)
                        else:
                            dve.tensor_tensor(s[:, cols], src[:, cols], chunked[:, cols], ALU.add
                                              ).then_inc(S["score_added"], 1)
                    for qb, cols in parts:
                        dve.wait_ge(S["score_added"], 2 * c + qb + 1)
                        ins = dve.tensor_reduce(neg_max[m % 2][:, qb:qb + 1], s[:, cols], AX.X, ALU.max, negate=True)
                    ins.then_inc(S["masked"], 1)

                def normalise(m, g, u):
                    c = 16 * a + 4 * g + m + 4 * u
                    s = scores[m % 2]
                    dve.wait_ge(S["exp_ready"], 2 * c + 2)
                    dve.reciprocal(inv_sum[m % 2][:, :], row_sum[m % 2][:, :]).then_inc(S["inv_sum_ready"], 1)
                    dve.wait_ge(S["inv_sum_ready"], c + 1)
                    if fox:
                        for qb, cols in enumerate((slice(0, P), slice(P, 384))):
                            ins = dve.tensor_scalar(s[:, cols], s[:, cols], inv_sum[m % 2][:, qb:qb + 1], None, ALU.mult)
                        ins.then_inc(S["probs_ready"], 1)

                def combine(h, g, u):
                    c = 2 * (g + u) + h
                    normalise(2 * h, g, u)
                    normalise(2 * h + 1, g, u)
                    dve.tensor_scalar(lam_inv_sum[:, :], inv_sum[1][:, :], neg_lam[:, 0:1], None, ALU.mult
                                      ).then_inc(S["lam_scaled"], 1)
                    for qb, cols in enumerate((slice(0, P), slice(P, 384))):
                        dve.tensor_scalar(scores[0][:, cols], scores[0][:, cols], inv_sum[0][:, qb:qb + 1], None,
                                          ALU.mult).then_inc(S["probs_half"], 1)
                    dve.wait_ge(S["lam_scaled"], c + 1)
                    for qb, cols in enumerate((slice(0, P), slice(P, 384))):
                        dve.wait_ge(S["probs_half"], 2 * c + qb + 1)
                        ins = dve.scalar_tensor_tensor(scores[0][:, cols], scores[1][:, cols],
                                                       lam_inv_sum[:, qb:qb + 1], scores[0][:, cols],
                                                       ALU.mult, ALU.add)
                    ins.then_inc(S["probs_ready"], 1)

                def values(j, u):
                    dve.wait_ge(S["block_done"], b + 3 * j + 3 + 3 * u)
                    if j:
                        per = 4 if fox else 2
                        dve.wait_ge(S["pv_done"], turned_before[i] + per * (j + u))
                    for tt in range(2):
                        ins = dve.tensor_scalar(v_nat[:, tt, :], bank[2][:, tt * 256:(tt + 1) * 256],
                                                inv_rms[:, SEQ + tt:SEQ + tt + 1], None, ALU.mult)
                    ins.then_inc(S["v_ready"], 1)

                def o_part(g, u):
                    at = bass.ds(2 * (g + u), 2)
                    if fox:
                        src = pair(bank[7][:, :])
                    else:
                        dve.wait_ge(S["o_inv_ready"], g + u + 1)
                        dve.scalar_tensor_tensor(gate_silu[:, :], hidden[:, :], vec[:, HEAD_COL + 6:HEAD_COL + 7],
                                                 q_square[:, :], ALU.mult, ALU.mult).then_inc(S["o_normed"], 1)
                        src = pair(gate_silu[:, :])
                    dve.wait_ge(S["o_high_ready"], o_before[i] + g + u + 1)
                    dve.tensor_tensor(o_low[:, at, :], src, o_high[:, at, :].bitcast(F32), ALU.subtract
                                      ).then_inc(S["o_bank_free"], 1)

                def group(j, u=0):
                    g = j - 1
                    split_low(b + 3 * j + 2, u, 3)
                    raw_part("q", j, u)
                    if j:
                        mask_and_max(0, g, u)
                        mask_and_max(1, g, u)
                        if fox:
                            normalise(0, g, u)
                            normalise(1, g, u)
                        else:
                            combine(0, g, u)
                    split_low(b + 3 * j + 3, u, 3)
                    if j:
                        mask_and_max(2, g, u)
                    raw_part("k", j, u)
                    if j:
                        mask_and_max(3, g, u)
                    normed("q", j, u)
                    if j:
                        if fox:
                            normalise(2, g, u)
                            normalise(3, g, u)
                        else:
                            combine(1, g, u)
                    if not fox:
                        rotated("q", j, u)
                    split_low(b + 3 * j + 4, u, 3)
                    normed("k", j, u)
                    if not fox:
                        rotated("k", j, u)
                    values(j, u)
                    if j:
                        o_part(g, u)

                if fox:
                    dve.wait_ge(S["gate_w_high_ready"], w + 1)
                    dve.tensor_tensor(gate_w_low[:, :, :], gate_w[:, :, :], gate_w_high[:, :, :].bitcast(F32),
                                      ALU.subtract).then_inc(S["gate_w_low_ready"], 1)
                    dve.wait_ge(S["logits_done"], w + 1)
                    for tt in range(2):
                        dve.scalar_tensor_tensor(logit[:, tt, :], bank[6][:, 16 * tt:16 * tt + 16],
                                                 inv_rms[:, SEQ + tt:SEQ + tt + 1],
                                                 fox_bias[:, w * FOX_HEADS:(w + 1) * FOX_HEADS],
                                                 ALU.mult, ALU.add).then_inc(S["logit_ready"], 1)
                    dve.wait_ge(S["logit_ready"], 2 * w + 2)
                    dve.tensor_scalar(logit_neg[:, :, :], logit[:, :, :], 0.0, None, ALU.min
                                      ).then_inc(S["logit_neg_ready"], 1)
                    dve.wait_ge(S["logit_neg_ready"], w + 1)
                    dve.wait_ge(S["logit_parts"], 3 * w + 3)
                    dve.tensor_tensor(log_f[:, :, :], logit_neg[:, :, :], logit_abs[:, :, :], ALU.subtract
                                      ).then_inc(S["log_f_ready"], 1)
                group(0)
                if fox:
                    dve.wait_ge(S["neg_cumT_ready"], w + 1)
                    dve.tensor_copy(cum_q[:, :], bank[6][:, 64:64 + 2 * FOX_HEADS]).then_inc(S["cum_q_ready"], 1)
                    dve.wait_ge(S["cum_q_ready"], w + 1)
                with dve.Fori(0, GROUPS - 1) as u:
                    group(1, u)
                g, e = GROUPS - 1, b + 3 * GROUPS
                mask_and_max(0, g, 0)
                mask_and_max(1, g, 0)
                if fox:
                    normalise(0, g, 0)
                    normalise(1, g, 0)
                else:
                    combine(0, g, 0)
                split_low(e + 2)
                mask_and_max(2, g, 0)
                mask_and_max(3, g, 0)
                if fox:
                    normalise(2, g, 0)
                    normalise(3, g, 0)
                else:
                    combine(1, g, 0)
                split_low(e + 3)
                split_low(e + 4)
                o_part(g, 0)

            def conv(i):
                b = starts[i]
                for j in range(GROUPS):
                    split_low(b + 2 * j + 2)
                    dve.wait_ge(S["block_done"], b + 2 * j + 1)
                    dve.tensor_tensor(pair(gate_in[:, :]), pair(bank[2 * (j % 2)][:, :]),
                                      over_tokens(inv_rms[:, 0:SEQ]), ALU.mult).then_inc(S["conv_a_ready"], 1)
                    split_low(b + 2 * j + 3)
                    dve.wait_ge(S["block_done"], b + 2 * j + 2)
                    dve.tensor_tensor(pair(gate_scaled[:, :]), pair(bank[2 * (j % 2) + 1][:, :]),
                                      over_tokens(inv_rms[:, 0:SEQ]), ALU.mult).then_inc(S["conv_g_ready"], 1)
                    dve.wait_ge(S["conv_a_ready"], j + 1)
                    dve.wait_ge(S["sigmoid_ready"], 2 * j + 2)
                    for m in range(2):
                        t = 2 * j + m
                        dve.scalar_tensor_tensor(u_pad[:, t, TAPS - 1:], gate_in[:, m * SEQ:(m + 1) * SEQ],
                                                 vec[:, PW1_COL + t:PW1_COL + t + 1],
                                                 gate_silu[:, m * SEQ:(m + 1) * SEQ], ALU.add, ALU.mult
                                                 ).then_inc(S["u_ready"], 1)
                    dve.wait_ge(S["u_ready"], 2 * j + 2)
                    for m in range(2):
                        t = 2 * j + m
                        dve.tensor_scalar(y_conv[:, t, :], u_pad[:, t, 0:SEQ], vec[:, DW_COL + t:DW_COL + t + 1],
                                          vec[:, DW_B_COL + t:DW_B_COL + t + 1], ALU.mult, ALU.add
                                          ).then_inc(S["tap_done"], 1)
                    with dve.Fori(0, (TAPS - 1) // 5) as r:
                        for k in range(1, 6):
                            for m in range(2):
                                t = 2 * j + m
                                dve.wait_ge(S["tap_done"], 2 * TAPS * j + 2 * k - 1 + m + 10 * r)
                                dve.scalar_tensor_tensor(y_conv[:, t, :], u_pad[:, t, bass.ds(r * 5 + k, SEQ)],
                                                         vec[:, bass.ds(r * (5 * KT) + (DW_COL + k * KT + t), 1)],
                                                         y_conv[:, t, :], ALU.mult, ALU.add
                                                         ).then_inc(S["tap_done"], 1)
                dve.wait_ge(S["mean_done"], 1)
                for T in range(4):
                    dve.scalar_tensor_tensor(y_conv[:, 2 * T:2 * T + 2, :], over_tokens(bank[4][:, 0:SEQ]), -1.0 / D,
                                             y_conv[:, 2 * T:2 * T + 2, :], ALU.mult, ALU.add
                                             ).then_inc(S["centred"], 1)
                dve.wait_ge(S["ln_root_ready"], 1)
                dve.reciprocal(ln_inv[:, :], root[:, 0:SEQ]).then_inc(S["ln_inv_ready"], 1)
                dve.wait_ge(S["ln_inv_ready"], 1)
                for T in range(4):
                    dve.tensor_tensor(y_conv[:, 2 * T:2 * T + 2, :], y_conv[:, 2 * T:2 * T + 2, :],
                                      over_tokens(ln_inv[:, :]), ALU.mult).then_inc(S["ln_scaled"], 1)
                for T in range(4):
                    dve.wait_ge(S["o_high_ready"], o_before[i] + T + 1)
                    dve.tensor_tensor(o_low[:, 2 * T:2 * T + 2, :], ln_work[:, 2 * T:2 * T + 2, :],
                                      o_high[:, 2 * T:2 * T + 2, :].bitcast(F32), ALU.subtract
                                      ).then_inc(S["o_bank_free"], 1)
                e = b + 2 * GROUPS
                for k in range(2, 5):
                    split_low(e + k)

            dve.memset(eps[:, :], EPS).then_inc(S["dve_consts"], 1)
            dve.memset(half_pi[:, :], math.pi / 2).then_inc(S["dve_consts"], 1)
            dve.memset(rope_rows[:, :, :], 0.0).then_inc(S["dve_consts"], 1)
            dve.wait_ge(S["dve_consts"], 3)
            half = ROT // 2
            per_head = rope_rows[:, :, :].rearrange("o r (h a c) -> o r h a c", h=2, c=half)
            for c in range(half):
                dve.memset(per_head[:, 0, :, 0:2, c], ROPE_THETA ** (-2.0 * c / ROT)).then_inc(S["dve_consts"], 1)
            dve.memset(per_head[:, 1, :, 0, :], -1.0).then_inc(S["dve_consts"], 1)
            dve.memset(per_head[:, 1, :, 1, :], 1.0).then_inc(S["dve_consts"], 1)
            dve.memset(per_head[:, 2, :, 0:2, :], 1.0).then_inc(S["dve_consts"], 1)
            dve.memset(row_sum[0][:, :], 1.0).then_inc(S["o_bank_free"], 1)
            dve.wait_ge(S["pool_consts"], N_POOL_CONSTS)
            for h in range(2):
                for c in range(2):
                    dve.tensor_copy(swap[:, HEAD * h + half * c:HEAD * h + half * (c + 1)],
                                    ident[:, HEAD * h + half * (1 - c):HEAD * h + half * (2 - c)]
                                    ).then_inc(S["dve_consts"], 1)
            dve.wait_ge(S["const_loaded"], 96)
            dve.tensor_copy(pos_row[:, :], pos_int[:, :]).then_inc(S["dve_consts"], 1)
            dve.tensor_tensor(lam_products[:, :, :], lam_rows[:, 0:4:2, :], lam_rows[:, 1:4:2, :], ALU.mult
                              ).then_inc(S["lam_step"], 1)
            dve.wait_ge(S["lam_step"], 1)
            dve.tensor_reduce(lam_sums[:, :], lam_products[:, :, :], AX.X, ALU.add).then_inc(S["lam_step"], 1)
            dve.wait_ge(S["vec_turned"], 1)
            for n, (col, width) in enumerate(((NORM_COL, 96), (PW1_COL, 48), (DW_COL, 124), (DW_COL + 124, 124),
                                              (HEAD_COL, 7))):
                at = [0, 96, 144, 268, 392][n]
                dve.tensor_copy(vec[:, col:col + width], bank[6][:, at:at + width]).then_inc(S["vec_copied"], 1)
            dve.wait_ge(S["vec_copied"], 5)
            for col, n, s in ((HEAD_COL, 2, fox_scale), (HEAD_COL + 4, 1, fox_scale), (HEAD_COL + 6, 1, 1.0 - lambda_init)):
                dve.tensor_scalar(vec[:, col:col + n], vec[:, col:col + n], s, None, ALU.mult
                                  ).then_inc(S["vec_copied"], 1)
            split_low(0)
            dve.wait_ge(S["lam_step"], 3)
            dve.tensor_tensor(neg_lam_row[:, :], lam_exps[:, 1:2], lam_exps[:, 0:1], ALU.subtract
                              ).then_inc(S["lam_step"], 1)
            dve.wait_ge(S["lam_step"], 4)
            dve.tensor_scalar(neg_lam_row[:, :], neg_lam_row[:, :], -lambda_init, None, ALU.add
                              ).then_inc(S["lam_step"], 1)
            dve.wait_ge(S["small_done"], 1)
            dve.tensor_copy(rope_cols[:, :], bank[5][:, 0:3]).then_inc(S["rope_step"], 1)
            dve.tensor_copy(fox_bias[:, :], bank[5][:, 32:64]).then_inc(S["rope_step"], 1)
            dve.wait_ge(S["rope_step"], 2)
            dve.tensor_scalar(angle[:, :], bank[5][:, 256:512], rope_cols[:, 0:1], None, ALU.mult
                              ).then_inc(S["rope_step"], 1)
            dve.wait_ge(S["rope_step"], 3)
            dve.tensor_scalar(turns[:, :], angle[:, :], 1.0 / (2.0 * math.pi), ROUND, ALU.mult, ALU.add
                              ).then_inc(S["rope_step"], 1)
            dve.wait_ge(S["rope_step"], 4)
            dve.tensor_scalar(turns[:, :], turns[:, :], ROUND, None, ALU.subtract).then_inc(S["rope_step"], 1)
            for n, part in enumerate((TWO_PI_1, TWO_PI_2, TWO_PI_3)):
                dve.wait_ge(S["rope_step"], 5 + n)
                dve.scalar_tensor_tensor(angle[:, :], turns[:, :], -part, angle[:, :], ALU.mult, ALU.add
                                         ).then_inc(S["rope_step"], 1)
            dve.wait_ge(S["rope_step"], 8)
            dve.tensor_scalar(angle[:, :], angle[:, :], math.pi, -math.pi, ALU.min, ALU.max
                              ).then_inc(S["rope_step"], 1)
            dve.wait_ge(S["act_rope_step"], 3)
            dve.tensor_scalar(sinT[:, :], sinT[:, :], rope_cols[:, 1:2], None, ALU.mult).then_inc(S["rope_step"], 1)
            dve.tensor_scalar(not_rotated[:, :], rope_cols[:, 2:3], -1.0, 1.0, ALU.mult, ALU.add
                              ).then_inc(S["rope_step"], 1)
            dve.wait_ge(S["rope_step"], 11)
            dve.tensor_scalar(cosT[:, :], cosT[:, :], rope_cols[:, 2:3], not_rotated[:, 0:1], ALU.mult, ALU.add
                              ).then_inc(S["rope_step"], 1)
            dve.wait_ge(S["small_done"], 2)
            dve.tensor_copy(neg_lam[:, :], bank[4][:, 0:1]).then_inc(S["rope_step"], 1)
            dve.wait_ge(S["rope_step"], 13)
            dve.wait_ge(S["vec_copied"], 8)

            for i, kind in enumerate(phases):
                boundary(i)
                {"ffn": ffn, "fox": attention, "diff": attention, "conv": conv}[kind](i)
            last = len(phases)
            for T in range(4):
                update_x(last, T)
            dve.wait_ge(S["wide_zeroed"], 1)
            for tt in range(2):
                for m in range(2):
                    n = 2 * tt + m
                    dve.wait_ge(S["final_turned"], n + 1)
                    dve.tensor_copy(by_token[tt][:, m * 512:(m + 1) * 512], bank[4 + n][:, :]
                                    ).then_inc(S["final_copied"], 1)

        @block.tensor
        def _(pe):
            def three_passes(dst, s_high, s_low, m_high, m_low, first, last, loose=False):
                pe.matmul(dst, s_high, m_high, start=first, stop=False, skip_group_check=loose)
                pe.matmul(dst, s_high, m_low, start=False, stop=False, skip_group_check=loose)
                return pe.matmul(dst, s_low, m_high, start=False, stop=last, skip_group_check=loose)

            def wait_block(b, u=0, per=0):
                pe.wait_ge(S["low_ready"], b + 1 + u * per)

            def columns_half(dst, b, n, fresh=None):
                high, low = (t[b % RING][:, :].rearrange("p (k n) -> p k n", k=KT) for t in (w_high, w_low))
                for k in range(KT):
                    if fresh is not None:
                        pe.wait_ge(S["xlow_ready"], 8 * fresh + k + 1)
                    cols = slice(n * P, (n + 1) * P)
                    ins = three_passes(dst[:, n * SEQ:(n + 1) * SEQ], high[:, k, cols], low[:, k, cols],
                                       x_high[:, k, :], x_low[:, k, :], k == 0, k == KT - 1)
                return ins

            def tokens_half(dst, b, tt):
                high, low = (t[b % RING][:, :].rearrange("p (k n) -> p k n", k=KT) for t in (w_high, w_low))
                toks = slice(tt * P, (tt + 1) * P)
                for k in range(KT):
                    ins = three_passes(dst[:, tt * 256:(tt + 1) * 256], x_high[:, k, toks], x_low[:, k, toks],
                                       high[:, k, :], low[:, k, :], k == 0, k == KT - 1)
                return ins

            def rows_block(b, m_high, m_low, first, last, u=0, per=0):
                wait_block(b, u, per)
                high, low = (t[b % RING][:, :].rearrange("p (f n) -> p f n", f=2) for t in (w_high, w_low))
                for d in range(KT):
                    for f in range(2):
                        cols = slice(d * P, (d + 1) * P)
                        ins = three_passes(bank[d // 2][:, (d % 2) * SEQ:(d % 2 + 1) * SEQ],
                                           high[:, f, cols], low[:, f, cols], m_high[:, f, :], m_low[:, f, :],
                                           first and d % 2 == 0 and f == 0, last and f == 1, True)
                    if last and d % 2 and d < KT - 1:
                        ins.then_inc(S["out_bank_done"], 1)
                ins.then_inc(S["block_done"], 1)

            def first_block(i, dst):
                b = starts[i]
                wait_block(b)
                columns_half(dst, b, 0, fresh=i)
                pe.wait_ge(S["xsq_ready"], 4 * i + 4)
                for k in range(KT):
                    ins = pe.matmul(bank[7][:, 0:SEQ], ones[:, :], x_square[:, k, :], start=k == 0, stop=k == KT - 1)
                if phases[i] in ("fox", "diff"):
                    for tt in range(2):
                        for k in range(KT):
                            ins = pe.matmul(bank[7][:, SEQ + tt:SEQ + tt + 1], x_square[:, k, tt * P:(tt + 1) * P],
                                            ones[:, 0:1], start=k == 0, stop=k == KT - 1)
                ins.then_inc(S["sumsq_done"], 1)
                columns_half(dst, b, 1).then_inc(S["block_done"], 1)

            def ffn(i):
                b, f = starts[i], number(i)

                def gate_up(which, p, u=0):
                    blk = b + 3 * p - 1 + which
                    wait_block(blk, u, 6)
                    pe.wait_ge(S["hidden_ready" if which else "gate_in_ready"], PAIRS * f + p + 2 * u)
                    columns_half(bank[4 + which], blk, 0)
                    columns_half(bank[4 + which], blk, 1).then_inc(S["block_done"], 1)

                def down(blk, p, u, first, last):
                    pe.wait_ge(S["h_low_ready"], PAIRS * f + p + 1 + 2 * u)
                    rows_block(blk, pair(h_high[p % 2][:, :]), pair(h_low[p % 2][:, :]), first, last, u, 6)

                def one_pair(p, u=0, first=False):
                    gate_up(0, p, u)
                    gate_up(1, p, u)
                    down(b + 3 * p + 1, p - 1, u, first, False)

                first_block(i, bank[4])
                wait_block(b + 1)
                columns_half(bank[5], b + 1, 0)
                columns_half(bank[5], b + 1, 1).then_inc(S["block_done"], 1)
                one_pair(1, first=True)
                one_pair(2)
                with pe.Fori(1, (PAIRS - 1) // 2) as u:
                    one_pair(1, u)
                    one_pair(2, u)
                down(b + 3 * PAIRS - 1, PAIRS - 1, 0, False, True)

            def attention(i):
                a, b, fox = number(i), starts[i], phases[i] == "fox"
                w = i // 9
                per = 4 if fox else 2

                def head_scores(m, g, u):
                    c = 16 * a + 4 * g + m + 4 * u
                    dst = bank[4 + m % 2]
                    if m == 0:
                        pe.wait_ge(S["q_ready"], 4 * a + g + u + 1)
                        pe.wait_ge(S["k_ready"], 4 * a + g + u + 1)
                        if fox:
                            pe.wait_ge(S["neg_cum_ready"], w + 1)
                    if fox and m == 3:
                        pe.wait_ge(S["probsT_ready"], turned_before[i] + 4 * g + 2 + 4 * u)
                    if m >= 2:
                        pe.wait_ge(S["masked"], c - 1)
                    tile, r = m // 2, slice(HEAD * (m % 2), HEAD * (m % 2) + HEAD)
                    for qb, cols, keys in ((0, slice(0, P), P), (1, slice(P, 384), SEQ)):
                        q = qT[r, tile * SEQ + qb * P:tile * SEQ + (qb + 1) * P]
                        ins = pe.matmul(dst[:, cols], q, kT[r, tile * SEQ:tile * SEQ + keys], start=True, stop=not fox)
                        if fox:
                            at = u * (4 * SEQ) + (4 * g + m) * SEQ
                            ins = pe.matmul(dst[:, cols], ones[:, :], wide[:, bass.ds(at, keys)], start=False, stop=True)
                    ins.then_inc(S["scores_done"], 1)

                def turn(m, g, u):
                    c = turned_before[i] + per * (g + u) + m
                    pe.wait_ge(S["probs_ready"], c + 1)
                    if m == 1 and not fox:
                        pe.wait_ge(S["probsT_ready"], c)
                    dst = bank[([6, 5, 6, 4] if fox else [6, 6])[m]]
                    for n in range(3):
                        ins = pe.transpose(dst[:, n * P:(n + 1) * P], scores[m % 2 if fox else 0][:, n * P:(n + 1) * P],
                                           ident[:, :])
                    ins.then_inc(S["probs_turned"], 1)

                def values(m, g, u):
                    c = turned_before[i] + per * (g + u) + m
                    pe.wait_ge(S["probsT_ready"], c + 1)
                    if m == 0:
                        pe.wait_ge(S["v_ready"], 4 * a + g + u + 1)
                        pe.wait_ge(S["o_bank_free"], o_before[i] + g + u + 1)
                    p = probsT[m % 2]
                    if fox:
                        r, at = slice(HEAD * (m % 2), HEAD * (m % 2) + HEAD), (m // 2) * SEQ
                        cols = slice(HEAD * m, HEAD * m + HEAD)
                    else:
                        r, at, cols = slice(0, P), m * SEQ, slice(P * m, P * m + P)
                    pe.matmul(bank[7][r, at:at + SEQ], v_nat[:, 0, cols], p[:, 0:SEQ], start=True, stop=False)
                    pe.matmul(bank[7][r, at + P:at + SEQ], v_nat[:, 1, cols], p[:, SEQ:384], start=False, stop=True
                              ).then_inc(S["pv_done"], 1)

                def head_sums(x, j, u):
                    c = 4 * a + j + u + 1
                    pe.wait_ge(S[x + "_sq_ready"], c)
                    if x == "k":
                        pe.wait_ge(S["q_log_ready"], c)
                        if not fox:
                            pe.wait_ge(S["q_sin"], j + u + 1)
                    pe.matmul(bank[3][:, :], ones_heads[:, :], {"q": q_square, "k": k_square}[x][:, :],
                              start=True, stop=True).then_inc(S[x + "_sum_done"], 1)

                def swapped(x, j, u):
                    pe.wait_ge(S[x + "_normed"], j + u + 1)
                    pe.matmul(bank[3][:, :], swap[:, :], {"q": q_raw, "k": k_raw}[x][:, :],
                              start=True, stop=True).then_inc(S[x + "_swapped"], 1)

                def o_sums(g, u):
                    pe.wait_ge(S["o_sq_ready"], g + u + 1)
                    pe.matmul(bank[6][:, :], ones[:, :], gate_in[:, :], start=True, stop=True
                              ).then_inc(S["o_sum_done"], 1)

                def group(j, u=0):
                    g = j - 1
                    q_blk, k_blk, v_blk = (b + 3 * j + n for n in range(3))
                    if j:
                        wait_block(q_blk, u, 3)
                        columns_half(bank[0], q_blk, 0)
                        columns_half(bank[0], q_blk, 1).then_inc(S["block_done"], 1)
                        head_scores(0, g, u)
                        head_scores(1, g, u)
                    else:
                        first_block(i, bank[0])
                        if fox:
                            forget_gates()
                    wait_block(k_blk, u, 3)
                    columns_half(bank[1], k_blk, 0)
                    columns_half(bank[1], k_blk, 1).then_inc(S["block_done"], 1)
                    if j:
                        turn(0, g, u)
                        if fox:
                            turn(1, g, u)
                        head_scores(2, g, u)
                    head_sums("q", j, u)
                    if j:
                        head_scores(3, g, u)
                    wait_block(v_blk, u, 3)
                    if j:
                        pe.wait_ge(S["v_ready"], 4 * a + j + u)
                    tokens_half(bank[2], v_blk, 0)
                    if not fox:
                        swapped("q", j, u)
                    if j:
                        values(0, g, u)
                        if fox:
                            values(1, g, u)
                    head_sums("k", j, u)
                    tokens_half(bank[2], v_blk, 1).then_inc(S["block_done"], 1)
                    if j:
                        if fox:
                            turn(2, g, u)
                            turn(3, g, u)
                        else:
                            turn(1, g, u)
                    if not fox:
                        swapped("k", j, u)
                    if j:
                        if fox:
                            values(2, g, u)
                            values(3, g, u)
                        else:
                            values(1, g, u)
                            o_sums(g, u)

                def forget_gates():
                    pe.wait_ge(S["gate_w_low_ready"], w + 1)
                    for tt in range(2):
                        toks = slice(tt * P, (tt + 1) * P)
                        for k in range(KT):
                            ins = three_passes(bank[6][:, 16 * tt:16 * tt + 16], x_high[:, k, toks], x_low[:, k, toks],
                                               gate_w_high[:, k, :], gate_w_low[:, k, :], k == 0, k == KT - 1)
                    ins.then_inc(S["logits_done"], 1)

                def cumulate():
                    pe.wait_ge(S["log_f_ready"], w + 1)
                    H = FOX_HEADS
                    f0, f1 = log_f[:, 0, :], log_f[:, 1, :]
                    pe.matmul(bank[6][:, 64:64 + H], upper[:, :], f0, start=True, stop=True)
                    pe.matmul(bank[6][:, 64 + H:64 + 2 * H], ones[:, :], f0, start=True, stop=False)
                    pe.matmul(bank[6][:, 64 + H:64 + 2 * H], upper[:, :], f1, start=False, stop=True)
                    pe.matmul(bank[6][0:H, P:2 * P], f0, upper[:, :], start=True, stop=True)
                    pe.matmul(bank[6][0:H, 2 * P:3 * P], f0, ones[:, :], start=True, stop=False)
                    pe.matmul(bank[6][0:H, 2 * P:3 * P], f1, upper[:, :], start=False, stop=True
                              ).then_inc(S["cum_done"], 1)

                def o_block(n):
                    pe.wait_ge(S["o_bank_free"], o_before[i] + n + 2)
                    rows_block(b + 3 * GROUPS + n, o_high[:, 2 * n:2 * n + 2, :], o_low[:, 2 * n:2 * n + 2, :],
                               n == 0, n == GROUPS - 1)

                group(0)
                if fox:
                    cumulate()
                with pe.Fori(0, GROUPS - 1) as u:
                    group(1, u)
                g = GROUPS - 1
                head_scores(0, g, 0)
                head_scores(1, g, 0)
                pe.wait_ge(S["v_ready"], 4 * a + GROUPS)
                o_block(0)
                turn(0, g, 0)
                if fox:
                    turn(1, g, 0)
                head_scores(2, g, 0)
                head_scores(3, g, 0)
                o_block(1)
                values(0, g, 0)
                if fox:
                    values(1, g, 0)
                    turn(2, g, 0)
                    turn(3, g, 0)
                else:
                    turn(1, g, 0)
                o_block(2)
                if fox:
                    values(2, g, 0)
                    values(3, g, 0)
                else:
                    values(1, g, 0)
                    o_sums(g, 0)
                o_block(GROUPS - 1)

            def conv(i):
                b = starts[i]
                for j in range(2 * GROUPS):
                    if j == 0:
                        first_block(i, bank[0])
                        continue
                    wait_block(b + j)
                    if j >= 4:
                        pe.wait_ge(S["conv_g_ready" if j % 2 else "conv_a_ready"], j // 2 - 1)
                    columns_half(bank[j % 4], b + j, 0)
                    columns_half(bank[j % 4], b + j, 1).then_inc(S["block_done"], 1)
                pe.wait_ge(S["tap_done"], 2 * TAPS * GROUPS)
                for k in range(KT):
                    ins = pe.matmul(bank[4][:, 0:SEQ], ones[:, :], y_conv[:, k, :], start=k == 0, stop=k == KT - 1)
                ins.then_inc(S["mean_done"], 1)
                for k in range(KT):
                    pe.wait_ge(S["centred_sq"], k // 2 + 1)
                    ins = pe.matmul(bank[5][:, 0:SEQ], ones[:, :], ln_work[:, k, :], start=k == 0, stop=k == KT - 1)
                ins.then_inc(S["var_done"], 1)
                for n in range(GROUPS):
                    pe.wait_ge(S["o_bank_free"], o_before[i] + n + 2)
                    rows_block(b + 2 * GROUPS + n, o_high[:, 2 * n:2 * n + 2, :], o_low[:, 2 * n:2 * n + 2, :],
                               n == 0, n == GROUPS - 1)

            pe.wait_ge(S["pool_consts"], N_POOL_CONSTS)
            pe.wait_ge(S["dve_consts"], DVE_CONSTS)
            pe.wait_ge(S["vec_loaded"], 16 * 19)
            at = 0
            for n, rows in enumerate((96, 48, 124, 124)):
                pe.transpose(bank[6][:, at:at + rows], vec_rows[0:rows, n, :], ident[0:rows, 0:rows])
                at += rows
            pe.transpose(bank[6][:, at:at + 7], head_rows[:, :], ident[0:7, 0:7]).then_inc(S["vec_turned"], 1)
            pe.wait_ge(S["const_loaded"], 96)
            for r in range(3):
                pe.matmul(bank[5][:, r:r + 1], rope_rows[:, r, :], ones[0:1, 0:1], start=True, stop=True)
            pe.matmul(bank[5][:, 32:64], ones[0:1, :], fox_bias_row[:, :], start=True, stop=True)
            pe.matmul(bank[5][:, 256:512], ones[0:1, :], pos_row[:, :], start=True, stop=True
                      ).then_inc(S["small_done"], 1)
            pe.wait_ge(S["x_loaded"], 32)
            for T in range(4):
                for m in range(2):
                    for tt in range(2):
                        t = 2 * T + m
                        ins = pe.transpose(bank[T][:, m * SEQ + tt * P:m * SEQ + (tt + 1) * P],
                                           by_token[tt][:, t * P:(t + 1) * P], ident[:, :])
                ins.then_inc(S["x_turned"], 1)
            pe.wait_ge(S["lam_step"], 5)
            pe.matmul(bank[4][:, 0:1], ones[0:1, :], neg_lam_row[:, :], start=True, stop=True
                      ).then_inc(S["small_done"], 1)
            for i, kind in enumerate(phases):
                {"ffn": ffn, "fox": attention, "diff": attention, "conv": conv}[kind](i)
            pe.wait_ge(S["x_ready"], 4 * len(phases) + 4)
            for tt in range(2):
                for m in range(2):
                    for t in range(4):
                        ins = pe.transpose(bank[4 + 2 * tt + m][:, t * P:(t + 1) * P],
                                           xT[:, 4 * m + t, tt * P:(tt + 1) * P], ident[:, :])
                    ins.then_inc(S["final_turned"], 1)


INPUTS = [
    "x", "positions", "norm_ffn1", "norm_mix", "norm_ffn2", "ffn1_w_gate", "ffn1_w_up", "ffn1_w_down",
    "ffn2_w_gate", "ffn2_w_up", "ffn2_w_down", "fox_w_in", "fox_b_f", "fox_q_gain", "fox_k_gain", "fox_w_out",
    "conv_w_pw1", "conv_b_pw1", "conv_w_dw", "conv_b_dw", "conv_ln_g", "conv_ln_b", "conv_w_pw2", "conv_b_pw2",
    "diff_w_in", "diff_q_gain", "diff_k_gain", "diff_lambda_q1", "diff_lambda_k1", "diff_lambda_q2",
    "diff_lambda_k2", "diff_sub_gain", "diff_w_out",
]


def kernel(**inputs):
    import numpy as np
    import concourse.bacc as bacc
    from concourse.bass_utils import run_bass_kernel_spmd

    nc = bacc.Bacc("TRN2", target_bir_lowering=False, num_devices=1)
    arrays, aps = {}, {}
    for name in INPUTS:
        a = np.ascontiguousarray(inputs[name])
        arrays[f"in_{name}"] = a
        aps[name] = nc.dram_tensor(f"in_{name}", a.shape, mybir.dt.from_np(a.dtype), kind="ExternalInput").ap()
    out = nc.dram_tensor("trunk_out", (1, SEQ, D), F32, kind="ExternalOutput").ap()
    build_trunk(nc, aps, out)
    r = run_bass_kernel_spmd(nc, [arrays], core_ids=[0])
    return r.results[0]["trunk_out"]
```

```python
import math
from contextlib import ExitStack

import concourse.bass as bass
from concourse import mybir

F32 = mybir.dt.float32
F32R = mybir.dt.float32r
I32 = mybir.dt.int32
BF16 = mybir.dt.bfloat16
ALU = mybir.AluOpType
ACT = mybir.ActivationFunctionType
AX = mybir.AxisListType

P = 128
DEPTH = 4
SEQ = 256
D = 1024
KT = D // P
D_FF = ((8 * D // 3 + 127) // 128) * 128
PAIRS = D_FF // 256
HEAD = 64
FOX_HEADS = D // HEAD
GROUPS = D // 256
TAPS = 31
ROT = HEAD // 4
ROPE_THETA = 500000.0
EPS = 1e-6
PE_TILES = (5, 6, 7)
TAP_HALVES = ((0, 16), (16, TAPS - 16))
RING = 3
MASKED = -1e30
ROUND = 1.5 * 2.0 ** 23
TWO_PI_1, TWO_PI_2 = 6.28125, 1.9350051879882812e-3
TWO_PI_3 = 2.0 * math.pi - TWO_PI_1 - TWO_PI_2

MIXERS = ["fox", "conv", "diff"]
PHASES = [k for i in range(DEPTH) for k in ("ffn", MIXERS[i % 3], "ffn")]
BLOCKS = {"ffn": 3 * PAIRS, "fox": 4 * GROUPS, "conv": 3 * GROUPS, "diff": 4 * GROUPS}

NORM_COL = 0
PW1_COL = NORM_COL + 3 * DEPTH * KT
DW_B_COL = PW1_COL + 16
LN_G_COL = DW_B_COL + KT
LN_B_COL = LN_G_COL + KT
PW2_COL = LN_B_COL + KT
HEAD_COL = PW2_COL + KT
DW_COL = HEAD_COL + 7
VEC_COLS = DW_COL + TAPS * KT


def build_trunk(nc, A, out):
    phases = PHASES
    starts = [sum(BLOCKS[k] for k in phases[:i]) for i in range(len(phases) + 1)]
    n_blocks = starts[-1]

    def number(i):
        family = {"ffn": ("ffn",), "fox": ("fox", "diff"), "diff": ("fox", "diff"), "conv": ("conv",)}[phases[i]]
        return sum(k in family for k in phases[:i])

    def layer_of(i):
        return i // 3

    with ExitStack() as ctx:
        def sb(name, shape, dt=F32):
            return ctx.enter_context(nc.sbuf_tensor("sb_" + name, shape, dt))

        def sem(name):
            return ctx.enter_context(nc.semaphore(name))

        raw = [sb(f"raw{i}", [P, 2048]) for i in range(RING)]
        w_high = [sb(f"w_high{i}", [P, 2048], F32R) for i in range(RING)]
        w_low = [sb(f"w_low{i}", [P, 2048], F32R) for i in range(RING)]

        xT = sb("xT", [P, KT, SEQ])
        x_square = sb("x_square", [P, KT, SEQ])
        x_high = sb("x_high", [P, KT, SEQ], F32R)
        x_low = sb("x_low", [P, KT, SEQ], F32R)
        square_sum = sb("square_sum", [P, 2, SEQ])
        root = sb("root", [P, SEQ + 2])
        inv_rms = sb("inv_rms", [P, SEQ + 2])

        gate_in = sb("gate_in", [P, 512])
        gate_silu = sb("gate_silu", [P, 512])
        gate_scaled = sb("gate_scaled", [P, 512])
        hidden = sb("hidden", [P, 512])
        h_high = [sb(f"h_high{i}", [P, 512], F32R) for i in range(2)]
        h_low = [sb(f"h_low{i}", [P, 512], F32R) for i in range(2)]

        q_raw, k_raw = sb("q_raw", [P, 512]), gate_scaled
        q_square, k_square = sb("q_square", [P, 512]), sb("k_square", [P, 512])
        q_inv, k_inv = sb("q_inv", [P, 512]), sb("k_inv", [P, 512])
        qT, kT = sb("qT", [P, 512]), sb("kT", [P, 512])
        v_nat = sb("v_nat", [P, 2, 256])
        scores = [sb(f"scores{i}", [P, 384]) for i in range(2)]
        probsT = [sb(f"probsT{i}", [P, 384]) for i in range(2)]
        neg_max = [sb(f"neg_max{i}", [P, 2]) for i in range(2)]
        row_sum = [sb(f"row_sum{i}", [P, 2]) for i in range(2)]
        inv_sum = [sb(f"inv_sum{i}", [P, 2]) for i in range(2)]
        lam_inv_sum = sb("lam_inv_sum", [P, 2])
        o_high = sb("o_high", [P, KT, SEQ], F32R)
        o_low = sb("o_low", [P, KT, SEQ], F32R)
        gate_w = sb("gate_w", [P, KT, FOX_HEADS])
        gate_w_gained = sb("gate_w_gained", [P, KT, FOX_HEADS])
        logit = sb("logit", [FOX_HEADS, SEQ])
        logit_min = sb("logit_min", [FOX_HEADS, SEQ])
        logit_log = sb("logit_log", [FOX_HEADS, SEQ])
        neg_cumT = sb("neg_cumT", [FOX_HEADS, SEQ])
        neg_cum_q = sb("neg_cum_q", [P, 2 * FOX_HEADS])
        cum_part = sb("cum_part", [FOX_HEADS, SEQ], BF16)
        cum_parts = sb("cum_parts", [P, SEQ], BF16)
        head_of_row = sb("head_of_row", [P, FOX_HEADS], BF16)
        ones_bf = sb("ones_bf", [P, P], BF16)
        wide = sb("wide", [P, 4096])
        neg_cum_wide = wide[:, 0:FOX_HEADS * SEQ // 2].bitcast(BF16)
        neg_cum_heads = neg_cum_wide.rearrange("p (h n) -> p h n", h=FOX_HEADS)
        by_token = [wide[:, tt * D:(tt + 1) * D] for tt in range(2)]
        u_pad = sb("u_pad", [P, KT, TAPS - 1 + SEQ])
        y_conv = x_square
        ln_work = u_pad[:, :, TAPS - 1:]
        ln_inv = q_raw[:, 0:SEQ]

        ident = sb("ident", [P, P])
        ones = sb("ones", [P, P])
        ones_heads = sb("ones_heads", [P, P])
        upper = sb("upper", [P, P])
        causal = sb("causal", [P, 384])
        chunked = sb("chunked", [P, 384])
        swap = sb("swap", [P, P])
        vec = sb("vec", [P, VEC_COLS])
        vec_rows = hidden[:, :].rearrange("p (a n) -> p a n", a=4)
        head_rows = q_raw[0:7, 0:P]
        eps = sb("eps", [P, 1])
        half_pi = sb("half_pi", [P, 1])
        rope_rows = sb("rope_rows", [1, 3, P])
        rope_cols = sb("rope_cols", [P, 3])
        not_rotated = sb("not_rotated", [P, 1])
        pos_int = sb("pos_int", [1, SEQ], I32)
        pos_row = q_square[0:1, 0:SEQ]
        angle, turns = q_inv[:, 0:SEQ], k_inv[:, 0:SEQ]
        cosT, sinT = sb("cosT", [P, SEQ]), sb("sinT", [P, SEQ])
        fox_bias_rows = sb("fox_bias_rows", [2, FOX_HEADS])
        fox_bias = sb("fox_bias", [FOX_HEADS, 2])
        lam_rows = sb("lam_rows", [1, 4, HEAD])
        lam_products = sb("lam_products", [1, 2, HEAD])
        lam_sums = sb("lam_sums", [1, 2])
        lam_exps = sb("lam_exps", [1, 2])
        neg_lam_row = sb("neg_lam_row", [1, 1])
        neg_lam = sb("neg_lam", [P, 1])

        bank = [ctx.enter_context(nc.psum_tensor(f"bank{i}", [P, 512], F32)) for i in range(8)]

        names = (
            "x_loaded vec_loaded const_loaded pool_consts dve_consts out_stored "
            "block_done out_bank_done sumsq_done high_ready low_ready "
            "x_ready xhigh_ready xsq_ready xlow_ready root_ready inv_rms_ready "
            "gate_in_ready silu_ready gate_scaled_ready hidden_ready h_high_ready h_low_ready "
            "x_turned vec_turned vec_copied small_done rope_step act_rope_step lam_step "
            "q_raw_ready k_raw_ready q_sq_ready k_sq_ready q_log_ready k_log_ready q_inv_ready k_inv_ready "
            "q_sum_done k_sum_done q_normed k_normed q_swapped k_swapped q_cos q_sin k_cos k_sin "
            "q_ready k_ready v_ready v_half_ready scores_done score_added masked exp_ready exp_half "
            "inv_sum_ready probs_ready probs_half probs_turned probsT_ready pv_done o_high_ready o_bank_free "
            "o_copied o_sq_ready o_sum_done o_log_ready o_inv_ready o_normed lam_scaled "
            "gate_w_loaded gate_w_ready logits_done logit_ready logit_parts logit_min_ready "
            "cum_turned cum_q_ready neg_cumT_ready neg_cum_ready "
            "conv_a_ready conv_g_ready sigmoid_ready u_ready tap_done mean_done centred centred_sq var_done "
            "ln_root_ready ln_inv_ready ln_scaled ln_silu "
            "final_turned final_copied square_folded diagonals_ready diagonals_used tile_convolved cum_split_step cum_parts_ready"
        ).split()
        S = {n: sem(n) for n in names}
        raw_landed = [sem(f"raw_landed{i}") for i in range(RING)]

        def raw_uses(b, u=0, per=0):
            return 16 * (b // RING + 1) + u * (16 * per // RING)

        def pair(t):
            return t.rearrange("p (a n) -> p a n", a=2)

        def over_tokens(row, n=2):
            return row.unsqueeze(1).broadcast_to([P, n, SEQ])

        fox_scale = HEAD ** -0.5
        lambda_init = 0.8 - 0.6 * math.exp(-0.3 * 2)

        N_POOL_CONSTS = 15
        DVE_CONSTS = 25
        DVE_TAPS = TAPS * (KT - len(PE_TILES))
        turned_before = [sum({"fox": FOX_HEADS, "diff": FOX_HEADS // 2}.get(k, 0) for k in phases[:i])
                         for i in range(len(phases))]
        o_before = [GROUPS * sum(k != "ffn" for k in phases[:i]) for i in range(len(phases))]

        block = ctx.enter_context(nc.Block())

        @block.sync
        def _(sp):
            def load(b, src, u=0, per=0):
                if b >= RING or not isinstance(u, int):
                    sp.wait_ge(S["low_ready"], b - RING + 1 + u * per)
                dst = raw[b % RING][:, :].rearrange("p (k n) -> p k n", k=src.shape[1])
                sp.dma_start(dst, src).then_inc(raw_landed[b % RING], 16)

            def columns(w, at):
                return w[:, bass.ds(at, 256)].rearrange("(k p) n -> p k n", p=P)

            def rows(w, at):
                return w[bass.ds(at, 256), :].rearrange("(f p) n -> p f n", p=P)

            for tt in range(2):
                sp.dma_start(by_token[tt], A["x"][0, tt * P:(tt + 1) * P, :]).then_inc(S["x_loaded"], 16)

            for i, kind in enumerate(phases):
                b, n, layer = starts[i], number(i), layer_of(i)
                if kind == "ffn":
                    which = "ffn1" if i % 3 == 0 else "ffn2"
                    wg, wu, wd = (A[f"{which}_w_{m}"][layer] for m in ("gate", "up", "down"))
                    def two_pairs(u):
                        for q in range(2):
                            at = u * 512 + (q + 1) * 256
                            load(b + 2 + 3 * q, columns(wg, at), u, 6)
                            load(b + 3 + 3 * q, columns(wu, at), u, 6)
                            load(b + 4 + 3 * q, rows(wd, at - 256), u, 6)

                    load(b, columns(wg, 0))
                    load(b + 1, columns(wu, 0))
                    two_pairs(0)
                    with sp.Fori(1, (PAIRS - 1) // 2) as u:
                        two_pairs(u)
                    load(b + 3 * PAIRS - 1, rows(wd, (PAIRS - 1) * 256))
                elif kind == "conv":
                    for j in range(GROUPS):
                        load(b + 2 * j, columns(A["conv_w_pw1"][0], 256 * j))
                        load(b + 2 * j + 1, columns(A["conv_w_pw1"][0], D + 256 * j))
                    for j in range(GROUPS):
                        load(b + 2 * GROUPS + j, rows(A["conv_w_pw2"][0], 256 * j))
                else:
                    which = layer // 3
                    w_in, w_out = A[kind + "_w_in"][which], A[kind + "_w_out"][which]
                    if kind == "fox":
                        if n:
                            sp.wait_ge(S["gate_w_ready"], which)
                        sp.dma_start(gate_w[:, :, :],
                                     w_in[:, 3 * D:3 * D + FOX_HEADS].rearrange("(k p) n -> p k n", p=P)
                                     ).then_inc(S["gate_w_loaded"], 16)
                    for part in range(3):
                        load(b + part, columns(w_in, part * D))
                    with sp.Fori(0, GROUPS - 1) as u:
                        for part in range(3):
                            load(b + 3 + part, columns(w_in, u * 256 + part * D + 256), u, 3)
                    for j in range(GROUPS):
                        load(b + 3 * GROUPS + j, rows(w_out, 256 * j))
            for tt in range(2):
                sp.wait_ge(S["final_copied"], 2 * (tt + 1))
                sp.dma_start(out[0, tt * P:(tt + 1) * P, :], by_token[tt]).then_inc(S["out_stored"], 16)
            sp.wait_ge(S["out_stored"], 32)

        @block.gpsimd
        def _(pool):
            zero = [ident, ones_heads, swap, causal, chunked]
            for t in zero:
                pool.memset(t[:, :], 0.0).then_inc(S["pool_consts"], 1)
            pool.memset(ones[:, :], 1.0).then_inc(S["pool_consts"], 1)
            pool.memset(u_pad[:, :, 0:TAPS - 1], 0.0).then_inc(S["pool_consts"], 1)
            pool.wait_ge(S["pool_consts"], 7)
            pool.affine_select(out=ident[:, :], in_=ident[:, :], compare_op=ALU.not_equal, fill=1.0, base=0,
                               pattern=[[-1, P]], channel_multiplier=1).then_inc(S["pool_consts"], 1)
            pool.affine_select(out=upper[:, :], in_=ones[:, :], compare_op=ALU.is_ge, fill=0.0, base=0,
                               pattern=[[1, P]], channel_multiplier=-1).then_inc(S["pool_consts"], 1)
            done = 9
            for at in (0, 256):
                pool.affine_select(out=causal[:, at:at + P], in_=causal[:, at:at + P], compare_op=ALU.is_ge,
                                   fill=MASKED, base=0, pattern=[[-1, P]],
                                   channel_multiplier=1).then_inc(S["pool_consts"], 1)
                pool.wait_ge(S["pool_consts"], done + 1)
                pool.memset(chunked[0:HEAD, at + HEAD:at + P], MASKED).then_inc(S["pool_consts"], 1)
                pool.wait_ge(S["pool_consts"], done + 2)
                done += 2
            for m in range(2):
                r = slice(HEAD * m, HEAD * m + HEAD)
                pool.memset(ones_heads[r, r], 1.0).then_inc(S["pool_consts"], 1)
                pool.wait_ge(S["pool_consts"], done + 1 + m)
            def fold_squares(i):
                c, low, high = 6 * i, square_sum[:, 0, :], square_sum[:, 1, :]

                def add(dst, a, b):
                    pool.tensor_tensor(dst, a, b, ALU.add).then_inc(S["square_folded"], 1)

                pool.wait_ge(S["xsq_ready"], 4 * i + 1)
                if i:
                    pool.wait_ge(S["sumsq_done"], i)
                add(low, x_square[:, 0, :], x_square[:, 1, :])
                for T in (1, 2):
                    pool.wait_ge(S["xsq_ready"], 4 * i + T + 1)
                    add(high, x_square[:, 2 * T, :], x_square[:, 2 * T + 1, :])
                    pool.wait_ge(S["square_folded"], c + 2 * T)
                    add(low, low, high)
                    pool.wait_ge(S["square_folded"], c + 2 * T + 1)
                pool.wait_ge(S["xsq_ready"], 4 * i + 4)
                add(high, x_square[:, 6, :], x_square[:, 7, :])

            def spread_cums(w):
                pool.wait_ge(S["cum_parts_ready"], w + 1)
                shape = [P, FOX_HEADS, SEQ]
                pool.tensor_tensor(neg_cum_heads, cum_parts[:, :].unsqueeze(1).broadcast_to(shape),
                                   head_of_row[:, :].unsqueeze(2).broadcast_to(shape),
                                   ALU.mult).then_inc(S["neg_cum_ready"], 1)

            def diagonals(tiles):
                for n in tiles:
                    t = PE_TILES[n]
                    for half, (k, taps) in enumerate(TAP_HALVES):
                        if n:
                            pool.wait_ge(S["diagonals_used"], 2 * n - 1 + half)
                        col = DW_COL + k * KT + t
                        shape = [P, taps, P]
                        pool.tensor_tensor(wide[:, half * 2048:half * 2048 + taps * P].rearrange("p (k c) -> p k c", c=P),
                                           ident[:, :].unsqueeze(1).broadcast_to(shape),
                                           vec[:, col:col + (taps - 1) * KT + 1:KT].unsqueeze(2).broadcast_to(shape),
                                           ALU.mult).then_inc(S["diagonals_ready"], 1)

            for i, kind in enumerate(phases):
                fold_squares(i)
                if kind == "fox":
                    spread_cums(i // 9)
                elif kind == "conv":
                    diagonals(range(1, len(PE_TILES)))
                if i + 1 < len(phases) and phases[i + 1] == "conv":
                    pool.wait_ge(S["vec_copied"], 8)
                    pool.wait_ge(S["block_done"], starts[i])
                    diagonals(range(1))


        @block.scalar
        def _(act):
            def rows_of(v):
                return v.rearrange("a (t p) -> (a t) p", p=P)

            for kind, name in enumerate(("norm_ffn1", "norm_mix", "norm_ffn2")):
                act.dma_start(vec_rows[32 * kind:32 * kind + 32, 0, :], rows_of(A[name])).then_inc(S["vec_loaded"], 16)
            at = 0
            for name in ("conv_b_pw1", "conv_b_dw", "conv_ln_g", "conv_ln_b", "conv_b_pw2"):
                n = 16 if name == "conv_b_pw1" else 8
                act.dma_start(vec_rows[at:at + n, 1, :], rows_of(A[name])).then_inc(S["vec_loaded"], 16)
                at += n
            taps = rows_of(A["conv_w_dw"][0])
            for half in range(2):
                act.dma_start(vec_rows[0:124, 2 + half, :], taps[124 * half:124 * half + 124, :]
                              ).then_inc(S["vec_loaded"], 16)
            r = 0
            for name, n in (("fox_q_gain", 2), ("fox_k_gain", 2), ("diff_q_gain", 1), ("diff_k_gain", 1)):
                for half in range(2):
                    act.dma_start(head_rows[r:r + n, HEAD * half:HEAD * half + HEAD], A[name]
                                  ).then_inc(S["vec_loaded"], 16)
                r += n
            act.dma_start(head_rows[6:7, :], A["diff_sub_gain"]).then_inc(S["vec_loaded"], 16)
            act.dma_start(pos_int[:, :], A["positions"]).then_inc(S["const_loaded"], 16)
            act.dma_start(fox_bias_rows[:, :], A["fox_b_f"]).then_inc(S["const_loaded"], 16)
            for m, name in enumerate(("q1", "k1", "q2", "k2")):
                act.dma_start(lam_rows[:, m, :], A["diff_lambda_" + name]).then_inc(S["const_loaded"], 16)

            def split_high(b, u=0, per=0):
                if b >= n_blocks:
                    return
                act.wait_ge(raw_landed[b % RING], raw_uses(b, u, per))
                if b >= RING:
                    act.wait_ge(S["block_done"], b - RING + 1 + u * per)
                act.activation(w_high[b % RING][:, :], raw[b % RING][:, :], ACT.Copy).then_inc(S["high_ready"], 1)

            def boundary(i):
                col = NORM_COL + (i % 3) * DEPTH * KT + layer_of(i) * KT
                if i:
                    split_high(starts[i] + 1)
                if i == 0:
                    act.wait_ge(S["vec_copied"], 5)
                for T in range(4):
                    act.wait_ge(S["x_ready"], 4 * i + T + 1)
                    for t in (2 * T, 2 * T + 1):
                        act.activation(x_high[:, t, :], xT[:, t, :], ACT.Copy, scale=vec[:, col + t:col + t + 1]
                                       ).then_inc(S["xhigh_ready"], 1)
                    act.activation(x_square[:, 2 * T:2 * T + 2, :], xT[:, 2 * T:2 * T + 2, :], ACT.Square
                                   ).then_inc(S["xsq_ready"], 1)
                if i == 0:
                    split_high(starts[i] + 1)
                width = SEQ + 2 if phases[i] in ("fox", "diff") else SEQ
                act.wait_ge(S["sumsq_done"], i + 1)
                if i:
                    act.wait_ge(S["inv_rms_ready"], i)
                act.activation(root[:, 0:width], bank[7][:, 0:width], ACT.Sqrt, scale=1.0 / D, bias=eps[:, :]
                               ).then_inc(S["root_ready"], 1)

            def ffn(i):
                b, f = starts[i], number(i)

                def silu(p, u=0):
                    act.wait_ge(S["gate_in_ready"], PAIRS * f + p + 1 + 2 * u)
                    act.activation(gate_silu[:, :], gate_in[:, :], ACT.Silu).then_inc(S["silu_ready"], 1)

                def high(p, u=0):
                    act.wait_ge(S["hidden_ready"], PAIRS * f + p + 1 + 2 * u)
                    act.activation(h_high[p % 2][:, :], hidden[:, :], ACT.Copy).then_inc(S["h_high_ready"], 1)

                def one_pair(p, u=0):
                    split_high(b + 3 * p + 1, u, 6)
                    silu(p, u)
                    split_high(b + 3 * p + 2, u, 6)
                    high(p, u)
                    split_high(b + 3 * p + 3, u, 6)

                split_high(b + 2)
                silu(0)
                split_high(b + 3)
                high(0)
                last = i == len(phases) - 1
                with act.Fori(0, (PAIRS - 1) // 2 - last) as u:
                    one_pair(1, u)
                    one_pair(2, u)
                if last:
                    one_pair(PAIRS - 2)
                    one_pair(PAIRS - 1)

            def attention(i):
                a, b, fox = number(i), starts[i], phases[i] == "fox"
                w = i // 9

                def inverse(x, g, u):
                    buf, at, n = {"q": (q_inv, 3, HEAD), "k": (k_inv, 3, HEAD), "o": (q_square, 6, P)}[x]
                    c = (0 if x == "o" else 4 * a) + g + u + 1
                    act.wait_ge(S[x + "_sum_done"], c)
                    act.activation(buf[:, :], bank[at][:, :], ACT.Ln, scale=1.0 / n, bias=eps[:, :]
                                   ).then_inc(S[x + "_log_ready"], 1)
                    act.wait_ge(S[x + "_log_ready"], c)
                    act.activation(buf[:, :], buf[:, :], ACT.Exp, scale=-0.5).then_inc(S[x + "_inv_ready"], 1)

                def square(x, g, u):
                    src, dst = {"q": (q_raw, q_square), "k": (k_raw, k_square)}[x]
                    act.wait_ge(S[x + "_raw_ready"], 4 * a + g + u + 1)
                    act.activation(dst[:, :], src[:, :], ACT.Square).then_inc(S[x + "_sq_ready"], 1)

                def exps(m, g, u):
                    c = 16 * a + 4 * g + m + 4 * u
                    act.wait_ge(S["masked"], c + 1)
                    s = scores[m % 2]
                    for qb, cols in enumerate((slice(0, P), slice(P, 384))):
                        act.activation(s[:, cols], s[:, cols], ACT.Exp, bias=neg_max[m % 2][:, qb:qb + 1],
                                       accum_out=row_sum[m % 2][:, qb:qb + 1]).then_inc(S["exp_ready"], 1)

                def softplus():
                    steps = ((logit, ACT.Abs, 1.0, fox_bias[:, w:w + 1]), (logit_log, ACT.Exp, -1.0, 0.0),
                             (logit_log, ACT.Ln, 1.0, ones[0:FOX_HEADS, 0:1]))
                    act.wait_ge(S["logit_ready"], w + 1)
                    for n, (src, f, scale, bias) in enumerate(steps):
                        if n:
                            act.wait_ge(S["logit_parts"], 3 * w + n)
                        act.activation(logit_log[:, :], src[:, :], f, scale=scale, bias=bias
                                       ).then_inc(S["logit_parts"], 1)

                def copy_probs(m, g, u):
                    per = 4 if fox else 2
                    c = turned_before[i] + per * g + m + per * u
                    act.wait_ge(S["probs_turned"], c + 1)
                    src = bank[([6, 5, 6, 4] if fox else [6, 6])[m]]
                    act.activation(probsT[m % 2][:, :], src[:, 0:384], ACT.Copy).then_inc(S["probsT_ready"], 1)

                def o_part(g, u):
                    c = turned_before[i] + (4 if fox else 2) * (g + u + 1)
                    act.wait_ge(S["pv_done"], c)
                    if fox:
                        src = pair(bank[7][:, :])
                    else:
                        act.activation(hidden[:, :], bank[7][:, :], ACT.Copy).then_inc(S["o_copied"], 1)
                        act.activation(gate_in[:, :], bank[7][:, :], ACT.Square).then_inc(S["o_sq_ready"], 1)
                        inverse("o", g, u)
                        act.wait_ge(S["o_normed"], g + u + 1)
                        src = pair(gate_silu[:, :])
                    act.activation(o_high[:, bass.ds(2 * (g + u), 2), :], src, ACT.Copy).then_inc(S["o_high_ready"], 1)

                def group(j, u=0):
                    g = j - 1
                    split_high(b + 3 * j + 2, u, 3)
                    if fox and not j:
                        softplus()
                    square("q", j, u)
                    if j:
                        exps(0, g, u)
                        exps(1, g, u)
                    split_high(b + 3 * j + 3, u, 3)
                    if j:
                        copy_probs(0, g, u)
                        if fox:
                            copy_probs(1, g, u)
                        exps(2, g, u)
                    square("k", j, u)
                    inverse("q", j, u)
                    if j:
                        exps(3, g, u)
                    split_high(b + 3 * j + 4, u, 3)
                    inverse("k", j, u)
                    if j:
                        if fox:
                            copy_probs(2, g, u)
                            copy_probs(3, g, u)
                        else:
                            copy_probs(1, g, u)
                        o_part(g, u)

                act.preload_act_table_set("natural_log_exp_and_others")
                group(0)
                with act.Fori(0, GROUPS - 1) as u:
                    group(1, u)
                g = GROUPS - 1
                e = b + 3 * GROUPS
                exps(0, g, 0)
                exps(1, g, 0)
                split_high(e + 2)
                copy_probs(0, g, 0)
                if fox:
                    copy_probs(1, g, 0)
                exps(2, g, 0)
                exps(3, g, 0)
                split_high(e + 3)
                if fox:
                    copy_probs(2, g, 0)
                    copy_probs(3, g, 0)
                else:
                    copy_probs(1, g, 0)
                split_high(e + 4)
                o_part(g, 0)

            def conv(i):
                b = starts[i]
                for j in range(GROUPS):
                    split_high(b + 2 * j + 2)
                    split_high(b + 2 * j + 3)
                    act.wait_ge(S["conv_g_ready"], j + 1)
                    for m in range(2):
                        col = PW1_COL + KT + 2 * j + m
                        act.activation(gate_silu[:, m * SEQ:(m + 1) * SEQ], gate_scaled[:, m * SEQ:(m + 1) * SEQ],
                                       ACT.Sigmoid, bias=vec[:, col:col + 1]).then_inc(S["sigmoid_ready"], 1)
                for n, t in enumerate(PE_TILES):
                    act.wait_ge(S["diagonals_used"], 2 * n + 2)
                    act.activation(y_conv[:, t, :], bank[4 + n][:, 0:SEQ], ACT.Identity,
                                   bias=vec[:, DW_B_COL + t:DW_B_COL + t + 1]).then_inc(S["tile_convolved"], 1)
                split_high(b + 2 * GROUPS + 2)
                for T in range(4):
                    act.wait_ge(S["centred"], T + 1)
                    act.activation(ln_work[:, 2 * T:2 * T + 2, :], y_conv[:, 2 * T:2 * T + 2, :], ACT.Square
                                   ).then_inc(S["centred_sq"], 1)
                act.wait_ge(S["var_done"], 1)
                act.activation(root[:, 0:SEQ], bank[5][:, 0:SEQ], ACT.Sqrt, scale=1.0 / D, bias=eps[:, :]
                               ).then_inc(S["ln_root_ready"], 1)
                e = b + 2 * GROUPS
                for T in range(4):
                    act.wait_ge(S["ln_scaled"], T + 1)
                    for t in (2 * T, 2 * T + 1):
                        act.activation(ln_work[:, t, :], y_conv[:, t, :], ACT.Silu,
                                       scale=vec[:, LN_G_COL + t:LN_G_COL + t + 1],
                                       bias=vec[:, LN_B_COL + t:LN_B_COL + t + 1]).then_inc(S["ln_silu"], 1)
                    act.wait_ge(S["ln_silu"], 2 * T + 2)
                    act.activation(o_high[:, 2 * T:2 * T + 2, :], ln_work[:, 2 * T:2 * T + 2, :], ACT.Copy
                                   ).then_inc(S["o_high_ready"], 1)
                for k in range(3, 5):
                    split_high(e + k)

            act.wait_ge(S["pool_consts"], N_POOL_CONSTS)
            act.wait_ge(S["dve_consts"], DVE_CONSTS)
            split_high(0)
            act.wait_ge(S["lam_step"], 2)
            act.activation(lam_exps[:, :], lam_sums[:, :], ACT.Exp).then_inc(S["lam_step"], 1)
            act.wait_ge(S["rope_step"], 9)
            act.activation(sinT[:, :], angle[:, :], ACT.Sin).then_inc(S["act_rope_step"], 1)
            act.activation(turns[:, :], angle[:, :], ACT.Abs).then_inc(S["act_rope_step"], 1)
            act.wait_ge(S["act_rope_step"], 2)
            act.activation(cosT[:, :], turns[:, :], ACT.Sin, scale=-1.0, bias=half_pi[:, :]
                           ).then_inc(S["act_rope_step"], 1)
            for i, kind in enumerate(phases):
                boundary(i)
                {"ffn": ffn, "fox": attention, "diff": attention, "conv": conv}[kind](i)

        @block.vector
        def _(dve):
            def split_low(b, u=0, per=0):
                if b >= n_blocks:
                    return
                dve.wait_ge(S["high_ready"], b + 1 + u * per)
                dve.tensor_tensor(w_low[b % RING][:, :], raw[b % RING][:, :], w_high[b % RING][:, :].bitcast(F32),
                                  ALU.subtract).then_inc(S["low_ready"], 1)

            def wait_out_bank(i, T):
                if T < 3:
                    dve.wait_ge(S["out_bank_done"], 3 * (i - 1) + T + 1)
                else:
                    dve.wait_ge(S["block_done"], starts[i])

            def update_x(i, T):
                if i == 0:
                    dve.wait_ge(S["x_turned"], T + 1)
                    dve.tensor_copy(xT[:, 2 * T:2 * T + 2, :], pair(bank[T][:, :])).then_inc(S["x_ready"], 1)
                    return
                wait_out_bank(i, T)
                if phases[i - 1] == "conv":
                    for m in range(2):
                        t = 2 * T + m
                        ins = dve.scalar_tensor_tensor(xT[:, t, :], bank[T][:, m * SEQ:(m + 1) * SEQ],
                                                       vec[:, PW2_COL + t:PW2_COL + t + 1], xT[:, t, :],
                                                       ALU.add, ALU.add)
                    ins.then_inc(S["x_ready"], 1)
                else:
                    weight = 0.5 if phases[i - 1] == "ffn" else 1.0
                    dve.scalar_tensor_tensor(xT[:, 2 * T:2 * T + 2, :], pair(bank[T][:, :]), weight,
                                             xT[:, 2 * T:2 * T + 2, :], ALU.mult, ALU.add).then_inc(S["x_ready"], 1)

            def boundary(i):
                col = NORM_COL + (i % 3) * DEPTH * KT + layer_of(i) * KT

                def low(T):
                    for t in (2 * T, 2 * T + 1):
                        dve.wait_ge(S["xhigh_ready"], 8 * i + t + 1)
                        dve.scalar_tensor_tensor(x_low[:, t, :], xT[:, t, :], vec[:, col + t:col + t + 1],
                                                 x_high[:, t, :].bitcast(F32), ALU.mult, ALU.subtract
                                                 ).then_inc(S["xlow_ready"], 1)

                if phases[i] == "fox":
                    w = i // 9
                    dve.wait_ge(S["gate_w_loaded"], 16 * (w + 1))
                    if w:
                        dve.wait_ge(S["logits_done"], w)
                    dve.tensor_tensor(gate_w_gained[:, :, :], gate_w[:, :, :],
                                      vec[:, col:col + KT].unsqueeze(2).broadcast_to([P, KT, FOX_HEADS]), ALU.mult
                                      ).then_inc(S["gate_w_ready"], 1)
                for T in range(4):
                    update_x(i, T)
                    if T:
                        low(T - 1)
                low(3)
                split_low(starts[i] + 1)
                width = SEQ + 2 if phases[i] in ("fox", "diff") else SEQ
                dve.wait_ge(S["root_ready"], i + 1)
                dve.reciprocal(inv_rms[:, 0:width], root[:, 0:width]).then_inc(S["inv_rms_ready"], 1)
                dve.wait_ge(S["inv_rms_ready"], i + 1)

            def ffn(i):
                b, f = starts[i], number(i)

                def gate(p, u=0):
                    dve.wait_ge(S["block_done"], b + (3 * p if p else 1) + 6 * u)
                    dve.tensor_tensor(pair(gate_in[:, :]), pair(bank[4][:, :]), over_tokens(inv_rms[:, 0:SEQ]),
                                      ALU.mult).then_inc(S["gate_in_ready"], 1)

                def up(p, u=0):
                    c = PAIRS * f + p + 1 + 2 * u
                    dve.wait_ge(S["silu_ready"], c)
                    dve.tensor_tensor(pair(gate_scaled[:, :]), pair(gate_silu[:, :]), over_tokens(inv_rms[:, 0:SEQ]),
                                      ALU.mult).then_inc(S["gate_scaled_ready"], 1)
                    dve.wait_ge(S["gate_scaled_ready"], c)
                    dve.wait_ge(S["block_done"], b + (3 * p + 1 if p else 2) + 6 * u)
                    dve.tensor_tensor(hidden[:, :], bank[5][:, :], gate_scaled[:, :], ALU.mult
                                      ).then_inc(S["hidden_ready"], 1)

                def low(p, u=0):
                    dve.wait_ge(S["h_high_ready"], PAIRS * f + p + 1 + 2 * u)
                    dve.tensor_tensor(h_low[p % 2][:, :], hidden[:, :], h_high[p % 2][:, :].bitcast(F32),
                                      ALU.subtract).then_inc(S["h_low_ready"], 1)

                def one_pair(p, u=0):
                    split_low(b + 3 * p + 1, u, 6)
                    gate(p, u)
                    split_low(b + 3 * p + 2, u, 6)
                    up(p, u)
                    low(p, u)
                    split_low(b + 3 * p + 3, u, 6)

                split_low(b + 2)
                gate(0)
                up(0)
                split_low(b + 3)
                low(0)
                last = i == len(phases) - 1
                with dve.Fori(0, (PAIRS - 1) // 2 - last) as u:
                    one_pair(1, u)
                    one_pair(2, u)
                if last:
                    one_pair(PAIRS - 2)
                    one_pair(PAIRS - 1)

            def attention(i):
                a, b, fox = number(i), starts[i], phases[i] == "fox"
                w = i // 9
                gain = {"q": HEAD_COL + (w if fox else 4), "k": HEAD_COL + (2 + w if fox else 5)}

                def raw_part(x, j, u):
                    src, dst = {"q": (bank[0], q_raw), "k": (bank[1], k_raw)}[x]
                    c = 4 * a + j + u
                    dve.wait_ge(S["block_done"], b + 3 * j + (1 if x == "q" else 2) + 3 * u)
                    if j or a:
                        dve.wait_ge(S[x + "_ready"], c)
                    dve.tensor_tensor(pair(dst[:, :]), pair(src[:, :]), over_tokens(inv_rms[:, 0:SEQ]), ALU.mult
                                      ).then_inc(S[x + "_raw_ready"], 1)

                def normed(x, j, u):
                    raw_, inv, fin = {"q": (q_raw, q_inv, qT), "k": (k_raw, k_inv, kT)}[x]
                    c = 4 * a + j + u + 1
                    dve.wait_ge(S[x + "_inv_ready"], c)
                    dst, ready = (fin, "_ready") if fox else (raw_, "_normed")
                    dve.scalar_tensor_tensor(dst[:, :], raw_[:, :], vec[:, gain[x]:gain[x] + 1], inv[:, :],
                                             ALU.mult, ALU.mult).then_inc(S[x + ready], 1)

                def rotated(x, j, u):
                    raw_, tmp, fin = {"q": (q_raw, q_square, qT), "k": (k_raw, k_square, kT)}[x]
                    c = j + u + 1
                    tmp2 = {"q": q_inv, "k": k_inv}[x]
                    dve.wait_ge(S[x + "_normed"], c)
                    dve.tensor_tensor(pair(tmp2[:, :]), pair(raw_[:, :]), over_tokens(cosT[:, :]), ALU.mult
                                      ).then_inc(S[x + "_cos"], 1)
                    dve.wait_ge(S[x + "_swapped"], c)
                    dve.tensor_tensor(pair(tmp[:, :]), pair(bank[3][:, :]), over_tokens(sinT[:, :]), ALU.mult
                                      ).then_inc(S[x + "_sin"], 1)
                    dve.wait_ge(S[x + "_cos"], c)
                    dve.wait_ge(S[x + "_sin"], c)
                    dve.tensor_tensor(fin[:, :], tmp2[:, :], tmp[:, :], ALU.add).then_inc(S[x + "_ready"], 1)

                def mask_and_max(m, g, u):
                    c = 16 * a + 4 * g + m + 4 * u
                    s, src = scores[m % 2], bank[4 + m % 2]
                    dve.wait_ge(S["scores_done"], c + 1)
                    parts = ((0, slice(0, P)), (1, slice(P, 384)))
                    for qb, cols in parts:
                        if fox:
                            cq = neg_cum_q[:, bass.ds(u * 4 + (FOX_HEADS * qb + 4 * g + m), 1)]
                            dve.scalar_tensor_tensor(s[:, cols], src[:, cols], cq, causal[:, cols],
                                                     ALU.subtract, ALU.add).then_inc(S["score_added"], 1)
                        else:
                            dve.tensor_tensor(s[:, cols], src[:, cols], chunked[:, cols], ALU.add
                                              ).then_inc(S["score_added"], 1)
                    for qb, cols in parts:
                        dve.wait_ge(S["score_added"], 2 * c + qb + 1)
                        ins = dve.tensor_reduce(neg_max[m % 2][:, qb:qb + 1], s[:, cols], AX.X, ALU.max, negate=True)
                    ins.then_inc(S["masked"], 1)

                def normalise(m, g, u):
                    c = 16 * a + 4 * g + m + 4 * u
                    s = scores[m % 2]
                    dve.wait_ge(S["exp_ready"], 2 * c + 2)
                    dve.reciprocal(inv_sum[m % 2][:, :], row_sum[m % 2][:, :]).then_inc(S["inv_sum_ready"], 1)
                    dve.wait_ge(S["inv_sum_ready"], c + 1)
                    if fox:
                        for qb, cols in enumerate((slice(0, P), slice(P, 384))):
                            ins = dve.tensor_scalar(s[:, cols], s[:, cols], inv_sum[m % 2][:, qb:qb + 1], None, ALU.mult)
                        ins.then_inc(S["probs_ready"], 1)

                def combine(h, g, u):
                    c = 2 * (g + u) + h
                    normalise(2 * h, g, u)
                    normalise(2 * h + 1, g, u)
                    dve.tensor_scalar(lam_inv_sum[:, :], inv_sum[1][:, :], neg_lam[:, 0:1], None, ALU.mult
                                      ).then_inc(S["lam_scaled"], 1)
                    for qb, cols in enumerate((slice(0, P), slice(P, 384))):
                        dve.tensor_scalar(scores[0][:, cols], scores[0][:, cols], inv_sum[0][:, qb:qb + 1], None,
                                          ALU.mult).then_inc(S["probs_half"], 1)
                    dve.wait_ge(S["lam_scaled"], c + 1)
                    for qb, cols in enumerate((slice(0, P), slice(P, 384))):
                        dve.wait_ge(S["probs_half"], 2 * c + qb + 1)
                        ins = dve.scalar_tensor_tensor(scores[0][:, cols], scores[1][:, cols],
                                                       lam_inv_sum[:, qb:qb + 1], scores[0][:, cols],
                                                       ALU.mult, ALU.add)
                    ins.then_inc(S["probs_ready"], 1)

                def values(j, u):
                    dve.wait_ge(S["block_done"], b + 3 * j + 3 + 3 * u)
                    if j:
                        per = 4 if fox else 2
                        dve.wait_ge(S["pv_done"], turned_before[i] + per * (j + u))
                    for tt in range(2):
                        ins = dve.tensor_scalar(v_nat[:, tt, :], bank[2][:, tt * 256:(tt + 1) * 256],
                                                inv_rms[:, SEQ + tt:SEQ + tt + 1], None, ALU.mult)
                    ins.then_inc(S["v_ready"], 1)

                def o_part(g, u):
                    at = bass.ds(2 * (g + u), 2)
                    if fox:
                        src = pair(bank[7][:, :])
                    else:
                        dve.wait_ge(S["o_inv_ready"], g + u + 1)
                        dve.scalar_tensor_tensor(gate_silu[:, :], hidden[:, :], vec[:, HEAD_COL + 6:HEAD_COL + 7],
                                                 q_square[:, :], ALU.mult, ALU.mult).then_inc(S["o_normed"], 1)
                        src = pair(gate_silu[:, :])
                    dve.wait_ge(S["o_high_ready"], o_before[i] + g + u + 1)
                    dve.tensor_tensor(o_low[:, at, :], src, o_high[:, at, :].bitcast(F32), ALU.subtract
                                      ).then_inc(S["o_bank_free"], 1)

                def logits():
                    dve.wait_ge(S["logits_done"], w + 1)
                    dve.tensor_tensor(logit[:, :], bank[6][0:FOX_HEADS, 0:SEQ], inv_rms[0:FOX_HEADS, 0:SEQ], ALU.mult
                                      ).then_inc(S["logit_ready"], 1)
                    dve.wait_ge(S["logit_ready"], w + 1)
                    dve.tensor_scalar(logit_min[:, :], logit[:, :], fox_bias[:, w:w + 1], 0.0, ALU.add, ALU.min
                                      ).then_inc(S["logit_min_ready"], 1)

                def cumulate():
                    dve.wait_ge(S["logit_parts"], 3 * w + 3)
                    dve.wait_ge(S["logit_min_ready"], w + 1)
                    dve.tensor_tensor_scan(neg_cumT[:, :], logit_log[:, :], logit_min[:, :], 0.0, ALU.add,
                                           ALU.subtract).then_inc(S["neg_cumT_ready"], 1)

                def split_cum():
                    dve.wait_ge(S["cum_turned"], w + 1)
                    dve.tensor_copy(neg_cum_q[:, :], bank[6][:, SEQ:SEQ + 2 * FOX_HEADS]).then_inc(S["cum_q_ready"], 1)
                    dve.wait_ge(S["cum_q_ready"], w + 1)
                    if w:
                        dve.wait_ge(S["neg_cum_ready"], w)
                    for c in range(3):
                        rows = slice(32 * c, 32 * c + FOX_HEADS)
                        dve.tensor_copy(cum_part[:, :], neg_cumT[:, :]).then_inc(S["cum_split_step"], 1)
                        dve.wait_ge(S["cum_split_step"], 7 * w + 3 * c + 1)
                        ins = dve.tensor_copy(cum_parts[rows, :], cum_part[:, :])
                        if c < 2:
                            ins.then_inc(S["cum_split_step"], 1)
                            dve.tensor_tensor(neg_cumT[:, :], neg_cumT[:, :], cum_part[:, :], ALU.subtract
                                              ).then_inc(S["cum_split_step"], 1)
                            dve.wait_ge(S["cum_split_step"], 7 * w + 3 * c + 3)
                        else:
                            ins.then_inc(S["cum_parts_ready"], 1)

                def group(j, u=0):
                    g = j - 1
                    if fox and not j:
                        logits()
                    split_low(b + 3 * j + 2, u, 3)
                    if fox and not j:
                        cumulate()
                    raw_part("q", j, u)
                    if j:
                        mask_and_max(0, g, u)
                        mask_and_max(1, g, u)
                        if fox:
                            normalise(0, g, u)
                            normalise(1, g, u)
                        else:
                            combine(0, g, u)
                    if j:
                        split_low(b + 3 * j + 3, u, 3)
                        mask_and_max(2, g, u)
                        raw_part("k", j, u)
                        mask_and_max(3, g, u)
                    else:
                        raw_part("k", j, u)
                        split_low(b + 3 * j + 3, u, 3)
                        if fox:
                            split_cum()
                    normed("q", j, u)
                    if j:
                        if fox:
                            normalise(2, g, u)
                            normalise(3, g, u)
                        else:
                            combine(1, g, u)
                    if not fox:
                        rotated("q", j, u)
                    split_low(b + 3 * j + 4, u, 3)
                    normed("k", j, u)
                    if not fox:
                        rotated("k", j, u)
                    values(j, u)
                    if j:
                        o_part(g, u)

                group(0)
                with dve.Fori(0, GROUPS - 1) as u:
                    group(1, u)
                g, e = GROUPS - 1, b + 3 * GROUPS
                mask_and_max(0, g, 0)
                mask_and_max(1, g, 0)
                if fox:
                    normalise(0, g, 0)
                    normalise(1, g, 0)
                else:
                    combine(0, g, 0)
                split_low(e + 2)
                mask_and_max(2, g, 0)
                mask_and_max(3, g, 0)
                if fox:
                    normalise(2, g, 0)
                    normalise(3, g, 0)
                else:
                    combine(1, g, 0)
                split_low(e + 3)
                split_low(e + 4)
                o_part(g, 0)

            def conv(i):
                b = starts[i]
                done = {}
                count = [0]

                def first_taps(tiles):
                    for t in tiles:
                        dve.tensor_scalar(y_conv[:, t, :], u_pad[:, t, 0:SEQ], vec[:, DW_COL + t:DW_COL + t + 1],
                                          vec[:, DW_B_COL + t:DW_B_COL + t + 1], ALU.mult, ALU.add
                                          ).then_inc(S["tap_done"], 1)
                        count[0] += 1

                def more_taps(tiles, k0, rounds, a_round):
                    n = len(tiles)
                    with dve.Fori(0, rounds) as r:
                        for k in range(a_round):
                            for m, t in enumerate(tiles):
                                dve.wait_ge(S["tap_done"], count[0] + n * (k - 1) + m + 1 + r * (n * a_round))
                                dve.scalar_tensor_tensor(
                                    y_conv[:, t, :], u_pad[:, t, bass.ds(r * a_round + (k0 + k), SEQ)],
                                    vec[:, bass.ds(r * (a_round * KT) + (DW_COL + (k0 + k) * KT + t), 1)],
                                    y_conv[:, t, :], ALU.mult, ALU.add).then_inc(S["tap_done"], 1)
                    count[0] += n * rounds * a_round

                for j in range(GROUPS):
                    split_low(b + 2 * j + 2)
                    dve.wait_ge(S["block_done"], b + 2 * j + 1)
                    dve.tensor_tensor(pair(gate_in[:, :]), pair(bank[2 * (j % 2)][:, :]),
                                      over_tokens(inv_rms[:, 0:SEQ]), ALU.mult).then_inc(S["conv_a_ready"], 1)
                    if j:
                        more_taps((0, 1), 10 * j - 4, 1, 5)
                    split_low(b + 2 * j + 3)
                    dve.wait_ge(S["block_done"], b + 2 * j + 2)
                    dve.tensor_tensor(pair(gate_scaled[:, :]), pair(bank[2 * (j % 2) + 1][:, :]),
                                      over_tokens(inv_rms[:, 0:SEQ]), ALU.mult).then_inc(S["conv_g_ready"], 1)
                    dve.wait_ge(S["conv_a_ready"], j + 1)
                    dve.wait_ge(S["sigmoid_ready"], 2 * j + 2)
                    for m in range(2):
                        t = 2 * j + m
                        dve.scalar_tensor_tensor(u_pad[:, t, TAPS - 1:], gate_in[:, m * SEQ:(m + 1) * SEQ],
                                                 vec[:, PW1_COL + t:PW1_COL + t + 1],
                                                 gate_silu[:, m * SEQ:(m + 1) * SEQ], ALU.add, ALU.mult
                                                 ).then_inc(S["u_ready"], 1)
                    dve.wait_ge(S["u_ready"], 2 * j + 2)
                    if j == 0:
                        first_taps((0, 1))
                    if j < GROUPS - 1:
                        more_taps((0, 1), 10 * j + 1, 1, 5)
                first_taps((2, 3, 4))
                more_taps((2, 3, 4), 1, 6, 5)
                e = b + 2 * GROUPS
                split_low(e + 2)
                assert count[0] == DVE_TAPS
                dve.wait_ge(S["mean_done"], 1)
                for T in range(4):
                    dve.scalar_tensor_tensor(y_conv[:, 2 * T:2 * T + 2, :], over_tokens(bank[7][:, 0:SEQ]), -1.0 / D,
                                             y_conv[:, 2 * T:2 * T + 2, :], ALU.mult, ALU.add
                                             ).then_inc(S["centred"], 1)
                dve.wait_ge(S["ln_root_ready"], 1)
                dve.reciprocal(ln_inv[:, :], root[:, 0:SEQ]).then_inc(S["ln_inv_ready"], 1)
                dve.wait_ge(S["ln_inv_ready"], 1)
                for T in range(4):
                    dve.tensor_tensor(y_conv[:, 2 * T:2 * T + 2, :], y_conv[:, 2 * T:2 * T + 2, :],
                                      over_tokens(ln_inv[:, :]), ALU.mult).then_inc(S["ln_scaled"], 1)
                for T in range(4):
                    dve.wait_ge(S["o_high_ready"], o_before[i] + T + 1)
                    dve.tensor_tensor(o_low[:, 2 * T:2 * T + 2, :], ln_work[:, 2 * T:2 * T + 2, :],
                                      o_high[:, 2 * T:2 * T + 2, :].bitcast(F32), ALU.subtract
                                      ).then_inc(S["o_bank_free"], 1)
                for k in range(3, 5):
                    split_low(e + k)

            dve.memset(eps[:, :], EPS).then_inc(S["dve_consts"], 1)
            dve.memset(half_pi[:, :], math.pi / 2).then_inc(S["dve_consts"], 1)
            dve.memset(rope_rows[:, :, :], 0.0).then_inc(S["dve_consts"], 1)
            dve.wait_ge(S["dve_consts"], 3)
            half = ROT // 2
            per_head = rope_rows[:, :, :].rearrange("o r (h a c) -> o r h a c", h=2, c=half)
            for c in range(half):
                dve.memset(per_head[:, 0, :, 0:2, c], ROPE_THETA ** (-2.0 * c / ROT)).then_inc(S["dve_consts"], 1)
            dve.memset(per_head[:, 1, :, 0, :], -1.0).then_inc(S["dve_consts"], 1)
            dve.memset(per_head[:, 1, :, 1, :], 1.0).then_inc(S["dve_consts"], 1)
            dve.memset(per_head[:, 2, :, 0:2, :], 1.0).then_inc(S["dve_consts"], 1)
            dve.memset(row_sum[0][:, :], 1.0).then_inc(S["o_bank_free"], 1)
            dve.memset(cum_parts[:, :], 0.0).then_inc(S["dve_consts"], 1)
            dve.memset(ones_bf[:, :], 1.0).then_inc(S["dve_consts"], 1)
            dve.memset(head_of_row[:, :], 0.0).then_inc(S["dve_consts"], 1)
            dve.wait_ge(S["pool_consts"], N_POOL_CONSTS)
            for h in range(2):
                for c in range(2):
                    dve.tensor_copy(swap[:, HEAD * h + half * c:HEAD * h + half * (c + 1)],
                                    ident[:, HEAD * h + half * (1 - c):HEAD * h + half * (2 - c)]
                                    ).then_inc(S["dve_consts"], 1)
            dve.wait_ge(S["dve_consts"], 21)
            for c in range(3):
                rows = slice(32 * c, 32 * c + 32)
                dve.tensor_copy(head_of_row[rows, :], ident[rows, 32 * c:32 * c + FOX_HEADS]
                                ).then_inc(S["dve_consts"], 1)
            dve.wait_ge(S["const_loaded"], 96)
            dve.tensor_copy(pos_row[:, :], pos_int[:, :]).then_inc(S["dve_consts"], 1)
            dve.tensor_tensor(lam_products[:, :, :], lam_rows[:, 0:4:2, :], lam_rows[:, 1:4:2, :], ALU.mult
                              ).then_inc(S["lam_step"], 1)
            dve.wait_ge(S["lam_step"], 1)
            dve.tensor_reduce(lam_sums[:, :], lam_products[:, :, :], AX.X, ALU.add).then_inc(S["lam_step"], 1)
            dve.wait_ge(S["vec_turned"], 1)
            for n, (col, width) in enumerate(((NORM_COL, 96), (PW1_COL, 48), (DW_COL, 124), (DW_COL + 124, 124),
                                              (HEAD_COL, 7))):
                at = [0, 96, 144, 268, 392][n]
                dve.tensor_copy(vec[:, col:col + width], bank[6][:, at:at + width]).then_inc(S["vec_copied"], 1)
            dve.wait_ge(S["vec_copied"], 5)
            for col, n, s in ((HEAD_COL, 2, fox_scale), (HEAD_COL + 4, 1, fox_scale), (HEAD_COL + 6, 1, 1.0 - lambda_init)):
                dve.tensor_scalar(vec[:, col:col + n], vec[:, col:col + n], s, None, ALU.mult
                                  ).then_inc(S["vec_copied"], 1)
            split_low(0)
            dve.wait_ge(S["lam_step"], 3)
            dve.tensor_tensor(neg_lam_row[:, :], lam_exps[:, 1:2], lam_exps[:, 0:1], ALU.subtract
                              ).then_inc(S["lam_step"], 1)
            dve.wait_ge(S["lam_step"], 4)
            dve.tensor_scalar(neg_lam_row[:, :], neg_lam_row[:, :], -lambda_init, None, ALU.add
                              ).then_inc(S["lam_step"], 1)
            dve.wait_ge(S["small_done"], 1)
            dve.tensor_copy(rope_cols[:, :], bank[5][:, 0:3]).then_inc(S["rope_step"], 1)
            dve.tensor_copy(fox_bias[:, :], bank[5][0:FOX_HEADS, 32:34]).then_inc(S["rope_step"], 1)
            dve.wait_ge(S["rope_step"], 2)
            dve.tensor_scalar(angle[:, :], bank[5][:, 256:512], rope_cols[:, 0:1], None, ALU.mult
                              ).then_inc(S["rope_step"], 1)
            dve.wait_ge(S["rope_step"], 3)
            dve.tensor_scalar(turns[:, :], angle[:, :], 1.0 / (2.0 * math.pi), ROUND, ALU.mult, ALU.add
                              ).then_inc(S["rope_step"], 1)
            dve.wait_ge(S["rope_step"], 4)
            dve.tensor_scalar(turns[:, :], turns[:, :], ROUND, None, ALU.subtract).then_inc(S["rope_step"], 1)
            for n, part in enumerate((TWO_PI_1, TWO_PI_2, TWO_PI_3)):
                dve.wait_ge(S["rope_step"], 5 + n)
                dve.scalar_tensor_tensor(angle[:, :], turns[:, :], -part, angle[:, :], ALU.mult, ALU.add
                                         ).then_inc(S["rope_step"], 1)
            dve.wait_ge(S["rope_step"], 8)
            dve.tensor_scalar(angle[:, :], angle[:, :], math.pi, -math.pi, ALU.min, ALU.max
                              ).then_inc(S["rope_step"], 1)
            dve.wait_ge(S["act_rope_step"], 3)
            dve.tensor_scalar(sinT[:, :], sinT[:, :], rope_cols[:, 1:2], None, ALU.mult).then_inc(S["rope_step"], 1)
            dve.tensor_scalar(not_rotated[:, :], rope_cols[:, 2:3], -1.0, 1.0, ALU.mult, ALU.add
                              ).then_inc(S["rope_step"], 1)
            dve.wait_ge(S["rope_step"], 11)
            dve.tensor_scalar(cosT[:, :], cosT[:, :], rope_cols[:, 2:3], not_rotated[:, 0:1], ALU.mult, ALU.add
                              ).then_inc(S["rope_step"], 1)
            dve.wait_ge(S["small_done"], 2)
            dve.tensor_copy(neg_lam[:, :], bank[4][:, 0:1]).then_inc(S["rope_step"], 1)
            dve.wait_ge(S["rope_step"], 13)
            dve.wait_ge(S["vec_copied"], 8)

            for i, kind in enumerate(phases):
                boundary(i)
                {"ffn": ffn, "fox": attention, "diff": attention, "conv": conv}[kind](i)
            last = len(phases)
            for T in range(4):
                update_x(last, T)
            for tt in range(2):
                for m in range(2):
                    n = 2 * tt + m
                    dve.wait_ge(S["final_turned"], n + 1)
                    dve.tensor_copy(by_token[tt][:, m * 512:(m + 1) * 512], bank[4 + n][:, :]
                                    ).then_inc(S["final_copied"], 1)

        @block.tensor
        def _(pe):
            def three_passes(dst, s_high, s_low, m_high, m_low, first, last, loose=False):
                pe.matmul(dst, s_high, m_high, start=first, stop=False, skip_group_check=loose)
                pe.matmul(dst, s_high, m_low, start=False, stop=False, skip_group_check=loose)
                return pe.matmul(dst, s_low, m_high, start=False, stop=last, skip_group_check=loose)

            def wait_block(b, u=0, per=0):
                pe.wait_ge(S["low_ready"], b + 1 + u * per)

            def columns_half(dst, b, n):
                high, low = (t[b % RING][:, :].rearrange("p (k n) -> p k n", k=KT) for t in (w_high, w_low))
                for k in range(KT):
                    cols = slice(n * P, (n + 1) * P)
                    ins = three_passes(dst[:, n * SEQ:(n + 1) * SEQ], high[:, k, cols], low[:, k, cols],
                                       x_high[:, k, :], x_low[:, k, :], k == 0, k == KT - 1)
                return ins

            def tokens_half(dst, b, tt):
                high, low = (t[b % RING][:, :].rearrange("p (k n) -> p k n", k=KT) for t in (w_high, w_low))
                toks = slice(tt * P, (tt + 1) * P)
                for k in range(KT):
                    ins = three_passes(dst[:, tt * 256:(tt + 1) * 256], x_high[:, k, toks], x_low[:, k, toks],
                                       high[:, k, :], low[:, k, :], k == 0, k == KT - 1)
                return ins

            def rows_block(b, m_high, m_low, first, last, u=0, per=0):
                wait_block(b, u, per)
                high, low = (t[b % RING][:, :].rearrange("p (f n) -> p f n", f=2) for t in (w_high, w_low))
                for d in range(KT):
                    for f in range(2):
                        cols = slice(d * P, (d + 1) * P)
                        ins = three_passes(bank[d // 2][:, (d % 2) * SEQ:(d % 2 + 1) * SEQ],
                                           high[:, f, cols], low[:, f, cols], m_high[:, f, :], m_low[:, f, :],
                                           first and d % 2 == 0 and f == 0, last and f == 1, True)
                    if last and d % 2 and d < KT - 1:
                        ins.then_inc(S["out_bank_done"], 1)
                ins.then_inc(S["block_done"], 1)

            def first_block(i, dst):
                b = starts[i]
                wait_block(b)
                high, low = (t[b % RING][:, :].rearrange("p (k n) -> p k n", k=KT) for t in (w_high, w_low))
                for k in range(KT):
                    pe.wait_ge(S["xlow_ready"], 8 * i + k + 1)
                    for n in range(2):
                        cols = slice(n * P, (n + 1) * P)
                        ins = three_passes(dst[:, n * SEQ:(n + 1) * SEQ], high[:, k, cols], low[:, k, cols],
                                           x_high[:, k, :], x_low[:, k, :], k == 0 and n == 0, k == KT - 1, True)
                ins.then_inc(S["block_done"], 1)
                pe.wait_ge(S["square_folded"], 6 * i + 6)
                for k in range(2):
                    ins = pe.matmul(bank[7][:, 0:SEQ], ones[:, :], square_sum[:, k, :], start=k == 0, stop=k == 1)
                if phases[i] in ("fox", "diff"):
                    for tt in range(2):
                        for k in range(2):
                            ins = pe.matmul(bank[7][:, SEQ + tt:SEQ + tt + 1], square_sum[:, k, tt * P:(tt + 1) * P],
                                            ones[:, 0:1], start=k == 0, stop=k == 1)
                ins.then_inc(S["sumsq_done"], 1)

            def ffn(i):
                b, f = starts[i], number(i)

                def gate_up(which, p, u=0):
                    blk = b + 3 * p - 1 + which
                    wait_block(blk, u, 6)
                    pe.wait_ge(S["hidden_ready" if which else "gate_in_ready"], PAIRS * f + p + 2 * u)
                    columns_half(bank[4 + which], blk, 0)
                    columns_half(bank[4 + which], blk, 1).then_inc(S["block_done"], 1)

                def down(blk, p, u, first, last):
                    pe.wait_ge(S["h_low_ready"], PAIRS * f + p + 1 + 2 * u)
                    rows_block(blk, pair(h_high[p % 2][:, :]), pair(h_low[p % 2][:, :]), first, last, u, 6)

                def one_pair(p, u=0, first=False):
                    gate_up(0, p, u)
                    gate_up(1, p, u)
                    down(b + 3 * p + 1, p - 1, u, first, False)

                first_block(i, bank[4])
                wait_block(b + 1)
                columns_half(bank[5], b + 1, 0)
                columns_half(bank[5], b + 1, 1).then_inc(S["block_done"], 1)
                one_pair(1, first=True)
                one_pair(2)
                with pe.Fori(1, (PAIRS - 1) // 2) as u:
                    one_pair(1, u)
                    one_pair(2, u)
                down(b + 3 * PAIRS - 1, PAIRS - 1, 0, False, True)

            def attention(i):
                a, b, fox = number(i), starts[i], phases[i] == "fox"
                w = i // 9
                per = 4 if fox else 2

                def head_scores(m, g, u):
                    c = 16 * a + 4 * g + m + 4 * u
                    dst = bank[4 + m % 2]
                    if m == 0:
                        pe.wait_ge(S["q_ready"], 4 * a + g + u + 1)
                        pe.wait_ge(S["k_ready"], 4 * a + g + u + 1)
                        if fox:
                            pe.wait_ge(S["neg_cum_ready"], w + 1)
                    if fox and m == 3:
                        pe.wait_ge(S["probsT_ready"], turned_before[i] + 4 * g + 2 + 4 * u)
                    if m >= 2:
                        pe.wait_ge(S["masked"], c - 1)
                    tile, r = m // 2, slice(HEAD * (m % 2), HEAD * (m % 2) + HEAD)
                    for qb, cols, keys in ((0, slice(0, P), P), (1, slice(P, 384), SEQ)):
                        q = qT[r, tile * SEQ + qb * P:tile * SEQ + (qb + 1) * P]
                        ins = pe.matmul(dst[:, cols], q, kT[r, tile * SEQ:tile * SEQ + keys], start=True, stop=not fox)
                        if fox:
                            at = u * (4 * SEQ) + (4 * g + m) * SEQ
                            ins = pe.matmul(dst[:, cols], ones_bf[:, :], neg_cum_wide[:, bass.ds(at, keys)],
                                            start=False, stop=True)
                    ins.then_inc(S["scores_done"], 1)

                def turn(m, g, u):
                    c = turned_before[i] + per * (g + u) + m
                    pe.wait_ge(S["probs_ready"], c + 1)
                    if m == 1 and not fox:
                        pe.wait_ge(S["probsT_ready"], c)
                    dst = bank[([6, 5, 6, 4] if fox else [6, 6])[m]]
                    for n in range(3):
                        ins = pe.transpose(dst[:, n * P:(n + 1) * P], scores[m % 2 if fox else 0][:, n * P:(n + 1) * P],
                                           ident[:, :])
                    ins.then_inc(S["probs_turned"], 1)

                def values(m, g, u):
                    c = turned_before[i] + per * (g + u) + m
                    pe.wait_ge(S["probsT_ready"], c + 1)
                    if m == 0:
                        pe.wait_ge(S["v_ready"], 4 * a + g + u + 1)
                        pe.wait_ge(S["o_bank_free"], o_before[i] + g + u + 1)
                    p = probsT[m % 2]
                    if fox:
                        r, at = slice(HEAD * (m % 2), HEAD * (m % 2) + HEAD), (m // 2) * SEQ
                        cols = slice(HEAD * m, HEAD * m + HEAD)
                    else:
                        r, at, cols = slice(0, P), m * SEQ, slice(P * m, P * m + P)
                    pe.matmul(bank[7][r, at:at + SEQ], v_nat[:, 0, cols], p[:, 0:SEQ], start=True, stop=False)
                    pe.matmul(bank[7][r, at + P:at + SEQ], v_nat[:, 1, cols], p[:, SEQ:384], start=False, stop=True
                              ).then_inc(S["pv_done"], 1)

                def head_sums(x, j, u):
                    c = 4 * a + j + u + 1
                    pe.wait_ge(S[x + "_sq_ready"], c)
                    if x == "k":
                        pe.wait_ge(S["q_log_ready"], c)
                        if not fox:
                            pe.wait_ge(S["q_sin"], j + u + 1)
                    pe.matmul(bank[3][:, :], ones_heads[:, :], {"q": q_square, "k": k_square}[x][:, :],
                              start=True, stop=True).then_inc(S[x + "_sum_done"], 1)

                def swapped(x, j, u):
                    pe.wait_ge(S[x + "_normed"], j + u + 1)
                    pe.matmul(bank[3][:, :], swap[:, :], {"q": q_raw, "k": k_raw}[x][:, :],
                              start=True, stop=True).then_inc(S[x + "_swapped"], 1)

                def o_sums(g, u):
                    pe.wait_ge(S["o_sq_ready"], g + u + 1)
                    pe.matmul(bank[6][:, :], ones[:, :], gate_in[:, :], start=True, stop=True
                              ).then_inc(S["o_sum_done"], 1)

                def group(j, u=0):
                    g = j - 1
                    q_blk, k_blk, v_blk = (b + 3 * j + n for n in range(3))
                    if j:
                        wait_block(q_blk, u, 3)
                        columns_half(bank[0], q_blk, 0)
                        columns_half(bank[0], q_blk, 1).then_inc(S["block_done"], 1)
                        head_scores(0, g, u)
                        head_scores(1, g, u)
                    else:
                        first_block(i, bank[0])
                        if fox:
                            forget_gates()
                    wait_block(k_blk, u, 3)
                    columns_half(bank[1], k_blk, 0)
                    columns_half(bank[1], k_blk, 1).then_inc(S["block_done"], 1)
                    if fox and not j:
                        turn_cum()
                    if j:
                        turn(0, g, u)
                        if fox:
                            turn(1, g, u)
                        head_scores(2, g, u)
                    head_sums("q", j, u)
                    if j:
                        head_scores(3, g, u)
                    wait_block(v_blk, u, 3)
                    if j:
                        pe.wait_ge(S["v_ready"], 4 * a + j + u)
                    tokens_half(bank[2], v_blk, 0)
                    if not fox:
                        swapped("q", j, u)
                    if j:
                        values(0, g, u)
                        if fox:
                            values(1, g, u)
                    head_sums("k", j, u)
                    tokens_half(bank[2], v_blk, 1).then_inc(S["block_done"], 1)
                    if j:
                        if fox:
                            turn(2, g, u)
                            turn(3, g, u)
                        else:
                            turn(1, g, u)
                    if not fox:
                        swapped("k", j, u)
                    if j:
                        if fox:
                            values(2, g, u)
                            values(3, g, u)
                        else:
                            values(1, g, u)
                            o_sums(g, u)

                def forget_gates():
                    pe.wait_ge(S["gate_w_ready"], w + 1)
                    for k in range(KT):
                        ins = pe.matmul(bank[6][0:FOX_HEADS, 0:SEQ], gate_w_gained[:, k, :], xT[:, k, :],
                                        start=k == 0, stop=k == KT - 1)
                    ins.then_inc(S["logits_done"], 1)

                def turn_cum():
                    pe.wait_ge(S["neg_cumT_ready"], w + 1)
                    for tt in range(2):
                        at = SEQ + FOX_HEADS * tt
                        ins = pe.transpose(bank[6][:, at:at + FOX_HEADS], neg_cumT[:, tt * P:(tt + 1) * P],
                                           ident[0:FOX_HEADS, 0:FOX_HEADS])
                    ins.then_inc(S["cum_turned"], 1)

                def o_block(n):
                    pe.wait_ge(S["o_bank_free"], o_before[i] + n + 2)
                    rows_block(b + 3 * GROUPS + n, o_high[:, 2 * n:2 * n + 2, :], o_low[:, 2 * n:2 * n + 2, :],
                               n == 0, n == GROUPS - 1)

                group(0)
                with pe.Fori(0, GROUPS - 1) as u:
                    group(1, u)
                g = GROUPS - 1
                head_scores(0, g, 0)
                head_scores(1, g, 0)
                pe.wait_ge(S["v_ready"], 4 * a + GROUPS)
                o_block(0)
                turn(0, g, 0)
                if fox:
                    turn(1, g, 0)
                head_scores(2, g, 0)
                head_scores(3, g, 0)
                o_block(1)
                values(0, g, 0)
                if fox:
                    values(1, g, 0)
                    turn(2, g, 0)
                    turn(3, g, 0)
                else:
                    turn(1, g, 0)
                o_block(2)
                if fox:
                    values(2, g, 0)
                    values(3, g, 0)
                else:
                    values(1, g, 0)
                    o_sums(g, 0)
                o_block(GROUPS - 1)

            def conv(i):
                b = starts[i]
                for j in range(2 * GROUPS):
                    if j == 0:
                        first_block(i, bank[0])
                        continue
                    wait_block(b + j)
                    if j >= 4:
                        pe.wait_ge(S["conv_g_ready" if j % 2 else "conv_a_ready"], j // 2 - 1)
                    columns_half(bank[j % 4], b + j, 0)
                    columns_half(bank[j % 4], b + j, 1).then_inc(S["block_done"], 1)
                pe.wait_ge(S["u_ready"], 2 * GROUPS)
                for n, t in enumerate(PE_TILES):
                    for half, (k0, taps) in enumerate(TAP_HALVES):
                        pe.wait_ge(S["diagonals_ready"], 2 * n + half + 1)
                        for k in range(taps):
                            at = half * 2048 + k * P
                            ins = pe.matmul(bank[4 + n][:, 0:SEQ], wide[:, at:at + P], u_pad[:, t, k0 + k:k0 + k + SEQ],
                                            start=k0 + k == 0, stop=k0 + k == TAPS - 1)
                        ins.then_inc(S["diagonals_used"], 1)
                order = PE_TILES + tuple(t for t in range(KT) if t not in PE_TILES)
                pe.wait_ge(S["tile_convolved"], len(PE_TILES))
                for k, t in enumerate(order):
                    if k == len(PE_TILES):
                        pe.wait_ge(S["tap_done"], DVE_TAPS)
                    ins = pe.matmul(bank[7][:, 0:SEQ], ones[:, :], y_conv[:, t, :], start=k == 0, stop=k == KT - 1)
                ins.then_inc(S["mean_done"], 1)
                for k in range(KT):
                    pe.wait_ge(S["centred_sq"], k // 2 + 1)
                    ins = pe.matmul(bank[5][:, 0:SEQ], ones[:, :], ln_work[:, k, :], start=k == 0, stop=k == KT - 1)
                ins.then_inc(S["var_done"], 1)
                for n in range(GROUPS):
                    pe.wait_ge(S["o_bank_free"], o_before[i] + n + 2)
                    rows_block(b + 2 * GROUPS + n, o_high[:, 2 * n:2 * n + 2, :], o_low[:, 2 * n:2 * n + 2, :],
                               n == 0, n == GROUPS - 1)

            pe.wait_ge(S["pool_consts"], N_POOL_CONSTS)
            pe.wait_ge(S["dve_consts"], DVE_CONSTS)
            pe.wait_ge(S["vec_loaded"], 16 * 19)
            at = 0
            for n, rows in enumerate((96, 48, 124, 124)):
                pe.transpose(bank[6][:, at:at + rows], vec_rows[0:rows, n, :], ident[0:rows, 0:rows])
                at += rows
            pe.transpose(bank[6][:, at:at + 7], head_rows[:, :], ident[0:7, 0:7]).then_inc(S["vec_turned"], 1)
            pe.wait_ge(S["const_loaded"], 96)
            for r in range(3):
                pe.matmul(bank[5][:, r:r + 1], rope_rows[:, r, :], ones[0:1, 0:1], start=True, stop=True)
            pe.transpose(bank[5][0:FOX_HEADS, 32:34], fox_bias_rows[:, :], ident[0:2, 0:2])
            pe.matmul(bank[5][:, 256:512], ones[0:1, :], pos_row[:, :], start=True, stop=True
                      ).then_inc(S["small_done"], 1)
            pe.wait_ge(S["x_loaded"], 32)
            for T in range(4):
                for m in range(2):
                    for tt in range(2):
                        t = 2 * T + m
                        ins = pe.transpose(bank[T][:, m * SEQ + tt * P:m * SEQ + (tt + 1) * P],
                                           by_token[tt][:, t * P:(t + 1) * P], ident[:, :])
                ins.then_inc(S["x_turned"], 1)
            pe.wait_ge(S["lam_step"], 5)
            pe.matmul(bank[4][:, 0:1], ones[0:1, :], neg_lam_row[:, :], start=True, stop=True
                      ).then_inc(S["small_done"], 1)
            for i, kind in enumerate(phases):
                {"ffn": ffn, "fox": attention, "diff": attention, "conv": conv}[kind](i)
            pe.wait_ge(S["x_ready"], 4 * len(phases) + 4)
            for tt in range(2):
                for m in range(2):
                    for t in range(4):
                        ins = pe.transpose(bank[4 + 2 * tt + m][:, t * P:(t + 1) * P],
                                           xT[:, 4 * m + t, tt * P:(tt + 1) * P], ident[:, :])
                    ins.then_inc(S["final_turned"], 1)


INPUTS = [
    "x", "positions", "norm_ffn1", "norm_mix", "norm_ffn2", "ffn1_w_gate", "ffn1_w_up", "ffn1_w_down",
    "ffn2_w_gate", "ffn2_w_up", "ffn2_w_down", "fox_w_in", "fox_b_f", "fox_q_gain", "fox_k_gain", "fox_w_out",
    "conv_w_pw1", "conv_b_pw1", "conv_w_dw", "conv_b_dw", "conv_ln_g", "conv_ln_b", "conv_w_pw2", "conv_b_pw2",
    "diff_w_in", "diff_q_gain", "diff_k_gain", "diff_lambda_q1", "diff_lambda_k1", "diff_lambda_q2",
    "diff_lambda_k2", "diff_sub_gain", "diff_w_out",
]


def kernel(**inputs):
    import numpy as np
    import concourse.bacc as bacc
    from concourse.bass_utils import run_bass_kernel_spmd

    nc = bacc.Bacc("TRN2", target_bir_lowering=False, num_devices=1)
    arrays, aps = {}, {}
    for name in INPUTS:
        a = np.ascontiguousarray(inputs[name])
        arrays[f"in_{name}"] = a
        aps[name] = nc.dram_tensor(f"in_{name}", a.shape, mybir.dt.from_np(a.dtype), kind="ExternalInput").ap()
    out = nc.dram_tensor("trunk_out", (1, SEQ, D), F32, kind="ExternalOutput").ap()
    build_trunk(nc, aps, out)
    r = run_bass_kernel_spmd(nc, [arrays], core_ids=[0])
    return r.results[0]["trunk_out"]
```

```python
import math
from contextlib import ExitStack

import concourse.bass as bass
from concourse import mybir

F32 = mybir.dt.float32
F32R = mybir.dt.float32r
I32 = mybir.dt.int32
BF16 = mybir.dt.bfloat16
ALU = mybir.AluOpType
ACT = mybir.ActivationFunctionType
AX = mybir.AxisListType

P = 128
DEPTH = 4
SEQ = 256
D = 1024
KT = D // P
D_FF = ((8 * D // 3 + 127) // 128) * 128
PAIRS = D_FF // 256
HEAD = 64
FOX_HEADS = D // HEAD
GROUPS = D // 256
TAPS = 31
ROT = HEAD // 4
ROPE_THETA = 500000.0
EPS = 1e-6
PE_BANK = {4: 7, 5: 4, 6: 5, 7: 6}
SHARED, SHARED_TAPS = 4, 26
TAP_CHUNKS = [(t, k0, n) for t in PE_BANK
              for k0, n in ((0, 16), (16, (SHARED_TAPS if t == SHARED else TAPS) - 16))]
RING = 3
MASKED = -1e30
ROUND = 1.5 * 2.0 ** 23
TWO_PI_1, TWO_PI_2 = 6.28125, 1.9350051879882812e-3
TWO_PI_3 = 2.0 * math.pi - TWO_PI_1 - TWO_PI_2

MIXERS = ["fox", "conv", "diff"]
PHASES = [k for i in range(DEPTH) for k in ("ffn", MIXERS[i % 3], "ffn")]
BLOCKS = {"ffn": 3 * PAIRS, "fox": 4 * GROUPS, "conv": 3 * GROUPS, "diff": 4 * GROUPS}

NORM_COL = 0
PW1_COL = NORM_COL + 3 * DEPTH * KT
DW_B_COL = PW1_COL + 16
LN_G_COL = DW_B_COL + KT
LN_B_COL = LN_G_COL + KT
PW2_COL = LN_B_COL + KT
HEAD_COL = PW2_COL + KT
DW_COL = HEAD_COL + 7
VEC_COLS = DW_COL + TAPS * KT


def build_trunk(nc, A, out):
    phases = PHASES
    starts = [sum(BLOCKS[k] for k in phases[:i]) for i in range(len(phases) + 1)]
    n_blocks = starts[-1]

    def number(i):
        family = {"ffn": ("ffn",), "fox": ("fox", "diff"), "diff": ("fox", "diff"), "conv": ("conv",)}[phases[i]]
        return sum(k in family for k in phases[:i])

    def layer_of(i):
        return i // 3

    with ExitStack() as ctx:
        def sb(name, shape, dt=F32):
            return ctx.enter_context(nc.sbuf_tensor("sb_" + name, shape, dt))

        def sem(name):
            return ctx.enter_context(nc.semaphore(name))

        raw = [sb(f"raw{i}", [P, 2048]) for i in range(RING)]
        w_high = [sb(f"w_high{i}", [P, 2048], F32R) for i in range(RING)]
        w_low = [sb(f"w_low{i}", [P, 2048], F32R) for i in range(RING)]

        xT = sb("xT", [P, KT, SEQ])
        x_square = sb("x_square", [P, KT, SEQ])
        x_high = sb("x_high", [P, KT, SEQ], F32R)
        x_low = sb("x_low", [P, KT, SEQ], F32R)
        square_sum = sb("square_sum", [P, SEQ])
        square_pair = sb("square_pair", [P, SEQ])
        root = sb("root", [P, SEQ + 2])
        inv_rms = sb("inv_rms", [P, SEQ + 2])

        gate_in = sb("gate_in", [P, 512])
        gate_silu = sb("gate_silu", [P, 512])
        gate_scaled = sb("gate_scaled", [P, 512])
        hidden = sb("hidden", [P, 512])
        h_high = [sb(f"h_high{i}", [P, 512], F32R) for i in range(2)]
        h_low = [sb(f"h_low{i}", [P, 512], F32R) for i in range(2)]

        q_raw, k_raw = sb("q_raw", [P, 512]), gate_scaled
        q_square, k_square = sb("q_square", [P, 512]), sb("k_square", [P, 512])
        q_inv, k_inv = sb("q_inv", [P, 512]), sb("k_inv", [P, 512])
        qT, kT = sb("qT", [P, 512]), sb("kT", [P, 512])
        v_nat = sb("v_nat", [P, 2, 256])
        scores = [sb(f"scores{i}", [P, 384]) for i in range(2)]
        probsT = [sb(f"probsT{i}", [P, 384]) for i in range(2)]
        neg_max = [sb(f"neg_max{i}", [P, 2]) for i in range(2)]
        row_sum = [sb(f"row_sum{i}", [P, 2]) for i in range(2)]
        inv_sum = [sb(f"inv_sum{i}", [P, 2]) for i in range(2)]
        o_copy, o_square, o_normal = hidden, gate_in, gate_silu
        o_inv = sb("o_inv", [P, 512])
        lam_inv_sum = sb("lam_inv_sum", [P, 2])
        o_high = sb("o_high", [P, KT, SEQ], F32R)
        o_low = sb("o_low", [P, KT, SEQ], F32R)
        gate_w = sb("gate_w", [P, KT, FOX_HEADS])
        gate_w_gained = sb("gate_w_gained", [P, KT, FOX_HEADS])
        logit = sb("logit", [FOX_HEADS, SEQ])
        logit_min = sb("logit_min", [FOX_HEADS, SEQ])
        logit_log = sb("logit_log", [FOX_HEADS, SEQ])
        neg_cumT = sb("neg_cumT", [FOX_HEADS, SEQ])
        neg_cum_q = sb("neg_cum_q", [P, 2 * FOX_HEADS])
        cum_part = sb("cum_part", [FOX_HEADS, SEQ], BF16)
        cum_parts = sb("cum_parts", [P, SEQ], BF16)
        head_of_row = sb("head_of_row", [P, FOX_HEADS], BF16)
        ones_bf = sb("ones_bf", [P, P], BF16)
        wide = sb("wide", [P, 4096])
        neg_cum_wide = wide[:, 0:FOX_HEADS * SEQ // 2].bitcast(BF16)
        neg_cum_heads = neg_cum_wide.rearrange("p (h n) -> p h n", h=FOX_HEADS)
        by_token = [wide[:, tt * D:(tt + 1) * D] for tt in range(2)]
        u_pad = sb("u_pad", [P, KT, TAPS - 1 + SEQ])
        y_conv = x_square
        ln_work = u_pad[:, :, TAPS - 1:]
        ln_inv = q_raw[:, 0:SEQ]

        ident = sb("ident", [P, P])
        ones = sb("ones", [P, P])
        ones_heads = sb("ones_heads", [P, P])
        upper = sb("upper", [P, P])
        causal = sb("causal", [P, 384])
        chunked = sb("chunked", [P, 384])
        swap = sb("swap", [P, P])
        vec = sb("vec", [P, VEC_COLS])
        vec_rows = kT[:, :].rearrange("p (a n) -> p a n", a=4)
        head_rows = q_raw[0:7, 0:P]
        eps = sb("eps", [P, 1])
        half_pi = sb("half_pi", [P, 1])
        rope_rows = sb("rope_rows", [1, 3, P])
        rope_cols = sb("rope_cols", [P, 3])
        not_rotated = sb("not_rotated", [P, 1])
        pos_int = qT[:, 0:SEQ].bitcast(I32)
        pos = qT[:, SEQ:2 * SEQ]
        angle, turns = q_inv[:, 0:SEQ], k_inv[:, 0:SEQ]
        cosT, sinT = sb("cosT", [P, SEQ]), sb("sinT", [P, SEQ])
        fox_bias_rows = sb("fox_bias_rows", [2, FOX_HEADS])
        fox_bias = sb("fox_bias", [FOX_HEADS, 2])
        lam_rows = k_square[:, 0:4 * HEAD].rearrange("p (a n) -> p a n", a=4)
        lam_products = k_square[:, 4 * HEAD:6 * HEAD].rearrange("p (a n) -> p a n", a=2)
        lam_sums = sb("lam_sums", [P, 2])
        lam_exps = sb("lam_exps", [P, 2])
        lam_gap = sb("lam_gap", [P, 1])
        neg_lam = sb("neg_lam", [P, 1])

        bank = [ctx.enter_context(nc.psum_tensor(f"bank{i}", [P, 512], F32)) for i in range(8)]

        names = (
            "x_loaded norm_loaded vec_loaded const_loaded pool_consts dve_consts out_stored "
            "block_done out_bank_done sumsq_done high_ready low_ready "
            "x_ready xhigh_ready xsq_ready xlow_ready root_ready inv_rms_ready "
            "gate_in_ready silu_ready gate_scaled_ready hidden_ready h_high_ready h_low_ready "
            "x_turned norm_turned norm_copied vec_turned vec_copied rope_step act_rope_step lam_step "
            "q_raw_ready k_raw_ready q_sq_ready k_sq_ready q_log_ready k_log_ready q_inv_ready k_inv_ready "
            "q_sum_done k_sum_done q_normed k_normed q_swapped k_swapped q_cos q_sin k_cos k_sin "
            "q_ready k_ready v_ready scores_done score_added masked exp_ready "
            "inv_sum_ready probs_ready probs_half probs_turned probsT_ready pv_done o_high_ready o_bank_free "
            "o_copied o_sq_ready o_sum_done o_log_ready o_inv_ready o_normed lam_scaled "
            "gate_w_loaded gate_w_ready logits_done logit_ready logit_parts logit_min_ready "
            "cum_turned cum_q_ready neg_cumT_ready neg_cum_ready "
            "conv_a_ready conv_g_ready sigmoid_ready u_ready tap_done mean_done centred centred_sq var_done "
            "ln_root_ready ln_inv_ready ln_scaled ln_silu "
            "final_turned token_tile_0_copied token_tile_1_copied square_folded "
            "diagonals_ready diagonals_used tile_convolved cum_split_step cum_parts_ready"
        ).split()
        S = {n: sem(n) for n in names}
        raw_landed = [sem(f"raw_landed{i}") for i in range(RING)]

        def rows_of(v):
            return v.rearrange("a (t p) -> (a t) p", p=P)

        def raw_uses(b, u=0, per=0):
            return 16 * (b // RING + 1) + u * (16 * per // RING)

        def pair(t):
            return t.rearrange("p (a n) -> p a n", a=2)

        def over_tokens(row, n=2):
            return row.unsqueeze(1).broadcast_to([P, n, SEQ])

        fox_scale = HEAD ** -0.5
        lambda_init = 0.8 - 0.6 * math.exp(-0.3 * 2)

        def norm_bank(x, j, fox):
            return bank[4 if x == "k" and j == 0 and not fox else 3]

        ROPE_AT, BIAS_AT, NORM_AT = 304, 308, 320
        N_POOL_CONSTS = 15
        DVE_CONSTS = 24
        DVE_TAPS = TAPS * SHARED + TAPS - SHARED_TAPS
        turned_before = [sum({"fox": FOX_HEADS, "diff": FOX_HEADS // 2}.get(k, 0) for k in phases[:i])
                         for i in range(len(phases))]
        o_before = [GROUPS * sum(k != "ffn" for k in phases[:i]) for i in range(len(phases))]

        block = ctx.enter_context(nc.Block())

        @block.sync
        def _(sp):
            def load(b, src, u=0, per=0):
                if b >= RING or not isinstance(u, int):
                    sp.wait_ge(S["low_ready"], b - RING + 1 + u * per)
                dst = raw[b % RING][:, :].rearrange("p (k n) -> p k n", k=src.shape[1])
                sp.dma_start(dst, src).then_inc(raw_landed[b % RING], 16)

            def columns(w, at):
                return w[:, bass.ds(at, 256)].rearrange("(k p) n -> p k n", p=P)

            def rows(w, at):
                return w[bass.ds(at, 256), :].rearrange("(f p) n -> p f n", p=P)

            def small_loads():
                at = 0
                for name in ("conv_b_pw1", "conv_b_dw", "conv_ln_g", "conv_ln_b", "conv_b_pw2"):
                    n = 16 if name == "conv_b_pw1" else 8
                    sp.dma_start(vec_rows[at:at + n, 1, :], rows_of(A[name])).then_inc(S["vec_loaded"], 16)
                    at += n
                taps = rows_of(A["conv_w_dw"][0])
                for half in range(2):
                    sp.dma_start(vec_rows[0:124, 2 + half, :], taps[124 * half:124 * half + 124, :]
                                  ).then_inc(S["vec_loaded"], 16)
                r = 0
                for name, n in (("fox_q_gain", 2), ("fox_k_gain", 2), ("diff_q_gain", 1), ("diff_k_gain", 1)):
                    for half in range(2):
                        sp.dma_start(head_rows[r:r + n, HEAD * half:HEAD * half + HEAD], A[name]
                                      ).then_inc(S["vec_loaded"], 16)
                    r += n
                sp.dma_start(head_rows[6:7, :], A["diff_sub_gain"]).then_inc(S["vec_loaded"], 16)
                sp.dma_start(pos_int, A["positions"].broadcast_to([P, SEQ])).then_inc(S["const_loaded"], 16)
                sp.dma_start(fox_bias_rows[:, :], A["fox_b_f"]).then_inc(S["const_loaded"], 16)
                for m, name in enumerate(("q1", "k1", "q2", "k2")):
                    sp.dma_start(lam_rows[:, m, :], A["diff_lambda_" + name].broadcast_to([P, HEAD])
                                  ).then_inc(S["const_loaded"], 16)

            for tt in range(2):
                sp.dma_start(by_token[tt], A["x"][0, tt * P:(tt + 1) * P, :]).then_inc(S["x_loaded"], 16)

            for i, kind in enumerate(phases):
                b, n, layer = starts[i], number(i), layer_of(i)
                if kind == "ffn":
                    which = "ffn1" if i % 3 == 0 else "ffn2"
                    wg, wu, wd = (A[f"{which}_w_{m}"][layer] for m in ("gate", "up", "down"))
                    def two_pairs(u):
                        for q in range(2):
                            at = u * 512 + (q + 1) * 256
                            load(b + 2 + 3 * q, columns(wg, at), u, 6)
                            load(b + 3 + 3 * q, columns(wu, at), u, 6)
                            load(b + 4 + 3 * q, rows(wd, at - 256), u, 6)

                    load(b, columns(wg, 0))
                    load(b + 1, columns(wu, 0))
                    if i == 0:
                        small_loads()
                    two_pairs(0)
                    with sp.Fori(1, (PAIRS - 1) // 2) as u:
                        two_pairs(u)
                    load(b + 3 * PAIRS - 1, rows(wd, (PAIRS - 1) * 256))
                elif kind == "conv":
                    for j in range(GROUPS):
                        load(b + 2 * j, columns(A["conv_w_pw1"][0], 256 * j))
                        load(b + 2 * j + 1, columns(A["conv_w_pw1"][0], D + 256 * j))
                    for j in range(GROUPS):
                        load(b + 2 * GROUPS + j, rows(A["conv_w_pw2"][0], 256 * j))
                else:
                    which = layer // 3
                    w_in, w_out = A[kind + "_w_in"][which], A[kind + "_w_out"][which]
                    if kind == "fox":
                        if n:
                            sp.wait_ge(S["gate_w_ready"], which)
                        sp.dma_start(gate_w[:, :, :],
                                     w_in[:, 3 * D:3 * D + FOX_HEADS].rearrange("(k p) n -> p k n", p=P)
                                     ).then_inc(S["gate_w_loaded"], 16)
                    for part in range(3):
                        load(b + part, columns(w_in, part * D))
                    with sp.Fori(0, GROUPS - 1) as u:
                        for part in range(3):
                            load(b + 3 + part, columns(w_in, u * 256 + part * D + 256), u, 3)
                    for j in range(GROUPS):
                        load(b + 3 * GROUPS + j, rows(w_out, 256 * j))
            for m in range(2):
                for tt in range(2):
                    sp.wait_ge(S["token_tile_1_copied" if tt else "token_tile_0_copied"], m + 1)
                    cols = slice(m * 512, (m + 1) * 512)
                    sp.dma_start(out[0, tt * P:(tt + 1) * P, cols], by_token[tt][:, cols]
                                 ).then_inc(S["out_stored"], 16)
            sp.wait_ge(S["out_stored"], 64)

        @block.gpsimd
        def _(pool):
            zero = [ident, ones_heads, swap, causal, chunked]
            for t in zero:
                pool.memset(t[:, :], 0.0).then_inc(S["pool_consts"], 1)
            pool.memset(ones[:, :], 1.0).then_inc(S["pool_consts"], 1)
            pool.memset(u_pad[:, :, 0:TAPS - 1], 0.0).then_inc(S["pool_consts"], 1)
            pool.wait_ge(S["pool_consts"], 7)
            pool.affine_select(out=ident[:, :], in_=ident[:, :], compare_op=ALU.not_equal, fill=1.0, base=0,
                               pattern=[[-1, P]], channel_multiplier=1).then_inc(S["pool_consts"], 1)
            pool.affine_select(out=upper[:, :], in_=ones[:, :], compare_op=ALU.is_ge, fill=0.0, base=0,
                               pattern=[[1, P]], channel_multiplier=-1).then_inc(S["pool_consts"], 1)
            done = 9
            for at in (0, 256):
                pool.affine_select(out=causal[:, at:at + P], in_=causal[:, at:at + P], compare_op=ALU.is_ge,
                                   fill=MASKED, base=0, pattern=[[-1, P]],
                                   channel_multiplier=1).then_inc(S["pool_consts"], 1)
                pool.wait_ge(S["pool_consts"], done + 1)
                pool.memset(chunked[0:HEAD, at + HEAD:at + P], MASKED).then_inc(S["pool_consts"], 1)
                pool.wait_ge(S["pool_consts"], done + 2)
                done += 2
            for m in range(2):
                r = slice(HEAD * m, HEAD * m + HEAD)
                pool.memset(ones_heads[r, r], 1.0).then_inc(S["pool_consts"], 1)
                pool.wait_ge(S["pool_consts"], done + 1 + m)
            def fold_squares(i):
                c, total, two = 7 * i, square_sum[:, :], square_pair[:, :]

                def add(dst, a, b):
                    pool.tensor_tensor(dst, a, b, ALU.add).then_inc(S["square_folded"], 1)

                pool.wait_ge(S["xsq_ready"], 4 * i + 1)
                if i:
                    pool.wait_ge(S["sumsq_done"], i)
                add(total, x_square[:, 0, :], x_square[:, 1, :])
                for T in (1, 2, 3):
                    pool.wait_ge(S["xsq_ready"], 4 * i + T + 1)
                    add(two, x_square[:, 2 * T, :], x_square[:, 2 * T + 1, :])
                    pool.wait_ge(S["square_folded"], c + 2 * T)
                    add(total, total, two)
                    if T < 3:
                        pool.wait_ge(S["square_folded"], c + 2 * T + 1)

            def spread_cums(w):
                pool.wait_ge(S["cum_parts_ready"], w + 1)
                shape = [P, 4, SEQ]
                for g in range(GROUPS):
                    heads = slice(4 * g, 4 * g + 4)
                    pool.tensor_tensor(neg_cum_heads[:, heads, :], cum_parts[:, :].unsqueeze(1).broadcast_to(shape),
                                       head_of_row[:, heads].unsqueeze(2).broadcast_to(shape),
                                       ALU.mult).then_inc(S["neg_cum_ready"], 1)

            def diagonals(chunks):
                for n in chunks:
                    t, k0, taps = TAP_CHUNKS[n]
                    if n > 1:
                        pool.wait_ge(S["diagonals_used"], n - 1)
                    col, at, shape = DW_COL + k0 * KT + t, n % 2 * 2048, [P, taps, P]
                    pool.tensor_tensor(wide[:, at:at + taps * P].rearrange("p (k c) -> p k c", c=P),
                                       ident[:, :].unsqueeze(1).broadcast_to(shape),
                                       vec[:, col:col + (taps - 1) * KT + 1:KT].unsqueeze(2).broadcast_to(shape),
                                       ALU.mult).then_inc(S["diagonals_ready"], 1)

            for i, kind in enumerate(phases):
                fold_squares(i)
                if kind == "fox":
                    spread_cums(i // 9)
                elif kind == "conv":
                    diagonals(range(2, len(TAP_CHUNKS)))
                if i + 1 < len(phases) and phases[i + 1] == "conv":
                    pool.wait_ge(S["vec_copied"], 7)
                    pool.wait_ge(S["block_done"], starts[i])
                    diagonals(range(2))


        @block.scalar
        def _(act):
            act.preload_act_table_set("sqrt_and_others")
            for kind, name in enumerate(("norm_ffn1", "norm_mix", "norm_ffn2")):
                act.dma_start(vec_rows[32 * kind:32 * kind + 32, 0, :], rows_of(A[name])).then_inc(S["norm_loaded"], 16)

            def split_high(b, u=0, per=0):
                if b >= n_blocks:
                    return
                act.wait_ge(raw_landed[b % RING], raw_uses(b, u, per))
                if b >= RING:
                    act.wait_ge(S["block_done"], b - RING + 1 + u * per)
                act.activation(w_high[b % RING][:, :], raw[b % RING][:, :], ACT.Copy).then_inc(S["high_ready"], 1)

            def boundary(i):
                col = NORM_COL + (i % 3) * DEPTH * KT + layer_of(i) * KT
                def high(T):
                    act.wait_ge(S["x_ready"], 4 * i + T + 1)
                    for t in (2 * T, 2 * T + 1):
                        act.activation(x_high[:, t, :], xT[:, t, :], ACT.Copy, scale=vec[:, col + t:col + t + 1]
                                       ).then_inc(S["xhigh_ready"], 1)

                def square(T):
                    act.activation(x_square[:, 2 * T:2 * T + 2, :], xT[:, 2 * T:2 * T + 2, :], ACT.Square
                                   ).then_inc(S["xsq_ready"], 1)

                if i == 0:
                    act.wait_ge(S["norm_copied"], 1)
                    for T in range(4):
                        high(T)
                    split_high(0)
                    for T in range(4):
                        square(T)
                    split_high(1)
                else:
                    split_high(starts[i] + 1)
                    for T in range(4):
                        high(T)
                        square(T)
                width = SEQ + 2 if phases[i] in ("fox", "diff") else SEQ
                act.wait_ge(S["sumsq_done"], i + 1)
                if i:
                    act.wait_ge(S["inv_rms_ready"], i)
                act.activation(root[:, 0:width], bank[7][:, 0:width], ACT.Sqrt, scale=1.0 / D, bias=eps[:, :]
                               ).then_inc(S["root_ready"], 1)

            def tables():
                act.wait_ge(S["lam_step"], 2)
                act.activation(lam_exps[:, :], lam_sums[:, :], ACT.Exp).then_inc(S["lam_step"], 1)
                act.wait_ge(S["rope_step"], 9)
                act.activation(sinT[:, :], angle[:, :], ACT.Sin).then_inc(S["act_rope_step"], 1)
                act.activation(turns[:, :], angle[:, :], ACT.Abs).then_inc(S["act_rope_step"], 1)
                act.wait_ge(S["act_rope_step"], 2)
                act.activation(cosT[:, :], turns[:, :], ACT.Sin, scale=-1.0, bias=half_pi[:, :]
                               ).then_inc(S["act_rope_step"], 1)

            def ffn(i):
                b, f = starts[i], number(i)

                def silu(p, u=0):
                    act.wait_ge(S["gate_in_ready"], PAIRS * f + p + 1 + 2 * u)
                    act.activation(gate_silu[:, :], gate_in[:, :], ACT.Silu).then_inc(S["silu_ready"], 1)

                def high(p, u=0):
                    act.wait_ge(S["hidden_ready"], PAIRS * f + p + 1 + 2 * u)
                    act.activation(h_high[p % 2][:, :], hidden[:, :], ACT.Copy).then_inc(S["h_high_ready"], 1)

                def one_pair(p, u=0):
                    split_high(b + 3 * p + 1, u, 6)
                    silu(p, u)
                    split_high(b + 3 * p + 2, u, 6)
                    high(p, u)
                    split_high(b + 3 * p + 3, u, 6)

                split_high(b + 2)
                silu(0)
                split_high(b + 3)
                high(0)
                last = i == len(phases) - 1
                with act.Fori(0, (PAIRS - 1) // 2 - last) as u:
                    one_pair(1, u)
                    one_pair(2, u)
                if last:
                    one_pair(PAIRS - 2)
                    one_pair(PAIRS - 1)
                if i == 0:
                    tables()

            def attention(i):
                a, b, fox = number(i), starts[i], phases[i] == "fox"
                w = i // 9

                def inverse(x, g, u):
                    buf, n = {"q": (q_inv, HEAD), "k": (k_inv, HEAD), "o": (o_inv, P)}[x]
                    src = bank[6] if x == "o" else norm_bank(x, g, fox)
                    c = (0 if x == "o" else 4 * a) + g + u + 1
                    act.wait_ge(S[x + "_sum_done"], c)
                    act.activation(buf[:, :], src[:, :], ACT.Ln, scale=1.0 / n, bias=eps[:, :]
                                   ).then_inc(S[x + "_log_ready"], 1)
                    act.wait_ge(S[x + "_log_ready"], c)
                    act.activation(buf[:, :], buf[:, :], ACT.Exp, scale=-0.5).then_inc(S[x + "_inv_ready"], 1)

                def square(x, g, u):
                    src, dst = {"q": (q_raw, q_square), "k": (k_raw, k_square)}[x]
                    act.wait_ge(S[x + "_raw_ready"], 4 * a + g + u + 1)
                    act.activation(dst[:, :], src[:, :], ACT.Square).then_inc(S[x + "_sq_ready"], 1)

                def exps(m, g, u):
                    c = 16 * a + 4 * g + m + 4 * u
                    act.wait_ge(S["masked"], c + 1)
                    s = scores[m % 2]
                    for qb, cols in enumerate((slice(0, P), slice(P, 384))):
                        act.activation(s[:, cols], s[:, cols], ACT.Exp, bias=neg_max[m % 2][:, qb:qb + 1],
                                       accum_out=row_sum[m % 2][:, qb:qb + 1]).then_inc(S["exp_ready"], 1)

                def softplus():
                    steps = ((logit, ACT.Abs, 1.0, fox_bias[:, w:w + 1]), (logit_log, ACT.Exp, -1.0, 0.0),
                             (logit_log, ACT.Ln, 1.0, ones[0:FOX_HEADS, 0:1]))
                    act.wait_ge(S["logit_ready"], w + 1)
                    for n, (src, f, scale, bias) in enumerate(steps):
                        if n:
                            act.wait_ge(S["logit_parts"], 3 * w + n)
                        act.activation(logit_log[:, :], src[:, :], f, scale=scale, bias=bias
                                       ).then_inc(S["logit_parts"], 1)

                def copy_probs(m, g, u):
                    per = 4 if fox else 2
                    c = turned_before[i] + per * g + m + per * u
                    act.wait_ge(S["probs_turned"], c + 1)
                    src = bank[([6, 5, 6, 4] if fox else [6, 6])[m]]
                    act.activation(probsT[m % 2][:, :], src[:, 0:384], ACT.Copy).then_inc(S["probsT_ready"], 1)

                def o_squares(g, u):
                    act.wait_ge(S["pv_done"], turned_before[i] + 2 * (g + u + 1))
                    act.activation(o_copy[:, :], bank[7][:, :], ACT.Copy).then_inc(S["o_copied"], 1)
                    act.activation(o_square[:, :], bank[7][:, :], ACT.Square).then_inc(S["o_sq_ready"], 1)

                def o_part(g, u):
                    if fox:
                        act.wait_ge(S["pv_done"], turned_before[i] + 4 * (g + u + 1))
                        src = bank[7]
                    else:
                        act.wait_ge(S["o_normed"], g + u + 1)
                        src = o_normal
                    act.activation(o_high[:, bass.ds(2 * (g + u), 2), :], pair(src[:, :]), ACT.Copy
                                   ).then_inc(S["o_high_ready"], 1)

                def fox_group(j, u=0):
                    g = j - 1
                    split_high(b + 3 * j + 2, u, 3)
                    if not j:
                        softplus()
                    square("q", j, u)
                    if j:
                        exps(0, g, u)
                        exps(1, g, u)
                    split_high(b + 3 * j + 3, u, 3)
                    if j:
                        copy_probs(0, g, u)
                        copy_probs(1, g, u)
                        exps(2, g, u)
                    square("k", j, u)
                    inverse("q", j, u)
                    if j:
                        exps(3, g, u)
                    split_high(b + 3 * j + 4, u, 3)
                    inverse("k", j, u)
                    if j:
                        copy_probs(2, g, u)
                        copy_probs(3, g, u)
                        o_part(g, u)

                def diff_group(j, u=0):
                    g = j - 1
                    if j > 1:
                        o_squares(g - 1, u)
                    split_high(b + 3 * j + 2, u, 3)
                    if j > 1:
                        inverse("o", g - 1, u)
                    square("q", j, u)
                    if j > 1:
                        o_part(g - 1, u)
                    if j:
                        exps(0, g, u)
                    inverse("q", j, u)
                    if j:
                        exps(1, g, u)
                        split_high(b + 3 * j + 3, u, 3)
                        copy_probs(0, g, u)
                        square("k", j, u)
                        split_high(b + 3 * j + 4, u, 3)
                        exps(2, g, u)
                        exps(3, g, u)
                        inverse("k", j, u)
                        copy_probs(1, g, u)
                    else:
                        square("k", j, u)
                        split_high(b + 3)
                        inverse("k", j, u)
                        split_high(b + 4)

                act.preload_act_table_set("natural_log_exp_and_others")
                g = GROUPS - 1
                e = b + 3 * GROUPS
                if fox:
                    fox_group(0)
                    with act.Fori(0, GROUPS - 1) as u:
                        fox_group(1, u)
                    exps(0, g, 0)
                    exps(1, g, 0)
                    split_high(e + 2)
                    copy_probs(0, g, 0)
                    copy_probs(1, g, 0)
                    exps(2, g, 0)
                    exps(3, g, 0)
                    split_high(e + 3)
                    copy_probs(2, g, 0)
                    copy_probs(3, g, 0)
                    split_high(e + 4)
                    o_part(g, 0)
                else:
                    diff_group(0)
                    diff_group(1)
                    with act.Fori(0, GROUPS - 2) as u:
                        diff_group(2, u)
                    o_squares(g - 1, 0)
                    exps(0, g, 0)
                    inverse("o", g - 1, 0)
                    exps(1, g, 0)
                    o_part(g - 1, 0)
                    split_high(e + 2)
                    copy_probs(0, g, 0)
                    exps(2, g, 0)
                    exps(3, g, 0)
                    split_high(e + 3)
                    copy_probs(1, g, 0)
                    split_high(e + 4)
                    o_squares(g, 0)
                    inverse("o", g, 0)
                    o_part(g, 0)

            def conv(i):
                b = starts[i]
                for j in range(GROUPS):
                    split_high(b + 2 * j + 2)
                    split_high(b + 2 * j + 3)
                    act.wait_ge(S["conv_g_ready"], j + 1)
                    for m in range(2):
                        col = PW1_COL + KT + 2 * j + m
                        act.activation(gate_silu[:, m * SEQ:(m + 1) * SEQ], gate_scaled[:, m * SEQ:(m + 1) * SEQ],
                                       ACT.Sigmoid, bias=vec[:, col:col + 1]).then_inc(S["sigmoid_ready"], 1)
                split_high(b + 2 * GROUPS + 2)
                for n, (t, at) in enumerate(PE_BANK.items()):
                    act.wait_ge(S["diagonals_used"], 2 * n + 2)
                    act.activation(y_conv[:, t, :], bank[at][:, 0:SEQ], ACT.Identity,
                                   bias=vec[:, DW_B_COL + t:DW_B_COL + t + 1]).then_inc(S["tile_convolved"], 1)
                for T in range(4):
                    act.wait_ge(S["centred"], T + 1)
                    act.activation(ln_work[:, 2 * T:2 * T + 2, :], y_conv[:, 2 * T:2 * T + 2, :], ACT.Square
                                   ).then_inc(S["centred_sq"], 1)
                act.wait_ge(S["var_done"], 1)
                act.activation(root[:, 0:SEQ], bank[5][:, 0:SEQ], ACT.Sqrt, scale=1.0 / D, bias=eps[:, :]
                               ).then_inc(S["ln_root_ready"], 1)
                e = b + 2 * GROUPS
                for T in range(4):
                    act.wait_ge(S["ln_scaled"], T + 1)
                    for t in (2 * T, 2 * T + 1):
                        act.activation(ln_work[:, t, :], y_conv[:, t, :], ACT.Silu,
                                       scale=vec[:, LN_G_COL + t:LN_G_COL + t + 1],
                                       bias=vec[:, LN_B_COL + t:LN_B_COL + t + 1]).then_inc(S["ln_silu"], 1)
                    act.wait_ge(S["ln_silu"], 2 * T + 2)
                    act.activation(o_high[:, 2 * T:2 * T + 2, :], ln_work[:, 2 * T:2 * T + 2, :], ACT.Copy
                                   ).then_inc(S["o_high_ready"], 1)
                for k in range(3, 5):
                    split_high(e + k)

            act.wait_ge(S["pool_consts"], N_POOL_CONSTS)
            act.wait_ge(S["dve_consts"], DVE_CONSTS)
            for i, kind in enumerate(phases):
                boundary(i)
                {"ffn": ffn, "fox": attention, "diff": attention, "conv": conv}[kind](i)
            for m in range(2):
                act.wait_ge(S["final_turned"], 2 * m + 2)
                act.activation(by_token[1][:, m * 512:(m + 1) * 512], bank[6 + m][:, :], ACT.Copy
                               ).then_inc(S["token_tile_1_copied"], 1)

        @block.vector
        def _(dve):
            def split_low(b, u=0, per=0):
                if b >= n_blocks:
                    return
                dve.wait_ge(S["high_ready"], b + 1 + u * per)
                dve.tensor_tensor(w_low[b % RING][:, :], raw[b % RING][:, :], w_high[b % RING][:, :].bitcast(F32),
                                  ALU.subtract).then_inc(S["low_ready"], 1)

            def wait_out_bank(i, T):
                if T < 3:
                    dve.wait_ge(S["out_bank_done"], 3 * (i - 1) + T + 1)
                else:
                    dve.wait_ge(S["block_done"], starts[i])

            def update_x(i, T):
                if i == 0:
                    dve.wait_ge(S["x_turned"], T + 1)
                    dve.tensor_copy(xT[:, 2 * T:2 * T + 2, :], pair(bank[T][:, :])).then_inc(S["x_ready"], 1)
                    return
                wait_out_bank(i, T)
                if phases[i - 1] == "conv":
                    for m in range(2):
                        t = 2 * T + m
                        ins = dve.scalar_tensor_tensor(xT[:, t, :], bank[T][:, m * SEQ:(m + 1) * SEQ],
                                                       vec[:, PW2_COL + t:PW2_COL + t + 1], xT[:, t, :],
                                                       ALU.add, ALU.add)
                    ins.then_inc(S["x_ready"], 1)
                else:
                    weight = 0.5 if phases[i - 1] == "ffn" else 1.0
                    dve.scalar_tensor_tensor(xT[:, 2 * T:2 * T + 2, :], pair(bank[T][:, :]), weight,
                                             xT[:, 2 * T:2 * T + 2, :], ALU.mult, ALU.add).then_inc(S["x_ready"], 1)

            def boundary(i):
                col = NORM_COL + (i % 3) * DEPTH * KT + layer_of(i) * KT

                def low(T):
                    for t in (2 * T, 2 * T + 1):
                        dve.wait_ge(S["xhigh_ready"], 8 * i + t + 1)
                        dve.scalar_tensor_tensor(x_low[:, t, :], xT[:, t, :], vec[:, col + t:col + t + 1],
                                                 x_high[:, t, :].bitcast(F32), ALU.mult, ALU.subtract
                                                 ).then_inc(S["xlow_ready"], 1)

                if phases[i] == "fox":
                    w = i // 9
                    dve.wait_ge(S["gate_w_loaded"], 16 * (w + 1))
                    if w:
                        dve.wait_ge(S["logits_done"], w)
                    dve.tensor_tensor(gate_w_gained[:, :, :], gate_w[:, :, :],
                                      vec[:, col:col + KT].unsqueeze(2).broadcast_to([P, KT, FOX_HEADS]), ALU.mult
                                      ).then_inc(S["gate_w_ready"], 1)
                for T in range(4):
                    update_x(i, T)
                    if T:
                        low(T - 1)
                low(3)
                if i == 0:
                    split_low(0)
                split_low(starts[i] + 1)
                width = SEQ + 2 if phases[i] in ("fox", "diff") else SEQ
                dve.wait_ge(S["root_ready"], i + 1)
                dve.reciprocal(inv_rms[:, 0:width], root[:, 0:width]).then_inc(S["inv_rms_ready"], 1)
                dve.wait_ge(S["inv_rms_ready"], i + 1)

            def before_tables():
                dve.wait_ge(S["const_loaded"], 96)
                dve.tensor_tensor(lam_products, lam_rows[:, 0:4:2, :], lam_rows[:, 1:4:2, :], ALU.mult
                                  ).then_inc(S["lam_step"], 1)
                dve.wait_ge(S["lam_step"], 1)
                dve.tensor_reduce(lam_sums[:, :], lam_products, AX.X, ALU.add).then_inc(S["lam_step"], 1)
                dve.wait_ge(S["vec_turned"], 1)
                dve.tensor_copy(rope_cols[:, :], bank[6][:, ROPE_AT:ROPE_AT + 3]).then_inc(S["rope_step"], 1)
                dve.tensor_copy(pos, pos_int).then_inc(S["rope_step"], 1)
                dve.wait_ge(S["rope_step"], 2)
                dve.tensor_scalar(angle[:, :], pos, rope_cols[:, 0:1], None, ALU.mult).then_inc(S["rope_step"], 1)
                dve.wait_ge(S["rope_step"], 3)
                dve.tensor_scalar(turns[:, :], angle[:, :], 1.0 / (2.0 * math.pi), ROUND, ALU.mult, ALU.add
                                  ).then_inc(S["rope_step"], 1)
                dve.wait_ge(S["rope_step"], 4)
                dve.tensor_scalar(turns[:, :], turns[:, :], ROUND, None, ALU.subtract).then_inc(S["rope_step"], 1)
                for n, part in enumerate((TWO_PI_1, TWO_PI_2, TWO_PI_3)):
                    dve.wait_ge(S["rope_step"], 5 + n)
                    dve.scalar_tensor_tensor(angle[:, :], turns[:, :], -part, angle[:, :], ALU.mult, ALU.add
                                             ).then_inc(S["rope_step"], 1)
                dve.wait_ge(S["rope_step"], 8)
                dve.tensor_scalar(angle[:, :], angle[:, :], math.pi, -math.pi, ALU.min, ALU.max
                                  ).then_inc(S["rope_step"], 1)
                at = 0
                for col, width in ((PW1_COL, 48), (DW_COL, 124), (DW_COL + 124, 124), (HEAD_COL, 7)):
                    dve.tensor_copy(vec[:, col:col + width], bank[6][:, at:at + width]).then_inc(S["vec_copied"], 1)
                    at += width
                dve.wait_ge(S["vec_copied"], 4)
                for col, n, scale in ((HEAD_COL, 2, fox_scale), (HEAD_COL + 4, 1, fox_scale),
                                      (HEAD_COL + 6, 1, 1.0 - lambda_init)):
                    dve.tensor_scalar(vec[:, col:col + n], vec[:, col:col + n], scale, None, ALU.mult
                                      ).then_inc(S["vec_copied"], 1)
                dve.tensor_copy(fox_bias[:, :], bank[6][0:FOX_HEADS, BIAS_AT:BIAS_AT + 2]).then_inc(S["rope_step"], 1)

            def after_tables():
                dve.wait_ge(S["lam_step"], 3)
                dve.tensor_tensor(lam_gap[:, :], lam_exps[:, 1:2], lam_exps[:, 0:1], ALU.subtract
                                  ).then_inc(S["lam_step"], 1)
                dve.wait_ge(S["lam_step"], 4)
                dve.tensor_scalar(neg_lam[:, :], lam_gap[:, :], -lambda_init, None, ALU.add).then_inc(S["lam_step"], 1)
                dve.tensor_scalar(not_rotated[:, :], rope_cols[:, 2:3], -1.0, 1.0, ALU.mult, ALU.add
                                  ).then_inc(S["rope_step"], 1)
                dve.wait_ge(S["act_rope_step"], 3)
                dve.tensor_scalar(sinT[:, :], sinT[:, :], rope_cols[:, 1:2], None, ALU.mult).then_inc(S["rope_step"], 1)
                dve.wait_ge(S["rope_step"], 12)
                dve.tensor_scalar(cosT[:, :], cosT[:, :], rope_cols[:, 2:3], not_rotated[:, 0:1], ALU.mult, ALU.add
                                  ).then_inc(S["rope_step"], 1)
                dve.wait_ge(S["rope_step"], 13)
                dve.wait_ge(S["lam_step"], 5)
                dve.wait_ge(S["vec_copied"], 7)

            def ffn(i):
                b, f = starts[i], number(i)

                def gate(p, u=0):
                    dve.wait_ge(S["block_done"], b + (3 * p if p else 1) + 6 * u)
                    dve.tensor_tensor(pair(gate_in[:, :]), pair(bank[4][:, :]), over_tokens(inv_rms[:, 0:SEQ]),
                                      ALU.mult).then_inc(S["gate_in_ready"], 1)

                def up(p, u=0):
                    c = PAIRS * f + p + 1 + 2 * u
                    dve.wait_ge(S["silu_ready"], c)
                    dve.tensor_tensor(pair(gate_scaled[:, :]), pair(gate_silu[:, :]), over_tokens(inv_rms[:, 0:SEQ]),
                                      ALU.mult).then_inc(S["gate_scaled_ready"], 1)
                    dve.wait_ge(S["gate_scaled_ready"], c)
                    dve.wait_ge(S["block_done"], b + (3 * p + 1 if p else 2) + 6 * u)
                    dve.tensor_tensor(hidden[:, :], bank[5][:, :], gate_scaled[:, :], ALU.mult
                                      ).then_inc(S["hidden_ready"], 1)

                def low(p, u=0):
                    dve.wait_ge(S["h_high_ready"], PAIRS * f + p + 1 + 2 * u)
                    dve.tensor_tensor(h_low[p % 2][:, :], hidden[:, :], h_high[p % 2][:, :].bitcast(F32),
                                      ALU.subtract).then_inc(S["h_low_ready"], 1)

                def one_pair(p, u=0):
                    split_low(b + 3 * p + 1, u, 6)
                    gate(p, u)
                    split_low(b + 3 * p + 2, u, 6)
                    up(p, u)
                    low(p, u)
                    split_low(b + 3 * p + 3, u, 6)

                split_low(b + 2)
                gate(0)
                up(0)
                split_low(b + 3)
                low(0)
                if i == 0:
                    before_tables()
                elif i == 2:
                    after_tables()
                last = i == len(phases) - 1
                with dve.Fori(0, (PAIRS - 1) // 2 - last) as u:
                    one_pair(1, u)
                    one_pair(2, u)
                if last:
                    one_pair(PAIRS - 2)
                    one_pair(PAIRS - 1)


            def attention(i):
                a, b, fox = number(i), starts[i], phases[i] == "fox"
                w = i // 9
                gain = {"q": HEAD_COL + (w if fox else 4), "k": HEAD_COL + (2 + w if fox else 5)}

                def raw_part(x, j, u):
                    src, dst = {"q": (bank[0], q_raw), "k": (bank[1], k_raw)}[x]
                    c = 4 * a + j + u
                    dve.wait_ge(S["block_done"], b + 3 * j + (1 if x == "q" else 2) + 3 * u)
                    if j or a:
                        dve.wait_ge(S[x + "_ready"], c)
                    dve.tensor_tensor(pair(dst[:, :]), pair(src[:, :]), over_tokens(inv_rms[:, 0:SEQ]), ALU.mult
                                      ).then_inc(S[x + "_raw_ready"], 1)

                def normed(x, j, u):
                    raw_, inv, fin = {"q": (q_raw, q_inv, qT), "k": (k_raw, k_inv, kT)}[x]
                    c = 4 * a + j + u + 1
                    dve.wait_ge(S[x + "_inv_ready"], c)
                    dst, ready = (fin, "_ready") if fox else (raw_, "_normed")
                    dve.scalar_tensor_tensor(dst[:, :], raw_[:, :], vec[:, gain[x]:gain[x] + 1], inv[:, :],
                                             ALU.mult, ALU.mult).then_inc(S[x + ready], 1)

                rotary = {"q": (q_raw, q_inv, q_square, qT), "k": (k_raw, k_inv, k_square, kT)}

                def rotary_cos(x, j, u):
                    raw_, x_cos, _, _ = rotary[x]
                    dve.wait_ge(S[x + "_normed"], j + u + 1)
                    dve.tensor_tensor(pair(x_cos[:, :]), pair(raw_[:, :]), over_tokens(cosT[:, :]), ALU.mult
                                      ).then_inc(S[x + "_cos"], 1)

                def rotary_sin(x, j, u):
                    _, _, x_sin, _ = rotary[x]
                    dve.wait_ge(S[x + "_swapped"], j + u + 1)
                    dve.tensor_tensor(pair(x_sin[:, :]), pair(norm_bank(x, j, fox)[:, :]), over_tokens(sinT[:, :]),
                                      ALU.mult).then_inc(S[x + "_sin"], 1)

                def rotary_sum(x, j, u):
                    _, x_cos, x_sin, fin = rotary[x]
                    dve.wait_ge(S[x + "_cos"], j + u + 1)
                    dve.wait_ge(S[x + "_sin"], j + u + 1)
                    dve.tensor_tensor(fin[:, :], x_cos[:, :], x_sin[:, :], ALU.add).then_inc(S[x + "_ready"], 1)

                def mask_and_max(m, g, u):
                    c = 16 * a + 4 * g + m + 4 * u
                    s, src = scores[m % 2], bank[4 + m % 2]
                    dve.wait_ge(S["scores_done"], c + 1)
                    parts = ((0, slice(0, P)), (1, slice(P, 384)))
                    for qb, cols in parts:
                        if fox:
                            cq = neg_cum_q[:, bass.ds(u * 4 + (FOX_HEADS * qb + 4 * g + m), 1)]
                            dve.scalar_tensor_tensor(s[:, cols], src[:, cols], cq, causal[:, cols],
                                                     ALU.subtract, ALU.add).then_inc(S["score_added"], 1)
                        else:
                            dve.tensor_tensor(s[:, cols], src[:, cols], chunked[:, cols], ALU.add
                                              ).then_inc(S["score_added"], 1)
                    for qb, cols in parts:
                        dve.wait_ge(S["score_added"], 2 * c + qb + 1)
                        ins = dve.tensor_reduce(neg_max[m % 2][:, qb:qb + 1], s[:, cols], AX.X, ALU.max, negate=True)
                    ins.then_inc(S["masked"], 1)

                def normalise(m, g, u):
                    c = 16 * a + 4 * g + m + 4 * u
                    s = scores[m % 2]
                    dve.wait_ge(S["exp_ready"], 2 * c + 2)
                    dve.reciprocal(inv_sum[m % 2][:, :], row_sum[m % 2][:, :]).then_inc(S["inv_sum_ready"], 1)
                    dve.wait_ge(S["inv_sum_ready"], c + 1)
                    if fox:
                        for qb, cols in enumerate((slice(0, P), slice(P, 384))):
                            ins = dve.tensor_scalar(s[:, cols], s[:, cols], inv_sum[m % 2][:, qb:qb + 1], None,
                                                    ALU.mult)
                        ins.then_inc(S["probs_ready"], 1)

                def combine(h, g, u):
                    c = 2 * (g + u) + h
                    normalise(2 * h, g, u)
                    normalise(2 * h + 1, g, u)
                    dve.tensor_scalar(lam_inv_sum[:, :], inv_sum[1][:, :], neg_lam[:, 0:1], None, ALU.mult
                                      ).then_inc(S["lam_scaled"], 1)
                    for qb, cols in enumerate((slice(0, P), slice(P, 384))):
                        dve.tensor_scalar(scores[0][:, cols], scores[0][:, cols], inv_sum[0][:, qb:qb + 1], None,
                                          ALU.mult).then_inc(S["probs_half"], 1)
                    dve.wait_ge(S["lam_scaled"], c + 1)
                    for qb, cols in enumerate((slice(0, P), slice(P, 384))):
                        dve.wait_ge(S["probs_half"], 2 * c + qb + 1)
                        ins = dve.scalar_tensor_tensor(scores[0][:, cols], scores[1][:, cols],
                                                       lam_inv_sum[:, qb:qb + 1], scores[0][:, cols],
                                                       ALU.mult, ALU.add)
                    ins.then_inc(S["probs_ready"], 1)

                def values(j, u):
                    dve.wait_ge(S["block_done"], b + 3 * j + 3 + 3 * u)
                    if j:
                        per = 4 if fox else 2
                        dve.wait_ge(S["pv_done"], turned_before[i] + per * (j + u))
                    for tt in range(2):
                        ins = dve.tensor_scalar(v_nat[:, tt, :], bank[2][:, tt * 256:(tt + 1) * 256],
                                                inv_rms[:, SEQ + tt:SEQ + tt + 1], None, ALU.mult)
                    ins.then_inc(S["v_ready"], 1)

                def o_normalised(g, u):
                    dve.wait_ge(S["o_inv_ready"], g + u + 1)
                    dve.scalar_tensor_tensor(o_normal[:, :], o_copy[:, :], vec[:, HEAD_COL + 6:HEAD_COL + 7],
                                             o_inv[:, :], ALU.mult, ALU.mult).then_inc(S["o_normed"], 1)

                def o_part(g, u):
                    at = bass.ds(2 * (g + u), 2)
                    src = bank[7] if fox else o_normal
                    dve.wait_ge(S["o_high_ready"], o_before[i] + g + u + 1)
                    dve.tensor_tensor(o_low[:, at, :], pair(src[:, :]), o_high[:, at, :].bitcast(F32), ALU.subtract
                                      ).then_inc(S["o_bank_free"], 1)

                def logits():
                    dve.wait_ge(S["logits_done"], w + 1)
                    dve.tensor_tensor(logit[:, :], bank[6][0:FOX_HEADS, 0:SEQ], inv_rms[0:FOX_HEADS, 0:SEQ], ALU.mult
                                      ).then_inc(S["logit_ready"], 1)
                    dve.wait_ge(S["logit_ready"], w + 1)
                    dve.tensor_scalar(logit_min[:, :], logit[:, :], fox_bias[:, w:w + 1], 0.0, ALU.add, ALU.min
                                      ).then_inc(S["logit_min_ready"], 1)

                def cumulate():
                    dve.wait_ge(S["logit_parts"], 3 * w + 3)
                    dve.wait_ge(S["logit_min_ready"], w + 1)
                    dve.tensor_tensor_scan(neg_cumT[:, :], logit_log[:, :], logit_min[:, :], 0.0, ALU.add,
                                           ALU.subtract).then_inc(S["neg_cumT_ready"], 1)

                def split_cum():
                    dve.wait_ge(S["cum_turned"], w + 1)
                    dve.tensor_copy(neg_cum_q[:, :], bank[6][:, SEQ:SEQ + 2 * FOX_HEADS]).then_inc(S["cum_q_ready"], 1)
                    dve.wait_ge(S["cum_q_ready"], w + 1)
                    if w:
                        dve.wait_ge(S["neg_cum_ready"], GROUPS * w)
                    for c in range(3):
                        rows = slice(32 * c, 32 * c + FOX_HEADS)
                        dve.tensor_copy(cum_part[:, :], neg_cumT[:, :]).then_inc(S["cum_split_step"], 1)
                        dve.wait_ge(S["cum_split_step"], 7 * w + 3 * c + 1)
                        ins = dve.tensor_copy(cum_parts[rows, :], cum_part[:, :])
                        if c < 2:
                            ins.then_inc(S["cum_split_step"], 1)
                            dve.tensor_tensor(neg_cumT[:, :], neg_cumT[:, :], cum_part[:, :], ALU.subtract
                                              ).then_inc(S["cum_split_step"], 1)
                            dve.wait_ge(S["cum_split_step"], 7 * w + 3 * c + 3)
                        else:
                            ins.then_inc(S["cum_parts_ready"], 1)

                def fox_group(j, u=0):
                    g = j - 1
                    if not j:
                        logits()
                    split_low(b + 3 * j + 2, u, 3)
                    if not j:
                        cumulate()
                    raw_part("q", j, u)
                    if j:
                        mask_and_max(0, g, u)
                        mask_and_max(1, g, u)
                        normalise(0, g, u)
                        normalise(1, g, u)
                        split_low(b + 3 * j + 3, u, 3)
                        mask_and_max(2, g, u)
                        raw_part("k", j, u)
                        mask_and_max(3, g, u)
                    else:
                        raw_part("k", j, u)
                        split_low(b + 3 * j + 3, u, 3)
                        split_cum()
                    normed("q", j, u)
                    if j:
                        normalise(2, g, u)
                        normalise(3, g, u)
                    split_low(b + 3 * j + 4, u, 3)
                    normed("k", j, u)
                    values(j, u)
                    if j:
                        o_part(g, u)

                def diff_group(j, u=0):
                    g = j - 1
                    if j:
                        split_low(b + 3 * j + 2, u, 3)
                    if j > 1:
                        o_normalised(g - 1, u)
                    raw_part("q", j, u)
                    if not j:
                        split_low(b + 2)
                        raw_part("k", j, u)
                    if j:
                        mask_and_max(0, g, u)
                        mask_and_max(1, g, u)
                    if j > 1:
                        o_part(g - 1, u)
                    normed("q", j, u)
                    if j:
                        combine(0, g, u)
                    split_low(b + 3 * j + 3, u, 3)
                    rotary_cos("q", j, u)
                    if j:
                        raw_part("k", j, u)
                        mask_and_max(2, g, u)
                    rotary_sin("q", j, u)
                    if j:
                        mask_and_max(3, g, u)
                    rotary_sum("q", j, u)
                    if j:
                        split_low(b + 3 * j + 4, u, 3)
                        combine(1, g, u)
                    normed("k", j, u)
                    rotary_cos("k", j, u)
                    if not j:
                        split_low(b + 4)
                    rotary_sin("k", j, u)
                    rotary_sum("k", j, u)
                    values(j, u)

                g, e = GROUPS - 1, b + 3 * GROUPS
                if fox:
                    fox_group(0)
                    with dve.Fori(0, GROUPS - 1) as u:
                        fox_group(1, u)
                    mask_and_max(0, g, 0)
                    mask_and_max(1, g, 0)
                    normalise(0, g, 0)
                    normalise(1, g, 0)
                    split_low(e + 2)
                    mask_and_max(2, g, 0)
                    mask_and_max(3, g, 0)
                    normalise(2, g, 0)
                    normalise(3, g, 0)
                    split_low(e + 3)
                    split_low(e + 4)
                    o_part(g, 0)
                else:
                    diff_group(0)
                    diff_group(1)
                    with dve.Fori(0, GROUPS - 2) as u:
                        diff_group(2, u)
                    mask_and_max(0, g, 0)
                    mask_and_max(1, g, 0)
                    o_normalised(g - 1, 0)
                    o_part(g - 1, 0)
                    combine(0, g, 0)
                    split_low(e + 2)
                    mask_and_max(2, g, 0)
                    mask_and_max(3, g, 0)
                    combine(1, g, 0)
                    split_low(e + 3)
                    split_low(e + 4)
                    o_normalised(g, 0)
                    o_part(g, 0)

            def conv(i):
                b = starts[i]
                count = [0]

                def first_taps(tiles):
                    for t in tiles:
                        dve.tensor_scalar(y_conv[:, t, :], u_pad[:, t, 0:SEQ], vec[:, DW_COL + t:DW_COL + t + 1],
                                          vec[:, DW_B_COL + t:DW_B_COL + t + 1], ALU.mult, ALU.add
                                          ).then_inc(S["tap_done"], 1)
                        count[0] += 1

                def more_taps(tiles, k0, rounds, a_round):
                    n = len(tiles)
                    with dve.Fori(0, rounds) as r:
                        for k in range(a_round):
                            for m, t in enumerate(tiles):
                                dve.wait_ge(S["tap_done"], count[0] + n * (k - 1) + m + 1 + r * (n * a_round))
                                dve.scalar_tensor_tensor(
                                    y_conv[:, t, :], u_pad[:, t, bass.ds(r * a_round + (k0 + k), SEQ)],
                                    vec[:, bass.ds(r * (a_round * KT) + (DW_COL + (k0 + k) * KT + t), 1)],
                                    y_conv[:, t, :], ALU.mult, ALU.add).then_inc(S["tap_done"], 1)
                    count[0] += n * rounds * a_round

                for j in range(GROUPS):
                    split_low(b + 2 * j + 2)
                    dve.wait_ge(S["block_done"], b + 2 * j + 1)
                    dve.tensor_tensor(pair(gate_in[:, :]), pair(bank[2 * (j % 2)][:, :]),
                                      over_tokens(inv_rms[:, 0:SEQ]), ALU.mult).then_inc(S["conv_a_ready"], 1)
                    if j:
                        more_taps((0, 1), 6 * j - 2, 1, 3)
                    split_low(b + 2 * j + 3)
                    dve.wait_ge(S["block_done"], b + 2 * j + 2)
                    dve.tensor_tensor(pair(gate_scaled[:, :]), pair(bank[2 * (j % 2) + 1][:, :]),
                                      over_tokens(inv_rms[:, 0:SEQ]), ALU.mult).then_inc(S["conv_g_ready"], 1)
                    dve.wait_ge(S["conv_a_ready"], j + 1)
                    dve.wait_ge(S["sigmoid_ready"], 2 * j + 2)
                    for m in range(2):
                        t = 2 * j + m
                        dve.scalar_tensor_tensor(u_pad[:, t, TAPS - 1:], gate_in[:, m * SEQ:(m + 1) * SEQ],
                                                 vec[:, PW1_COL + t:PW1_COL + t + 1],
                                                 gate_silu[:, m * SEQ:(m + 1) * SEQ], ALU.add, ALU.mult
                                                 ).then_inc(S["u_ready"], 1)
                    dve.wait_ge(S["u_ready"], 2 * j + 2)
                    if j == 0:
                        first_taps((0, 1))
                    if j < GROUPS - 1:
                        more_taps((0, 1), 6 * j + 1, 1, 3)
                e = b + 2 * GROUPS
                more_taps((0, 1), 19, 4, 3)
                first_taps((2, 3))
                more_taps((2, 3), 1, 5, 5)
                split_low(e + 2)
                dve.wait_ge(S["tile_convolved"], 1)
                dve.wait_ge(S["tap_done"], count[0])
                more_taps((2, 3, SHARED), SHARED_TAPS, 1, 5)
                assert count[0] == DVE_TAPS
                dve.wait_ge(S["mean_done"], 1)
                for T in range(4):
                    dve.scalar_tensor_tensor(y_conv[:, 2 * T:2 * T + 2, :], over_tokens(bank[7][:, 0:SEQ]), -1.0 / D,
                                             y_conv[:, 2 * T:2 * T + 2, :], ALU.mult, ALU.add
                                             ).then_inc(S["centred"], 1)
                dve.wait_ge(S["ln_root_ready"], 1)
                dve.reciprocal(ln_inv[:, :], root[:, 0:SEQ]).then_inc(S["ln_inv_ready"], 1)
                dve.wait_ge(S["ln_inv_ready"], 1)
                for T in range(4):
                    dve.tensor_tensor(y_conv[:, 2 * T:2 * T + 2, :], y_conv[:, 2 * T:2 * T + 2, :],
                                      over_tokens(ln_inv[:, :]), ALU.mult).then_inc(S["ln_scaled"], 1)
                for T in range(4):
                    dve.wait_ge(S["o_high_ready"], o_before[i] + T + 1)
                    dve.tensor_tensor(o_low[:, 2 * T:2 * T + 2, :], ln_work[:, 2 * T:2 * T + 2, :],
                                      o_high[:, 2 * T:2 * T + 2, :].bitcast(F32), ALU.subtract
                                      ).then_inc(S["o_bank_free"], 1)
                for k in range(3, 5):
                    split_low(e + k)

            dve.memset(eps[:, :], EPS).then_inc(S["dve_consts"], 1)
            dve.memset(half_pi[:, :], math.pi / 2).then_inc(S["dve_consts"], 1)
            dve.memset(rope_rows[:, :, :], 0.0).then_inc(S["dve_consts"], 1)
            dve.wait_ge(S["dve_consts"], 3)
            half = ROT // 2
            per_head = rope_rows[:, :, :].rearrange("o r (h a c) -> o r h a c", h=2, c=half)
            for c in range(half):
                dve.memset(per_head[:, 0, :, 0:2, c], ROPE_THETA ** (-2.0 * c / ROT)).then_inc(S["dve_consts"], 1)
            dve.memset(per_head[:, 1, :, 0, :], -1.0).then_inc(S["dve_consts"], 1)
            dve.memset(per_head[:, 1, :, 1, :], 1.0).then_inc(S["dve_consts"], 1)
            dve.memset(per_head[:, 2, :, 0:2, :], 1.0).then_inc(S["dve_consts"], 1)
            dve.memset(row_sum[0][:, :], 1.0).then_inc(S["o_bank_free"], 1)
            dve.memset(cum_parts[:, :], 0.0).then_inc(S["dve_consts"], 1)
            dve.memset(ones_bf[:, :], 1.0).then_inc(S["dve_consts"], 1)
            dve.memset(head_of_row[:, :], 0.0).then_inc(S["dve_consts"], 1)
            dve.wait_ge(S["pool_consts"], N_POOL_CONSTS)
            for h in range(2):
                for c in range(2):
                    dve.tensor_copy(swap[:, HEAD * h + half * c:HEAD * h + half * (c + 1)],
                                    ident[:, HEAD * h + half * (1 - c):HEAD * h + half * (2 - c)]
                                    ).then_inc(S["dve_consts"], 1)
            dve.wait_ge(S["dve_consts"], 21)
            for c in range(3):
                rows = slice(32 * c, 32 * c + 32)
                dve.tensor_copy(head_of_row[rows, :], ident[rows, 32 * c:32 * c + FOX_HEADS]
                                ).then_inc(S["dve_consts"], 1)
            dve.wait_ge(S["norm_turned"], 1)
            dve.tensor_copy(vec[:, NORM_COL:NORM_COL + 96], bank[6][:, NORM_AT:NORM_AT + 96]
                            ).then_inc(S["norm_copied"], 1)
            dve.wait_ge(S["norm_copied"], 1)

            for i, kind in enumerate(phases):
                boundary(i)
                {"ffn": ffn, "fox": attention, "diff": attention, "conv": conv}[kind](i)
            last = len(phases)
            for T in range(4):
                update_x(last, T)
            for m in range(2):
                dve.wait_ge(S["final_turned"], 2 * m + 1)
                dve.tensor_copy(by_token[0][:, m * 512:(m + 1) * 512], bank[4 + m][:, :]
                                ).then_inc(S["token_tile_0_copied"], 1)

        @block.tensor
        def _(pe):
            def three_passes(dst, s_high, s_low, m_high, m_low, first, last, loose=False):
                pe.matmul(dst, s_high, m_high, start=first, stop=False, skip_group_check=loose)
                pe.matmul(dst, s_high, m_low, start=False, stop=False, skip_group_check=loose)
                return pe.matmul(dst, s_low, m_high, start=False, stop=last, skip_group_check=loose)

            def wait_block(b, u=0, per=0):
                pe.wait_ge(S["low_ready"], b + 1 + u * per)

            def columns_half(dst, b, n):
                high, low = (t[b % RING][:, :].rearrange("p (k n) -> p k n", k=KT) for t in (w_high, w_low))
                for k in range(KT):
                    cols = slice(n * P, (n + 1) * P)
                    ins = three_passes(dst[:, n * SEQ:(n + 1) * SEQ], high[:, k, cols], low[:, k, cols],
                                       x_high[:, k, :], x_low[:, k, :], k == 0, k == KT - 1)
                return ins

            def tokens_half(dst, b, tt, tiles=range(KT)):
                high, low = (t[b % RING][:, :].rearrange("p (k n) -> p k n", k=KT) for t in (w_high, w_low))
                toks = slice(tt * P, (tt + 1) * P)
                for k in tiles:
                    ins = three_passes(dst[:, tt * 256:(tt + 1) * 256], x_high[:, k, toks], x_low[:, k, toks],
                                       high[:, k, :], low[:, k, :], k == 0, k == KT - 1)
                return ins

            def rows_block(b, m_high, m_low, first, last, u=0, per=0, tiles=(0, KT)):
                wait_block(b, u, per)
                high, low = (t[b % RING][:, :].rearrange("p (f n) -> p f n", f=2) for t in (w_high, w_low))
                for d in range(*tiles):
                    for f in range(2):
                        cols = slice(d * P, (d + 1) * P)
                        ins = three_passes(bank[d // 2][:, (d % 2) * SEQ:(d % 2 + 1) * SEQ],
                                           high[:, f, cols], low[:, f, cols], m_high[:, f, :], m_low[:, f, :],
                                           first and d % 2 == 0 and f == 0, last and f == 1, True)
                    if last and d % 2 and d < KT - 1:
                        ins.then_inc(S["out_bank_done"], 1)
                if tiles[1] == KT:
                    ins.then_inc(S["block_done"], 1)

            def first_block(i, dst):
                b = starts[i]
                wait_block(b)
                high, low = (t[b % RING][:, :].rearrange("p (k n) -> p k n", k=KT) for t in (w_high, w_low))
                for k in range(KT):
                    pe.wait_ge(S["xlow_ready"], 8 * i + k + 1)
                    for n in range(2):
                        cols = slice(n * P, (n + 1) * P)
                        ins = three_passes(dst[:, n * SEQ:(n + 1) * SEQ], high[:, k, cols], low[:, k, cols],
                                           x_high[:, k, :], x_low[:, k, :], k == 0 and n == 0, k == KT - 1, True)
                ins.then_inc(S["block_done"], 1)
                pe.wait_ge(S["square_folded"], 7 * i + 7)
                ins = pe.matmul(bank[7][:, 0:SEQ], ones[:, :], square_sum[:, :], start=True, stop=True)
                if phases[i] in ("fox", "diff"):
                    for tt in range(2):
                        ins = pe.matmul(bank[7][:, SEQ + tt:SEQ + tt + 1], square_sum[:, tt * P:(tt + 1) * P],
                                        ones[:, 0:1], start=True, stop=True)
                ins.then_inc(S["sumsq_done"], 1)

            def turn_vectors():
                pe.wait_ge(S["vec_loaded"], 16 * 16)
                pe.wait_ge(S["const_loaded"], 96)
                pe.wait_ge(S["norm_copied"], 1)
                at = 0
                for n, rows in enumerate((48, 124, 124)):
                    pe.transpose(bank[6][:, at:at + rows], vec_rows[0:rows, n + 1, :], ident[0:rows, 0:rows])
                    at += rows
                pe.transpose(bank[6][:, at:at + 7], head_rows[:, :], ident[0:7, 0:7])
                pe.transpose(bank[6][0:FOX_HEADS, BIAS_AT:BIAS_AT + 2], fox_bias_rows[:, :], ident[0:2, 0:2])
                for r in range(3):
                    ins = pe.matmul(bank[6][:, ROPE_AT + r:ROPE_AT + r + 1], rope_rows[:, r, :], ones[0:1, 0:1],
                                    start=True, stop=True)
                ins.then_inc(S["vec_turned"], 1)

            def ffn(i):
                b, f = starts[i], number(i)

                def gate_up(which, p, u=0):
                    blk = b + 3 * p - 1 + which
                    wait_block(blk, u, 6)
                    pe.wait_ge(S["hidden_ready" if which else "gate_in_ready"], PAIRS * f + p + 2 * u)
                    columns_half(bank[4 + which], blk, 0)
                    columns_half(bank[4 + which], blk, 1).then_inc(S["block_done"], 1)

                def down(blk, p, u, first, last):
                    pe.wait_ge(S["h_low_ready"], PAIRS * f + p + 1 + 2 * u)
                    rows_block(blk, pair(h_high[p % 2][:, :]), pair(h_low[p % 2][:, :]), first, last, u, 6)

                def one_pair(p, u=0, first=False):
                    gate_up(0, p, u)
                    gate_up(1, p, u)
                    down(b + 3 * p + 1, p - 1, u, first, False)

                first_block(i, bank[4])
                wait_block(b + 1)
                columns_half(bank[5], b + 1, 0)
                columns_half(bank[5], b + 1, 1).then_inc(S["block_done"], 1)
                if i == 0:
                    turn_vectors()
                one_pair(1, first=True)
                one_pair(2)
                with pe.Fori(1, (PAIRS - 1) // 2) as u:
                    one_pair(1, u)
                    one_pair(2, u)
                down(b + 3 * PAIRS - 1, PAIRS - 1, 0, False, True)

            def attention(i):
                a, b, fox = number(i), starts[i], phases[i] == "fox"
                w = i // 9
                per = 4 if fox else 2

                def head_scores(m, g, u):
                    c = 16 * a + 4 * g + m + 4 * u
                    dst = bank[4 + m % 2]
                    if m == 0:
                        pe.wait_ge(S["q_ready"], 4 * a + g + u + 1)
                        pe.wait_ge(S["k_ready"], 4 * a + g + u + 1)
                        if fox:
                            pe.wait_ge(S["neg_cum_ready"], GROUPS * w + g + u + 1)
                    if fox and m == 3:
                        pe.wait_ge(S["probsT_ready"], turned_before[i] + 4 * g + 2 + 4 * u)
                    if m >= 2:
                        pe.wait_ge(S["masked"], c - 1)
                    tile, r = m // 2, slice(HEAD * (m % 2), HEAD * (m % 2) + HEAD)
                    for qb, cols, keys in ((0, slice(0, P), P), (1, slice(P, 384), SEQ)):
                        q = qT[r, tile * SEQ + qb * P:tile * SEQ + (qb + 1) * P]
                        ins = pe.matmul(dst[:, cols], q, kT[r, tile * SEQ:tile * SEQ + keys], start=True, stop=not fox)
                        if fox:
                            at = u * (4 * SEQ) + (4 * g + m) * SEQ
                            ins = pe.matmul(dst[:, cols], ones_bf[:, :], neg_cum_wide[:, bass.ds(at, keys)],
                                            start=False, stop=True)
                    ins.then_inc(S["scores_done"], 1)

                def turn(m, g, u):
                    c = turned_before[i] + per * (g + u) + m
                    pe.wait_ge(S["probs_ready"], c + 1)
                    if m == 1 and not fox:
                        pe.wait_ge(S["probsT_ready"], c)
                    dst = bank[([6, 5, 6, 4] if fox else [6, 6])[m]]
                    for n in range(3):
                        ins = pe.transpose(dst[:, n * P:(n + 1) * P], scores[m % 2 if fox else 0][:, n * P:(n + 1) * P],
                                           ident[:, :])
                    ins.then_inc(S["probs_turned"], 1)

                def values(m, g, u):
                    c = turned_before[i] + per * (g + u) + m
                    pe.wait_ge(S["probsT_ready"], c + 1)
                    if m == 0:
                        pe.wait_ge(S["v_ready"], 4 * a + g + u + 1)
                        pe.wait_ge(S["o_bank_free"], o_before[i] + g + u + 1)
                    p = probsT[m % 2]
                    if fox:
                        r, at = slice(HEAD * (m % 2), HEAD * (m % 2) + HEAD), (m // 2) * SEQ
                        cols = slice(HEAD * m, HEAD * m + HEAD)
                    else:
                        r, at, cols = slice(0, P), m * SEQ, slice(P * m, P * m + P)
                    pe.matmul(bank[7][r, at:at + SEQ], v_nat[:, 0, cols], p[:, 0:SEQ], start=True, stop=False)
                    pe.matmul(bank[7][r, at + P:at + SEQ], v_nat[:, 1, cols], p[:, SEQ:384], start=False, stop=True
                              ).then_inc(S["pv_done"], 1)

                def head_sums(x, j, u):
                    c = 4 * a + j + u + 1
                    pe.wait_ge(S[x + "_sq_ready"], c)
                    if x == "k" and fox:
                        pe.wait_ge(S["q_log_ready"], c)
                    elif x == "k" and j:
                        pe.wait_ge(S["q_sin"], j + u + 1)
                    elif j and not fox:
                        pe.wait_ge(S["k_sin"], j + u)
                    pe.matmul(norm_bank(x, j, fox)[:, :], ones_heads[:, :], {"q": q_square, "k": k_square}[x][:, :],
                              start=True, stop=True).then_inc(S[x + "_sum_done"], 1)

                def swapped(x, j, u):
                    pe.wait_ge(S[x + "_normed"], j + u + 1)
                    pe.matmul(norm_bank(x, j, fox)[:, :], swap[:, :], {"q": q_raw, "k": k_raw}[x][:, :],
                              start=True, stop=True).then_inc(S[x + "_swapped"], 1)

                def o_sums(g, u):
                    pe.wait_ge(S["o_sq_ready"], g + u + 1)
                    pe.matmul(bank[6][:, :], ones[:, :], o_square[:, :], start=True, stop=True
                              ).then_inc(S["o_sum_done"], 1)

                def fox_group(j, u=0):
                    g = j - 1
                    q_blk, k_blk, v_blk = (b + 3 * j + n for n in range(3))
                    if j:
                        wait_block(q_blk, u, 3)
                        columns_half(bank[0], q_blk, 0)
                        columns_half(bank[0], q_blk, 1).then_inc(S["block_done"], 1)
                        head_scores(0, g, u)
                        head_scores(1, g, u)
                    else:
                        first_block(i, bank[0])
                        forget_gates()
                    wait_block(k_blk, u, 3)
                    columns_half(bank[1], k_blk, 0)
                    columns_half(bank[1], k_blk, 1).then_inc(S["block_done"], 1)
                    if j:
                        turn(0, g, u)
                        turn(1, g, u)
                        head_scores(2, g, u)
                    else:
                        turn_cum()
                    head_sums("q", j, u)
                    if j:
                        head_scores(3, g, u)
                    wait_block(v_blk, u, 3)
                    if j:
                        pe.wait_ge(S["v_ready"], 4 * a + j + u)
                    tokens_half(bank[2], v_blk, 0)
                    if j:
                        values(0, g, u)
                        values(1, g, u)
                    head_sums("k", j, u)
                    tokens_half(bank[2], v_blk, 1, range(6))
                    if j:
                        turn(2, g, u)
                        turn(3, g, u)
                    tokens_half(bank[2], v_blk, 1, range(6, KT)).then_inc(S["block_done"], 1)
                    if j:
                        values(2, g, u)
                        values(3, g, u)

                def diff_group(j, u=0):
                    g = j - 1
                    q_blk, k_blk, v_blk = (b + 3 * j + n for n in range(3))
                    if j:
                        wait_block(q_blk, u, 3)
                        columns_half(bank[0], q_blk, 0)
                        if j > 1:
                            o_sums(g - 1, u)
                        columns_half(bank[0], q_blk, 1).then_inc(S["block_done"], 1)
                        head_scores(0, g, u)
                        head_scores(1, g, u)
                        head_sums("q", j, u)
                    else:
                        first_block(i, bank[0])
                    wait_block(k_blk, u, 3)
                    columns_half(bank[1], k_blk, 0)
                    columns_half(bank[1], k_blk, 1).then_inc(S["block_done"], 1)
                    if j:
                        turn(0, g, u)
                        head_scores(2, g, u)
                        swapped("q", j, u)
                        head_scores(3, g, u)
                    else:
                        head_sums("q", j, u)
                    wait_block(v_blk, u, 3)
                    if j:
                        pe.wait_ge(S["v_ready"], 4 * a + j + u)
                    tokens_half(bank[2], v_blk, 0)
                    if j:
                        values(0, g, u)
                    head_sums("k", j, u)
                    if not j:
                        swapped("q", j, u)
                    tokens_half(bank[2], v_blk, 1).then_inc(S["block_done"], 1)
                    if j:
                        turn(1, g, u)
                    swapped("k", j, u)
                    if j:
                        values(1, g, u)

                def forget_gates():
                    pe.wait_ge(S["gate_w_ready"], w + 1)
                    for k in range(KT):
                        ins = pe.matmul(bank[6][0:FOX_HEADS, 0:SEQ], gate_w_gained[:, k, :], xT[:, k, :],
                                        start=k == 0, stop=k == KT - 1)
                    ins.then_inc(S["logits_done"], 1)

                def turn_cum():
                    pe.wait_ge(S["neg_cumT_ready"], w + 1)
                    for tt in range(2):
                        at = SEQ + FOX_HEADS * tt
                        ins = pe.transpose(bank[6][:, at:at + FOX_HEADS], neg_cumT[:, tt * P:(tt + 1) * P],
                                           ident[0:FOX_HEADS, 0:FOX_HEADS])
                    ins.then_inc(S["cum_turned"], 1)

                def o_block(n, tiles=(0, KT)):
                    pe.wait_ge(S["o_bank_free"], o_before[i] + n + 2)
                    rows_block(b + 3 * GROUPS + n, o_high[:, 2 * n:2 * n + 2, :], o_low[:, 2 * n:2 * n + 2, :],
                               n == 0, n == GROUPS - 1, tiles=tiles)

                g = GROUPS - 1
                if fox:
                    fox_group(0)
                    with pe.Fori(0, GROUPS - 1) as u:
                        fox_group(1, u)
                    head_scores(0, g, 0)
                    head_scores(1, g, 0)
                    pe.wait_ge(S["v_ready"], 4 * a + GROUPS)
                    o_block(0)
                    turn(0, g, 0)
                    turn(1, g, 0)
                    head_scores(2, g, 0)
                    head_scores(3, g, 0)
                    o_block(1)
                    values(0, g, 0)
                    values(1, g, 0)
                    turn(2, g, 0)
                    turn(3, g, 0)
                    o_block(2, (0, 4))
                    values(2, g, 0)
                    values(3, g, 0)
                    o_block(2, (4, KT))
                    o_block(3)
                else:
                    diff_group(0)
                    diff_group(1)
                    with pe.Fori(0, GROUPS - 2) as u:
                        diff_group(2, u)
                    head_scores(0, g, 0)
                    head_scores(1, g, 0)
                    o_sums(g - 1, 0)
                    pe.wait_ge(S["v_ready"], 4 * a + GROUPS)
                    o_block(0)
                    turn(0, g, 0)
                    head_scores(2, g, 0)
                    head_scores(3, g, 0)
                    o_block(1, (0, 4))
                    values(0, g, 0)
                    o_block(1, (4, KT))
                    turn(1, g, 0)
                    o_block(2, (0, 1))
                    values(1, g, 0)
                    o_block(2, (1, 4))
                    o_sums(g, 0)
                    o_block(2, (4, KT))
                    o_block(3)

            def conv(i):
                b = starts[i]
                for j in range(2 * GROUPS):
                    if j == 0:
                        first_block(i, bank[0])
                        continue
                    wait_block(b + j)
                    if j >= 4:
                        pe.wait_ge(S["conv_g_ready" if j % 2 else "conv_a_ready"], j // 2 - 1)
                    columns_half(bank[j % 4], b + j, 0)
                    columns_half(bank[j % 4], b + j, 1).then_inc(S["block_done"], 1)
                for n, (t, k0, taps) in enumerate(TAP_CHUNKS):
                    last_tap = (SHARED_TAPS if t == SHARED else TAPS) - 1
                    pe.wait_ge(S["u_ready"], t + 1)
                    pe.wait_ge(S["diagonals_ready"], n + 1)
                    for k in range(taps):
                        at = n % 2 * 2048 + k * P
                        ins = pe.matmul(bank[PE_BANK[t]][:, 0:SEQ], wide[:, at:at + P],
                                        u_pad[:, t, k0 + k:k0 + k + SEQ],
                                        start=k0 + k == 0, stop=k0 + k == last_tap)
                    ins.then_inc(S["diagonals_used"], 1)
                for k, t in enumerate((5, 6, 0, 1, 2, 3, SHARED, 7)):
                    if t > SHARED:
                        pe.wait_ge(S["tile_convolved"], t - SHARED + 1)
                    elif t < 2:
                        pe.wait_ge(S["tap_done"], 2 * TAPS)
                    else:
                        pe.wait_ge(S["tap_done"], DVE_TAPS - SHARED + t)
                    ins = pe.matmul(bank[7][:, 0:SEQ], ones[:, :], y_conv[:, t, :], start=k == 0, stop=k == KT - 1)
                ins.then_inc(S["mean_done"], 1)
                for k in range(KT):
                    pe.wait_ge(S["centred_sq"], k // 2 + 1)
                    ins = pe.matmul(bank[5][:, 0:SEQ], ones[:, :], ln_work[:, k, :], start=k == 0, stop=k == KT - 1)
                ins.then_inc(S["var_done"], 1)
                for n in range(GROUPS):
                    pe.wait_ge(S["o_bank_free"], o_before[i] + n + 2)
                    rows_block(b + 2 * GROUPS + n, o_high[:, 2 * n:2 * n + 2, :], o_low[:, 2 * n:2 * n + 2, :],
                               n == 0, n == GROUPS - 1)

            pe.wait_ge(S["pool_consts"], N_POOL_CONSTS)
            pe.wait_ge(S["dve_consts"], DVE_CONSTS)
            pe.wait_ge(S["norm_loaded"], 16 * 3)
            pe.transpose(bank[6][:, NORM_AT:NORM_AT + 96], vec_rows[0:96, 0, :], ident[0:96, 0:96]
                         ).then_inc(S["norm_turned"], 1)
            pe.wait_ge(S["x_loaded"], 32)
            for T in range(4):
                for m in range(2):
                    for tt in range(2):
                        t = 2 * T + m
                        ins = pe.transpose(bank[T][:, m * SEQ + tt * P:m * SEQ + (tt + 1) * P],
                                           by_token[tt][:, t * P:(t + 1) * P], ident[:, :])
                ins.then_inc(S["x_turned"], 1)
            for i, kind in enumerate(phases):
                {"ffn": ffn, "fox": attention, "diff": attention, "conv": conv}[kind](i)
            for m in range(2):
                pe.wait_ge(S["x_ready"], 4 * len(phases) + 2 * m + 2)
                for tt in range(2):
                    for t in range(4):
                        ins = pe.transpose(bank[4 + 2 * tt + m][:, t * P:(t + 1) * P],
                                           xT[:, 4 * m + t, tt * P:(tt + 1) * P], ident[:, :])
                    ins.then_inc(S["final_turned"], 1)


INPUTS = [
    "x", "positions", "norm_ffn1", "norm_mix", "norm_ffn2", "ffn1_w_gate", "ffn1_w_up", "ffn1_w_down",
    "ffn2_w_gate", "ffn2_w_up", "ffn2_w_down", "fox_w_in", "fox_b_f", "fox_q_gain", "fox_k_gain", "fox_w_out",
    "conv_w_pw1", "conv_b_pw1", "conv_w_dw", "conv_b_dw", "conv_ln_g", "conv_ln_b", "conv_w_pw2", "conv_b_pw2",
    "diff_w_in", "diff_q_gain", "diff_k_gain", "diff_lambda_q1", "diff_lambda_k1", "diff_lambda_q2",
    "diff_lambda_k2", "diff_sub_gain", "diff_w_out",
]


def kernel(**inputs):
    import numpy as np
    import concourse.bacc as bacc
    from concourse.bass_utils import run_bass_kernel_spmd

    nc = bacc.Bacc("TRN2", target_bir_lowering=False, num_devices=1)
    arrays, aps = {}, {}
    for name in INPUTS:
        a = np.ascontiguousarray(inputs[name])
        arrays[f"in_{name}"] = a
        aps[name] = nc.dram_tensor(f"in_{name}", a.shape, mybir.dt.from_np(a.dtype), kind="ExternalInput").ap()
    out = nc.dram_tensor("trunk_out", (1, SEQ, D), F32, kind="ExternalOutput").ap()
    build_trunk(nc, aps, out)
    r = run_bass_kernel_spmd(nc, [arrays], core_ids=[0])
    return r.results[0]["trunk_out"]
```
